# Optimizing a Trainium2 kernel written in Bass

```python
import math
import numpy as np
import jax
import jax.numpy as jnp
from jax import lax

D_MODEL = 1024
BATCH = 1
SEQ = 512
DEPTH = 1
DEC_BATCH = 8
DEC_SEQ = 4
PAST_LEN = 2048
PAGE_SIZE = 128

MLSTM_W = D_MODEL // 2
MLSTM_HEADS = 4
MLSTM_DH = MLSTM_W // MLSTM_HEADS
MLSTM_CHUNK = 64
SWA_W = D_MODEL // 4
SWA_DH = 64
SWA_HEADS = SWA_W // SWA_DH
SWA_KV_HEADS = SWA_HEADS // 2
SWA_GROUP = SWA_HEADS // SWA_KV_HEADS
WINDOW = 128
CONV_W = D_MODEL - MLSTM_W - SWA_W
CONV_WIDTH = 3
MIX_W = MLSTM_W + SWA_W + CONV_W
IN_SPLITS = (MLSTM_W, MLSTM_W, MLSTM_W, MLSTM_W, MLSTM_HEADS, MLSTM_HEADS,
             SWA_W, SWA_KV_HEADS * SWA_DH, SWA_KV_HEADS * SWA_DH,
             CONV_W, CONV_W, CONV_W)
IN_W = sum(IN_SPLITS)
PEER_HEADS = 8
PEER_NKEYS = 128
PEER_EXPERTS = PEER_NKEYS * PEER_NKEYS
PEER_DKEY = 256
PEER_TOPK = 16
PEER_BLOCK = 256
EPS = 1e-6

kernel_name = 'hybrid_mlstm_swa_conv_peer_step'

def rmsnorm(x, g):
    xf = x.astype(jnp.float32)
    y = xf * lax.rsqrt(jnp.mean(jnp.square(xf), axis=-1, keepdims=True) + EPS)
    return (y * g.astype(jnp.float32)).astype(x.dtype)

def alibi_slopes():
    h = jnp.arange(1, SWA_HEADS + 1, dtype=jnp.float32)
    return jnp.exp2(-8.0 * h / SWA_HEADS).reshape(SWA_KV_HEADS, SWA_GROUP)

def _mlstm_chunk(carry, xs):
    C, n, m = carry
    q, k, v, ig, lf = xs
    L = q.shape[2]
    b = jnp.cumsum(lf, axis=-1)
    a = b + m[..., None]
    d = b[..., :, None] - b[..., None, :] + ig[..., None, :]
    causal = jnp.tril(jnp.ones((L, L), dtype=bool))
    d = jnp.where(causal, d, -jnp.inf)
    m_t = jnp.maximum(a, jnp.max(d, axis=-1))
    w_inter = jnp.exp(a - m_t)
    w_intra = jnp.exp(d - m_t[..., None])
    qk = jnp.einsum('bhtk,bhsk->bhts', q, k) * w_intra
    num = w_inter[..., None] * jnp.einsum('bhvk,bhtk->bhtv', C, q) + jnp.einsum('bhts,bhsv->bhtv', qk, v)
    den = w_inter * jnp.einsum('bhk,bhtk->bht', n, q) + jnp.sum(qk, axis=-1)
    h = num / jnp.maximum(jnp.abs(den), jnp.exp(-m_t))[..., None]
    wl_inter = w_inter[..., -1]
    wl_intra = w_intra[..., -1, :]
    C_new = wl_inter[..., None, None] * C + jnp.einsum('bhs,bhsv,bhsk->bhvk', wl_intra, v, k)
    n_new = wl_inter[..., None] * n + jnp.einsum('bhs,bhsk->bhk', wl_intra, k)
    return (C_new, n_new, m_t[..., -1]), h

def mlstm(q, k, v, ig, lf, C0, n0, m0):
    B, T = q.shape[:2]
    L = math.gcd(T, MLSTM_CHUNK)
    nc = T // L

    def to_chunks(t):
        t = jnp.swapaxes(t, 1, 2)
        t = t.reshape(t.shape[:2] + (nc, L) + t.shape[3:])
        return jnp.moveaxis(t, 2, 0)

    carry0 = (C0.astype(jnp.float32), n0.astype(jnp.float32), m0.astype(jnp.float32))
    xs = (to_chunks(q), to_chunks(k), to_chunks(v), to_chunks(ig), to_chunks(lf))
    (C1, n1, m1), h = lax.scan(_mlstm_chunk, carry0, xs)
    h = jnp.moveaxis(h, 0, 2).reshape(B, MLSTM_HEADS, T, MLSTM_DH)
    return jnp.swapaxes(h, 1, 2), C1, n1, m1

def swa_attend(q, k, v, q_pos, k_pos, sinks):
    s = jnp.einsum('...qhgd,...khd->...hgqk', q, k).astype(jnp.float32) * (SWA_DH ** -0.5)
    dist = q_pos[..., :, None] - k_pos[..., None, :]
    visible = (dist >= 0) & (dist <= WINDOW) & (k_pos[..., None, :] >= 0)
    s = s - alibi_slopes()[:, :, None, None] * jnp.expand_dims(dist, (-4, -3)).astype(jnp.float32)
    s = jnp.where(jnp.expand_dims(visible, (-4, -3)), s, -jnp.inf)
    sink = jnp.broadcast_to(sinks.astype(jnp.float32).reshape(SWA_KV_HEADS, SWA_GROUP, 1, 1), s.shape[:-1] + (1,))
    p = jax.nn.softmax(jnp.concatenate([s, sink], axis=-1), axis=-1)[..., :-1]
    return jnp.einsum('...hgqk,...khd->...qhgd', p.astype(v.dtype), v)

def swa_banded(q, k, v, sinks):
    B, S = q.shape[:2]
    nb = S // WINDOW
    qb = q.reshape(B, nb, WINDOW, SWA_KV_HEADS, SWA_GROUP, SWA_DH)
    kb = k.reshape(B, nb, WINDOW, SWA_KV_HEADS, SWA_DH)
    vb = v.reshape(B, nb, WINDOW, SWA_KV_HEADS, SWA_DH)
    pad = ((0, 0), (1, 0), (0, 0), (0, 0), (0, 0))
    kband = jnp.concatenate([jnp.pad(kb[:, :-1], pad), kb], axis=2)
    vband = jnp.concatenate([jnp.pad(vb[:, :-1], pad), vb], axis=2)
    pos = jnp.arange(S, dtype=jnp.int32).reshape(nb, WINDOW)
    kpos = jnp.concatenate([pos - WINDOW, pos], axis=1)
    o = swa_attend(qb, kband, vband, pos, kpos, sinks)
    return o.reshape(B, S, SWA_KV_HEADS, SWA_GROUP, SWA_DH)

def short_conv(u, buf, w):
    T = u.shape[1]
    full = jnp.concatenate([buf.astype(u.dtype), u], axis=1)
    y = sum(w[j] * full[:, j:j + T] for j in range(CONV_WIDTH))
    return y, full[:, T:]

def token_mixers(h, w_in, w_out, gate_b, mh_g, sinks, conv_w, state):
    B, T, _ = h.shape
    f32 = jnp.float32
    z = h @ w_in
    offs = np.cumsum(IN_SPLITS)[:-1].tolist()
    mq, mk, mv, mo, mi, mf, sq, sk, sv, cb, cc, ch = jnp.split(z, offs, axis=-1)
    if state is None:
        kbuf = vbuf = None
        cbuf = jnp.zeros((B, CONV_WIDTH - 1, CONV_W), h.dtype)
        C0 = jnp.zeros((B, MLSTM_HEADS, MLSTM_DH, MLSTM_DH), f32)
        n0 = jnp.zeros((B, MLSTM_HEADS, MLSTM_DH), f32)
        m0 = jnp.zeros((B, MLSTM_HEADS), f32)
        win_rows = min(WINDOW, PAST_LEN)
    else:
        kbuf, vbuf, cbuf, C0, n0, m0 = state
        win_rows = kbuf.shape[1]

    shp = (B, T, MLSTM_HEADS, MLSTM_DH)
    q = mq.reshape(shp).astype(f32)
    k = mk.reshape(shp).astype(f32) * (MLSTM_DH ** -0.5)
    v = mv.reshape(shp).astype(f32)
    pre = jnp.concatenate([mi, mf], axis=-1).astype(f32) + gate_b.astype(f32)
    ig = pre[..., :MLSTM_HEADS]
    lf = jax.nn.log_sigmoid(pre[..., MLSTM_HEADS:])
    hm, C1, n1, m1 = mlstm(q, k, v, ig, lf, C0, n0, m0)
    hm = hm * lax.rsqrt(jnp.mean(jnp.square(hm), axis=-1, keepdims=True) + EPS) * mh_g.astype(f32).reshape(MLSTM_HEADS, MLSTM_DH)
    hm = (hm * jax.nn.sigmoid(mo.reshape(shp).astype(f32))).astype(h.dtype).reshape(B, T, MLSTM_W)

    qa = sq.reshape(B, T, SWA_KV_HEADS, SWA_GROUP, SWA_DH)
    ka = sk.reshape(B, T, SWA_KV_HEADS, SWA_DH)
    va = sv.reshape(B, T, SWA_KV_HEADS, SWA_DH)
    if kbuf is None:
        oa = swa_banded(qa, ka, va, sinks)
        k_all, v_all = ka, va
    else:
        k_all = jnp.concatenate([kbuf.astype(ka.dtype), ka], axis=1)
        v_all = jnp.concatenate([vbuf.astype(va.dtype), va], axis=1)
        q_pos = PAST_LEN + jnp.arange(T, dtype=jnp.int32)
        k_pos = PAST_LEN - win_rows + jnp.arange(win_rows + T, dtype=jnp.int32)
        oa = swa_attend(qa, k_all, v_all, q_pos, k_pos, sinks)
    oa = oa.reshape(B, T, SWA_W)
    k_keep = k_all[:, -win_rows:]
    v_keep = v_all[:, -win_rows:]

    yconv, cbuf_new = short_conv(cc * ch, cbuf, conv_w)
    yc = cb * yconv

    out = jnp.concatenate([hm, oa, yc], axis=-1) @ w_out
    return out, (k_keep, v_keep, cbuf_new, C1, n1, m1)

def peer_ffn(h, wq, subkeys, u_tab, v_tab):
    B, T, D = h.shape
    n = B * T
    nb = -(-n // PEER_BLOCK)
    x = jnp.pad(h.reshape(n, D), ((0, nb * PEER_BLOCK - n), (0, 0))).reshape(nb, PEER_BLOCK, D)

    def block(xb):
        q = (xb @ wq).reshape(PEER_BLOCK, PEER_HEADS, 2, PEER_DKEY // 2)
        s = jnp.einsum('thpd,pkd->thpk', q, subkeys).astype(jnp.float32)
        s1, i1 = lax.top_k(s[:, :, 0], PEER_TOPK)
        s2, i2 = lax.top_k(s[:, :, 1], PEER_TOPK)
        cand = (s1[..., :, None] + s2[..., None, :]).reshape(PEER_BLOCK, PEER_HEADS, PEER_TOPK * PEER_TOPK)
        cidx = (i1[..., :, None] * PEER_NKEYS + i2[..., None, :]).reshape(PEER_BLOCK, PEER_HEADS, PEER_TOPK * PEER_TOPK)
        top_s, sel = lax.top_k(cand, PEER_TOPK)
        idx = jnp.take_along_axis(cidx, sel, axis=-1)
        g = jax.nn.softmax(top_s, axis=-1)
        u = u_tab[idx]
        act = jax.nn.gelu(jnp.einsum('thkd,td->thk', u, xb).astype(jnp.float32))
        vv = v_tab[idx]
        return jnp.einsum('thk,thkd->td', (g * act).astype(vv.dtype), vv)

    y = lax.map(block, x)
    return y.reshape(nb * PEER_BLOCK, D)[:n].reshape(B, T, D)

def trunk_layer(x, c, ada_w, ada_b, g_mix, g_ffn, w_in, w_out, gate_b, mh_g, sinks, conv_w,
                wq, subkeys, u_tab, v_tab, state):
    mod = (jax.nn.silu(c) @ ada_w + ada_b)[:, None, :]
    sh1, sc1, gt1, sh2, sc2, gt2 = jnp.split(mod, 6, axis=-1)
    h = rmsnorm(x, g_mix) * (1 + sc1) + sh1
    mix, new_state = token_mixers(h, w_in, w_out, gate_b, mh_g, sinks, conv_w, state)
    x = x + gt1 * mix
    h = rmsnorm(x, g_ffn) * (1 + sc2) + sh2
    x = x + gt2 * peer_ffn(h, wq, subkeys, u_tab, v_tab)
    return x, new_state

def setup_inputs(seed: int = 0) -> dict:
    key = jax.random.key(seed)
    ks = jax.random.split(key, 26)
    f32 = jnp.float32
    D = D_MODEL
    win_rows = min(WINDOW, PAST_LEN)

    def nrm(k, shape, s):
        return jax.random.normal(k, shape, f32) * s

    gate_b = jnp.concatenate([
        nrm(ks[0], (DEPTH, MLSTM_HEADS), 0.1),
        jnp.linspace(3.0, 6.0, MLSTM_HEADS, dtype=f32)[None, :] + nrm(ks[1], (DEPTH, MLSTM_HEADS), 0.1)], axis=-1)
    return {
        'x_prompt': nrm(ks[2], (BATCH, SEQ, D), 1.0),
        'x_sample': nrm(ks[3], (DEC_BATCH, DEC_SEQ, D), 1.0),
        'cache_swa_k': nrm(ks[4], (DEPTH, DEC_BATCH, win_rows, SWA_KV_HEADS, SWA_DH), 1.0),
        'cache_swa_v': nrm(ks[5], (DEPTH, DEC_BATCH, win_rows, SWA_KV_HEADS, SWA_DH), 1.0),
        'state_conv': nrm(ks[6], (DEPTH, DEC_BATCH, CONV_WIDTH - 1, CONV_W), 1.0),
        'state_mlstm_C': nrm(ks[7], (DEPTH, DEC_BATCH, MLSTM_HEADS, MLSTM_DH, MLSTM_DH), 0.5),
        'state_mlstm_n': nrm(ks[8], (DEPTH, DEC_BATCH, MLSTM_HEADS, MLSTM_DH), 0.5),
        'state_mlstm_m': nrm(ks[9], (DEPTH, DEC_BATCH, MLSTM_HEADS), 1.0),
        'c_prompt': nrm(ks[10], (BATCH, D), 1.0),
        'c_sample': nrm(ks[11], (DEC_BATCH, D), 1.0),
        'ada_w': nrm(ks[12], (DEPTH, D, 6 * D), D ** -0.5),
        'ada_b': nrm(ks[13], (DEPTH, 6 * D), 0.01),
        'norm_mix_g': 1.0 + nrm(ks[14], (DEPTH, D), 0.01),
        'norm_ffn_g': 1.0 + nrm(ks[15], (DEPTH, D), 0.01),
        'w_in': nrm(ks[16], (DEPTH, D, IN_W), D ** -0.5),
        'w_out': nrm(ks[17], (DEPTH, MIX_W, D), MIX_W ** -0.5),
        'mlstm_gate_b': gate_b,
        'mlstm_norm_g': 1.0 + nrm(ks[18], (DEPTH, MLSTM_W), 0.01),
        'swa_sinks': nrm(ks[19], (DEPTH, SWA_HEADS), 0.5),
        'conv_w': nrm(ks[20], (DEPTH, CONV_WIDTH, CONV_W), CONV_WIDTH ** -0.5),
        'peer_wq': nrm(ks[21], (DEPTH, D, PEER_HEADS * PEER_DKEY), D ** -0.5),
        'peer_subkeys': nrm(ks[22], (DEPTH, 2, PEER_NKEYS, PEER_DKEY // 2), (PEER_DKEY // 2) ** -0.5),
        'peer_u': nrm(ks[23], (DEPTH, PEER_EXPERTS, D), D ** -0.5),
        'peer_v': nrm(ks[24], (DEPTH, PEER_EXPERTS, D), PEER_HEADS ** -0.5),
        'final_g': 1.0 + nrm(ks[25], (D,), 0.01),
    }

def reference(x_prompt, x_sample, cache_swa_k, cache_swa_v, state_conv, state_mlstm_C, state_mlstm_n,
              state_mlstm_m, c_prompt, c_sample, ada_w, ada_b, norm_mix_g, norm_ffn_g, w_in, w_out,
              mlstm_gate_b, mlstm_norm_g, swa_sinks, conv_w, peer_wq, peer_subkeys, peer_u, peer_v, final_g):
    xp, xs = x_prompt, x_sample
    new_p, new_s = [], []
    for l in range(DEPTH):
        w = (ada_w[l], ada_b[l], norm_mix_g[l], norm_ffn_g[l], w_in[l], w_out[l], mlstm_gate_b[l],
             mlstm_norm_g[l], swa_sinks[l], conv_w[l], peer_wq[l], peer_subkeys[l], peer_u[l], peer_v[l])
        xp, sp = trunk_layer(xp, c_prompt, *w, None)
        st = (cache_swa_k[l], cache_swa_v[l], state_conv[l], state_mlstm_C[l], state_mlstm_n[l], state_mlstm_m[l])
        xs, ss = trunk_layer(xs, c_sample, *w, st)
        new_p.append(sp)
        new_s.append(ss)
    y_prompt = rmsnorm(xp, final_g)
    y_sample = rmsnorm(xs, final_g)
    pk, pv, pc, pC, pn, pm = [jnp.stack(t) for t in zip(*new_p)]
    sk, sv, sc, sC, sn, sm = [jnp.stack(t) for t in zip(*new_s)]
    return (y_prompt, y_sample, pk, pv, pc, pC, pn, pm, sk, sv, sc, sC, sn, sm)


_drawn_inputs = setup_inputs


def setup_inputs(seed=0):
    import zlib

    import numpy as np

    out = dict(_drawn_inputs(seed))
    spreads = {}
    factors = {'norm_mix_g': 11.351,
     'norm_ffn_g': 200.0,
     'mlstm_norm_g': 200.0,
     'swa_sinks': 200.0,
     'final_g': 174.75,
     'state_conv': 8.0,
     'state_mlstm_C': 3.489,
     'state_mlstm_m': 8.0}
    for name, (base, spread) in spreads.items():
        noise = np.random.default_rng([zlib.crc32(name.encode()), seed]).standard_normal(out[name].shape)
        drawn = base * np.exp(spread * noise) if base else spread * noise
        out[name] = jnp.asarray(drawn.astype(out[name].dtype))
    for name, factor in factors.items():
        out[name] = (out[name] * factor).astype(out[name].dtype)
    return out
```

```python
from contextlib import ExitStack

import concourse.bass as bass
from concourse import mybir

F32 = mybir.dt.float32
U32 = mybir.dt.uint32
I32 = mybir.dt.int32
ALU = mybir.AluOpType
ACT = mybir.ActivationFunctionType
AX = mybir.AxisListType.X

P = 128
D = 1024
KC = D // P
SEQ = 512
NT = SEQ // P
B = 8
TS = 4
NS = B * TS
NC = 1 + B
MH, DH = 4, 128
MW = MH * DH
AH, KVH, AD = 4, 2, 64
WIN = 128
CW, CK = 256, 3
INW = 3336
EPS = 1e-6
NEG = -1e30
KSCALE = DH ** -0.5
SLOPES = [2.0 ** (-8.0 * (h + 1) / AH) for h in range(AH)]
PH, PK, TOPK, NEXP = 8, 128, 16, 16384

GATES, QZ, KZ, VZ, SVCB, CCCH, OZ = range(7)
CHUNKS = [(2048, 2440), (0, 512), (512, 1024), (1024, 1536), (2440, 2824), (2824, 3336), (1536, 2048)]


def hold(eng, sem, value):
    eng.wait_ge(sem, value)
    if not isinstance(value, int):
        eng.nop(nofuse=True)


class Chain:

    def __init__(self, eng, sem):
        self.eng, self.sem, self.base, self.n = eng, sem, 0, 0

    def __call__(self, ins):
        ins.then_inc(self.sem, 1)
        self.n += 1
        hold(self.eng, self.sem, self.base + self.n)

    def enter(self, t, per):
        self.start, self.per = self.base + self.n, per
        self.base, self.n = t * per + self.start, 0

    def leave(self, trips):
        assert self.n == self.per, (self.n, self.per)
        self.base, self.n = self.start + trips * self.per, 0


def same_cols(ap, n):
    return ap.rearrange("p (m o) -> p m o", o=1).to_broadcast([ap.shape[0], ap.shape[1], n])


def repeat_last(ap, n):
    return ap.unsqueeze(len(ap.shape)).broadcast_to([*ap.shape, n])


def repeat_mid(ap, n):
    return ap.unsqueeze(1).broadcast_to([ap.shape[0], n, *ap.shape[1:]])


def make_constants(nc, K):
    with ExitStack() as ctx:
        cleared = ctx.enter_context(nc.semaphore("const_cleared"))
        dist_ready = ctx.enter_context(nc.semaphore("const_dist"))
        bias_ready = ctx.enter_context(nc.semaphore("const_bias"))
        dist_i = ctx.enter_context(nc.sbuf_tensor("dist_i", [P, 2 * P], I32))
        sdist_i = ctx.enter_context(nc.sbuf_tensor("sdist_i", [P, WIN + NS], I32))
        dist = ctx.enter_context(nc.sbuf_tensor("dist", [P, 2 * P], F32))
        sdist = ctx.enter_context(nc.sbuf_tensor("sdist", [P, WIN + NS], F32))
        tpat_i = ctx.enter_context(nc.sbuf_tensor("tpat_i", [P, P], I32))
        tpat = ctx.enter_context(nc.sbuf_tensor("tpat", [P, P], F32))
        cols = ctx.enter_context(nc.sbuf_tensor("row_cols", [P, 2], F32))
        beyond = ctx.enter_context(nc.sbuf_tensor("beyond", [P, WIN + NS], F32))
        sdist_ready = ctx.enter_context(nc.semaphore("const_sdist"))
        s_step = ctx.enter_context(nc.semaphore("const_s_step"))
        block = ctx.enter_context(nc.Block())

        @block.vector
        def _(dve):
            v = nc.vector
            for h in range(AH):
                v.memset(cols[h * NS:(h + 1) * NS, 1:2], -SLOPES[h])
            dve.wait_ge(sdist_ready, 1)
            v.tensor_tensor(tpat[:, :], tpat[:, :], K["ident"][:, :], ALU.mult).then_inc(s_step, 1)
            dve.wait_ge(s_step, 1)
            v.tensor_reduce(cols[:, 0:1], tpat[:, :], AX, ALU.add).then_inc(s_step, 1)
            dve.wait_ge(s_step, 2)
            v.tensor_scalar(K["s_bias"][:, :], sdist[:, :], cols[:, 0:1], cols[:, 1:2], ALU.add, ALU.mult)
            v.tensor_scalar(beyond[:, :], sdist[:, :], cols[:, 0:1], float(WIN), ALU.add, ALU.is_gt).then_inc(s_step, 1)
            dve.wait_ge(s_step, 3)
            v.scalar_tensor_tensor(K["s_bias"][:, :], beyond[:, :], NEG, K["s_bias"][:, :], ALU.mult, ALU.add)\
                .then_inc(s_step, 1)
            dve.wait_ge(dist_ready, 1)
            for h in range(AH):
                last = v.tensor_copy(tpat[h * NS:(h + 1) * NS, 0:NS], K["mask_s"][:, :])
            last.then_inc(s_step, 1)
            dve.wait_ge(s_step, 5)
            v.tensor_tensor(K["s_bias"][:, WIN:], K["s_bias"][:, WIN:], tpat[:, 0:NS], ALU.add)

        @block.gpsimd
        def _(pool):
            g = nc.gpsimd
            g.iota(sdist_i[:, 0:WIN], pattern=[[-1, WIN]], base=WIN, channel_multiplier=0)
            g.iota(sdist_i[:, WIN:].rearrange("p (b i) -> p b i", i=TS), pattern=[[0, B], [-1, TS]], base=0, channel_multiplier=0)
            g.iota(tpat_i[:, :].rearrange("p (a i) -> p a i", i=TS), pattern=[[0, P // TS], [1, TS]], base=0,
                   channel_multiplier=0)
            zero = [K["ident"], K["tri"], K["mask"], K["last"], K["tri_s"], K["mask_s"], K["last_s"], K["same"]]
            for m in zero:
                g.memset(m[:], 0.0)
            g.memset(K["ones"][:], 1.0)
            g.memset(K["live_bias"][:, :, 0:P], NEG)
            g.iota(dist_i[:, :], pattern=[[-1, 2 * P]], base=P, channel_multiplier=1)
            g.iota(K["iota16"][:, :], pattern=[[1, TOPK]], base=0, channel_multiplier=0).then_inc(cleared, 1)
            pool.wait_ge(cleared, 1)

            def fill(m, pattern, op, value, base, per_row):
                return g.affine_select(out=m, in_=m, compare_op=op, fill=value, base=base,
                                       pattern=pattern, channel_multiplier=per_row)

            def blocks(m):
                return m.rearrange("p (b i) -> p b i", i=TS)

            fill(K["ident"][:, :], [[-1, P]], ALU.not_equal, 1.0, 0, 1)
            fill(K["tri"][:, :], [[-1, P]], ALU.is_gt, 1.0, 0, 1)
            fill(K["mask"][:, :], [[-1, P]], ALU.is_ge, NEG, 0, 1)
            fill(K["last"][:, :], [[0, P]], ALU.not_equal, 1.0, -(P - 1), 1)
            fill(blocks(K["mask_s"][:, :]), [[-TS, B], [-1, TS]], ALU.is_ge, NEG, 0, 1)
            fill(K["tri_s"][:, :], [[-1, NS]], ALU.is_gt, 1.0, 0, 1)
            fill(blocks(K["last_s"][:, :]), [[-TS, B], [0, TS]], ALU.not_equal, 1.0, -(TS - 1), 1)
            fill(K["same"][:, :], [[TS, B]], ALU.is_gt, 1.0, 0, -1).then_inc(cleared, 1)
            pool.wait_ge(cleared, 2)
            fill(blocks(K["mask_s"][:, :]), [[TS, B], [0, TS]], ALU.is_ge, NEG, TS - 1, -1)
            fill(blocks(K["tri_s"][:, :]), [[-TS, B], [0, TS]], ALU.is_ge, 0.0, 0, 1)
            fill(K["same"][:, :], [[TS, B]], ALU.is_ge, 0.0, TS - 1, -1)
            g.tensor_copy(sdist[:, :], sdist_i[:, :])
            g.tensor_copy(tpat[:, :], tpat_i[:, :]).then_inc(sdist_ready, 1)
            g.tensor_copy(dist[:, :], dist_i[:, :]).then_inc(dist_ready, 1)
            pool.wait_ge(dist_ready, 1)
            for h in range(AH):
                g.tensor_scalar(K["bias"][:, h, :], dist[:, :], -SLOPES[h], None, ALU.mult).then_inc(bias_ready, 1)
            pool.wait_ge(bias_ready, AH)
            fill(K["bias"][:, :, :], [[0, AH], [1, 2 * P]], ALU.is_ge, NEG, 0, -1).then_inc(bias_ready, 1)
            pool.wait_ge(bias_ready, AH + 1)
            fill(K["bias"][:, :, :], [[0, AH], [-1, 2 * P]], ALU.is_ge, NEG, P, 1).then_inc(bias_ready, 1)
            pool.wait_ge(bias_ready, AH + 2)
            g.tensor_copy(K["live_bias"][:, :, P:2 * P], K["bias"][:, :, P:2 * P])


def modulation_rows(nc, I, mod, w_in, w_in_in, K):
    NCH = 6 * D // 512
    RING = 3
    with ExitStack() as ctx:
        def sb(name, shape, dt=F32):
            return ctx.enter_context(nc.sbuf_tensor(name, shape, dt))

        def sem(name):
            return ctx.enter_context(nc.semaphore(name))

        c_rows = sb("c_rows", [NC, D])
        c_sig = sb("c_sig", [NC, D])
        cT = sb("cT", [P, KC, NC])
        w = sb("ada_ring", [P, RING, KC, 512])
        bias = sb("ada_bias", [NC, RING, 512])
        row = sb("ada_row", [NC, RING, 512])
        ps_t = ctx.enter_context(nc.psum_tensor("ada_ps_t", [P, KC, NC], F32))
        ps = [ctx.enter_context(nc.psum_tensor(f"ada_ps{i}", [NC, 512], F32)) for i in range(RING)]
        c_in, c_silu, c_sgm, ct_ps, ct_ready = sem("c_in"), sem("c_silu"), sem("c_sgm"), sem("ct_ps"), sem("ct_ready")
        ring_in = [sem(f"ada_w_in{i}") for i in range(RING)]
        row_ps, row_ready = sem("ada_row_ps"), sem("ada_row_ready")
        row_out = [sem(f"ada_row_out{i}") for i in range(RING)]
        ada = I["ada_w"][0].rearrange("(kc p) n -> p kc n", p=P)
        block = ctx.enter_context(nc.Block())

        @block.sync
        def _(sp):
            sp.dma_start(c_rows[0:1, :], I["c_prompt"]).then_inc(c_in, 16)
            sp.dma_start(c_rows[1:NC, :], I["c_sample"]).then_inc(c_in, 16)

            def load(c, i, first=False):
                if not first:
                    hold(sp, row_ready, c - RING + 1)
                cols = bass.ds(c * 512, 512)
                sp.dma_start(w[:, i, :, :], ada[:, :, cols]).then_inc(ring_in[i], 16)
                sp.dma_start(bias[:, i, :], I["ada_b"][0, cols].partition_broadcast(NC)).then_inc(ring_in[i], 16)

            for i in range(RING):
                load(i, i, first=True)
            with sp.Fori(1, NCH // RING) as r:
                for i in range(RING):
                    load(r * RING + i, i)
            sp.dma_start(w_in[:, :, :], I["w_in"][0].rearrange("(kc p) n -> p kc n", p=P)).then_inc(w_in_in, 16)

        @block.scalar
        def _(act):
            act.wait_ge(c_in, 32)
            nc.scalar.activation(c_sig[:, :], c_rows[:, :], ACT.Sigmoid).then_inc(c_sgm, 1)
            def store(c, i):
                hold(act, row_ready, c + 1)
                act.dma_start(mod[:, bass.ds(c * 512, 512)], row[:, i, :]).then_inc(row_out[i], 16)

            with act.Fori(0, NCH // RING) as r:
                for i in range(RING):
                    store(r * RING + i, i)
            for i in range(RING):
                act.wait_ge(row_out[i], 16 * (NCH // RING))

        @block.vector
        def _(dve):
            dve.wait_ge(c_sgm, 1)
            nc.vector.tensor_tensor(c_rows[:, :], c_rows[:, :], c_sig[:, :], ALU.mult).then_inc(c_silu, 1)
            dve.wait_ge(ct_ps, 1)
            nc.vector.tensor_copy(cT[:, :, :], ps_t[:, :, :]).then_inc(ct_ready, 1)

            def add_bias(c, r, i, first=False):
                hold(dve, ring_in[i], r * 32 + 32)
                if not first:
                    hold(dve, row_out[i], r * 16)
                hold(dve, row_ps, c + 1)
                nc.vector.tensor_tensor(row[:, i, :], ps[i][:, :], bias[:, i, :], ALU.add).then_inc(row_ready, 1)

            for i in range(RING):
                add_bias(i, 0, i, first=True)
            with dve.Fori(1, NCH // RING) as r:
                for i in range(RING):
                    add_bias(r * RING + i, r, i)

        @block.tensor
        def _(pe):
            pe.wait_ge(c_silu, 1)
            for kc in range(KC):
                last = nc.tensor.transpose(ps_t[:, kc, :], c_rows[:, kc * P:(kc + 1) * P], K["ident"][0:NC, 0:NC])
            last.then_inc(ct_ps, 1)
            pe.wait_ge(ct_ready, 1)

            def product(c, r, i, first=False):
                hold(pe, ring_in[i], r * 32 + 32)
                if not first:
                    hold(pe, row_ready, c - RING + 1)
                for kc in range(KC):
                    mm = nc.tensor.matmul(ps[i][:, :], cT[:, kc, :], w[:, i, kc, :], start=(kc == 0), stop=(kc == KC - 1))
                mm.then_inc(row_ps, 1)

            for i in range(RING):
                product(i, 0, i, first=True)
            with pe.Fori(1, NCH // RING) as r:
                for i in range(RING):
                    product(r * RING + i, r, i)


class Mixer:

    def __init__(self, nc, ctx, w_in):
        def sb(name, shape, dt=F32):
            return ctx.enter_context(nc.sbuf_tensor(name, shape, dt))

        def ps(name, shape):
            return ctx.enter_context(nc.psum_tensor(name, shape, F32))

        self.w_in = w_in
        self.w_out = sb("w_out", [P, KC, D])
        self.row_a, self.row_s, self.row_g = sb("mod_scale", [P, D]), sb("mod_shift", [P, D]), sb("mod_gate", [P, D])
        self.xt = sb("xt", [P, D])
        self.h = sb("h", [P, D])
        self.hT = sb("hT", [P, KC, P])
        self.g5 = sb("z_gates_sq_sk", [P, 392])
        self.qz, self.kz = sb("z_q", [P, MW]), sb("z_k", [P, MW])
        self.vz = sb("z_v", [P, MH, DH])
        self.g6, self.g7 = sb("z_sv_cb", [P, 384]), sb("z_cc_ch", [P, 512])
        self.oz = sb("z_o", [P, MW])
        self.stat = sb("mix_stat", [P, 4])
        self.eps = sb("eps", [P, 1])
        self.gb, self.mg, self.sink = sb("gate_b", [P, 2 * MH]), sb("mlstm_g", [P, MW]), sb("sinks", [P, AH])
        self.pre, self.absf = sb("gate_pre", [P, 8]), sb("gate_abs", [P, MH])
        self.lg, self.lf = sb("gate_log", [P, MH]), sb("gate_lf", [P, MH])
        self.mb = sb("mm_b", [P, 8])
        self.w, self.rowmax = sb("gate_w", [P, MH]), sb("d_max", [P, MH])
        self.mprev, self.nmm, self.mt = sb("m_prev", [P, MH]), sb("neg_mm", [P, MH]), sb("m_t", [P, MH])
        self.earg, self.eval = sb("exp_arg", [P, 8]), sb("exp_val", [P, 8])
        self.dm = sb("d_matrix", [P, MH, P])
        self.diag = sb("diag_w", [P, MH, P])
        self.qk = sb("qT_kT", [P, 2, MH, P])
        self.qT, self.kT = self.qk[:, 0], self.qk[:, 1]
        self.mixT = self.qk[:, :, :, :].rearrange("p a h t -> p (a h) t")
        self.pT = sb("pT", [P, MH, P])
        self.den, self.rden = sb("den", [P, 8]), sb("rden", [P, MH])
        self.ss2, self.r2 = sb("ss2", [P, MH]), sb("r2", [P, MH])
        self.lastv, self.larg, self.lval = sb("last_mm_b", [P, 8]), sb("last_arg", [P, 8]), sb("last_val", [P, 8])
        self.CT, self.nT = sb("CT", [P, MH, DH]), sb("nT", [P, MH])
        self.sqT, self.skT = sb("sqT", [P, 2, P]), sb("skT", [P, 2 * P])
        self.sv_prev = sb("sv_prev", [P, KVH * AD])
        self.sc = sb("swa_scores", [P, AH, 2 * P])
        self.smx, self.ssum, self.ses = sb("swa_max", [P, 2 * AH]), sb("swa_sum", [P, AH]), sb("swa_sink", [P, AH])
        self.ps_t, self.ps_m = ps("ps_t", [P, 4, P]), ps("ps_m", [P, 512])
        self.ps_z = [ps("ps_z0", [P, 512]), ps("ps_z1", [P, 512])]
        self.ps_s = ps("ps_s", [P, 2, 512])
        self.ps_n = [ps("ps_n0", [P, 512]), ps("ps_n1", [P, 512])]
        self.u = self.g7[:, 0:CW]
        self.uT = sb("conv_uT", [P, 2, P + CK - 1])
        self.cbT = self.pT[:, 2:4]
        self.cw = sb("conv_taps", [P, CK, 2])


TB = 11
T_H0, T_H1, T_SWA, T_Q, T_K, T_P, T_A0, T_A1, T_CONV, T_HM, T_OA = range(TB)
SIGNALS = ("w_out_in small_in rows_in rows_ready init x_in ss_ready h_ready t_full t_free zfull0 zfull1 zfree0 zfree1 "
           "gate_abs_ready lg_ready lf_ready b_full diag_ready wb_full d_ready expw_ready "
           "s_full p_ready num_full inter_ready numf_ready ss2_ready hm_ready larg_ready lval_ready vw_ready "
           "upd_full state_ready swa_full sc_ready swa_exp pv_full oa_ready u_ready yc_ready og_ready "
           "o_full x1_ready x1_stored pool_done act_step dve_step").split()


class Tile:

    def __init__(self, nc, X, s, t, rows, tri, mask, last):
        self.nc, self.X, self.s, self.t, self.n = nc, X, s, t, rows
        self.tri, self.mask, self.last = tri, mask, last

    def on(self, eng, name, per=1, k=None):
        hold(eng, self.s[name], self.t * per + (per if k is None else k))

    def z_landed(self, eng, i):
        self.on(eng, f"zfull{i % 2}", 4 - i % 2, i // 2 + 1)

    def z_out(self, eng, i):
        self.on(eng, f"zfree{i % 2}", 4 - i % 2, i // 2 + 1)

    def t_landed(self, eng, k):
        self.on(eng, "t_full", self.per_t, k + 1)

    def t_out(self, eng, k):
        self.on(eng, "t_free", self.per_t, k + 1)

    def batch(self, pe, k, blocks, ident):
        if k:
            self.t_out(pe, k - 1)
        for j, (src, rows, cols) in enumerate(blocks):
            last = self.nc.tensor.transpose(self.X.ps_t[0:cols, j, 0:rows], src, ident[0:rows, 0:rows])
        last.then_inc(self.s["t_full"], 1)

    def chunk(self, pe, i):
        a, b = CHUNKS[i]
        X, n = self.X, self.n
        if i >= 2:
            self.z_out(pe, i - 2)
        for kc in range(KC):
            mm = self.nc.tensor.matmul(X.ps_z[i % 2][0:n, 0:b - a], X.hT[:, kc, 0:n], X.w_in[:, kc, a:b],
                                       start=(kc == 0), stop=(kc == KC - 1))
        mm.then_inc(self.s[f"zfull{i % 2}"], 1)

    def project(self, pe, K):
        nc, X, s, n, e = self.nc, self.X, self.s, self.n, K["ident"]
        self.on(pe, "h_ready")
        self.batch(pe, T_H0, [(X.h[0:n, j * P:(j + 1) * P], n, P) for j in range(4)], e)
        self.batch(pe, T_H1, [(X.h[0:n, j * P:(j + 1) * P], n, P) for j in range(4, 8)], e)
        self.t_out(pe, T_H1)
        self.chunk(pe, GATES)
        self.chunk(pe, QZ)
        self.z_out(pe, GATES)
        self.batch(pe, T_SWA, [(X.g5[0:n, 8 + j * P:8 + (j + 1) * P], n, P) for j in range(3)], e)
        self.chunk(pe, KZ)
        self.on(pe, "lf_ready")
        nc.tensor.matmul(X.ps_m[0:n, 0:4], self.tri, X.lf[0:n, :], start=True, stop=True).then_inc(s["b_full"], 1)
        self.chunk(pe, VZ)
        self.z_out(pe, QZ)
        self.batch(pe, T_Q, [(X.qz[0:n, h * DH:(h + 1) * DH], n, DH) for h in range(MH)], e)
        self.on(pe, "diag_ready")
        for h in range(MH):
            mm = nc.tensor.matmul(X.ps_s[0:n, 1, h * P:h * P + n], K["ones"][0:n, 0:n], X.diag[0:n, h, 0:n],
                                  start=True, stop=True)
        mm.then_inc(s["wb_full"], 1)
        self.chunk(pe, SVCB)
        self.z_out(pe, KZ)
        self.batch(pe, T_K, [(X.kz[0:n, h * DH:(h + 1) * DH], n, DH) for h in range(MH)], e)
        self.chunk(pe, CCCH)
        self.t_out(pe, T_K)
        for h in range(MH):
            mm = nc.tensor.matmul(X.ps_s[0:n, 0, h * P:h * P + n], X.qT[:, h, 0:n], X.kT[:, h, 0:n],
                                  start=True, stop=True)
        mm.then_inc(s["s_full"], 1)
        self.chunk(pe, OZ)
        self.on(pe, "p_ready")
        self.batch(pe, T_P, [(X.dm[0:n, h, 0:n], n, n) for h in range(MH)], e)

    def intra(self, pe, K):
        nc, X, s, n = self.nc, self.X, self.s, self.n
        self.t_out(pe, T_P)
        self.z_out(pe, VZ)
        nc.tensor.matmul(X.ps_m[0:n, 16:24], self.last, X.mb[0:n, :], start=True, stop=True)
        for h in range(MH):
            nc.tensor.matmul(X.ps_n[0][0:n, h * DH:(h + 1) * DH], X.pT[0:n, h, 0:n], X.vz[0:n, h, :],
                             start=True, stop=True)
            mm = nc.tensor.matmul(X.ps_m[0:n, 12 + h:13 + h], X.pT[0:n, h, 0:n], K["ones"][0:n, 0:1],
                                  start=True, stop=True)
        mm.then_inc(s["num_full"], 1)

    def out_product(self, pe):
        nc, X, s, n = self.nc, self.X, self.s, self.n
        pe.wait_ge(s["w_out_in"], 16)
        self.z_out(pe, CCCH)
        self.z_out(pe, OZ)
        self.on(pe, "yc_ready")
        for c in range(2):
            for kc in range(KC):
                mm = nc.tensor.matmul(X.ps_z[c][0:n, :], X.mixT[:, kc, 0:n], X.w_out[:, kc, c * 512:(c + 1) * 512],
                                      start=(kc == 0), stop=(kc == KC - 1))
        mm.then_inc(s["o_full"], 1)

    def act_front(self, act, chain):
        nc, X, s, n = self.nc, self.X, self.s, self.n
        a = nc.scalar.activation
        self.on(act, "x_in", 16)
        chain(a(X.h[0:n, :], X.xt[0:n, :], ACT.Square, accum_out=X.stat[0:n, 0:1]))
        a(X.stat[0:n, 1:2], X.stat[0:n, 0:1], ACT.Sqrt, scale=1.0 / D, bias=X.eps[0:n, :]).then_inc(s["ss_ready"], 1)
        self.t_landed(act, T_H0)
        a(X.hT[:, 0:4, 0:n], X.ps_t[:, :, 0:n], ACT.Copy).then_inc(s["t_free"], 1)
        self.z_landed(act, QZ)
        a(X.qz[0:n, :], X.ps_z[QZ % 2][0:n, :], ACT.Copy).then_inc(s[f"zfree{QZ % 2}"], 1)
        self.on(act, "gate_abs_ready")
        chain(a(X.lg[0:n, :], X.absf[0:n, :], ACT.Exp, scale=-1.0))
        a(X.lg[0:n, :], X.lg[0:n, :], ACT.Ln, bias=1.0).then_inc(s["lg_ready"], 1)
        self.z_landed(act, KZ)
        a(X.kz[0:n, :], X.ps_z[KZ % 2][0:n, :], ACT.Copy, scale=KSCALE).then_inc(s[f"zfree{KZ % 2}"], 1)
        self.t_landed(act, T_Q)
        a(X.qT[:, :, 0:n], X.ps_t[:, :, 0:n], ACT.Copy).then_inc(s["t_free"], 1)
        self.on(act, "d_ready")
        for h in range(MH):
            a(X.dm[0:n, h, 0:n], X.dm[0:n, h, 0:n], ACT.Exp, bias=X.nmm[0:n, h:h + 1])
        a(X.eval[0:n, :], X.earg[0:n, :], ACT.Exp).then_inc(s["expw_ready"], 1)
        self.z_landed(act, SVCB)
        a(X.g6[0:n, :], X.ps_z[SVCB % 2][0:n, 0:384], ACT.Copy).then_inc(s[f"zfree{SVCB % 2}"], 1)
        self.z_landed(act, OZ)
        a(X.oz[0:n, :], X.ps_z[OZ % 2][0:n, :], ACT.Sigmoid).then_inc(s[f"zfree{OZ % 2}"], 1)
        self.t_landed(act, T_P)
        a(X.pT[0:n, :, 0:n], X.ps_t[0:n, :, 0:n], ACT.Copy).then_inc(s["t_free"], 1)

    def act_norm(self, act, chain, inter, landed, out):
        nc, X, s, n = self.nc, self.X, self.s, self.n
        a = nc.scalar.activation
        landed(act)
        for h in range(MH):
            last = a(X.h[0:n, h * DH:(h + 1) * DH], inter[:, h, :], ACT.Copy, scale=X.eval[0:n, h:h + 1])
        last.then_inc(s[out], 1)
        self.on(act, "larg_ready")
        a(X.lval[0:n, :], X.larg[0:n, :], ACT.Exp).then_inc(s["lval_ready"], 1)
        self.on(act, "numf_ready")
        for h in range(MH):
            last = a(X.sc[0:n, h, 0:DH], X.h[0:n, h * DH:(h + 1) * DH], ACT.Square, scale=X.rden[0:n, h:h + 1],
                     accum_out=X.ss2[0:n, h:h + 1])
        chain(last)
        a(X.r2[0:n, :], X.ss2[0:n, :], ACT.Sqrt, scale=1.0 / DH, bias=X.eps[0:n, :]).then_inc(s["ss2_ready"], 1)

    def dve_front(self, dve, chain, K):
        nc, X, s, n = self.nc, self.X, self.s, self.n
        v = nc.vector
        self.on(dve, "ss_ready")
        chain(v.reciprocal(X.stat[0:n, 2:3], X.stat[0:n, 1:2]))
        chain(v.scalar_tensor_tensor(X.h[0:n, :], X.xt[0:n, :], X.stat[0:n, 2:3], X.row_a[0:n, :], ALU.mult, ALU.mult))
        v.tensor_tensor(X.h[0:n, :], X.h[0:n, :], X.row_s[0:n, :], ALU.add).then_inc(s["h_ready"], 1)
        self.t_landed(dve, T_H1)
        v.tensor_copy(X.hT[:, 4:8, 0:n], X.ps_t[:, :, 0:n]).then_inc(s["t_free"], 1)
        self.z_landed(dve, GATES)
        zg = X.ps_z[GATES % 2][0:n, :]
        v.tensor_copy(X.g5[0:n, 0:8], zg[:, 0:8])
        v.tensor_copy(X.g5[0:n, 264:392], zg[:, 264:392])
        v.tensor_copy(X.g5[0:n, 8:264].rearrange("p (g kv d) -> p g kv d", g=2, kv=KVH),
                      zg[:, 8:264].rearrange("p (kv g d) -> p g kv d", kv=KVH, g=2)).then_inc(s[f"zfree{GATES % 2}"], 1)
        self.z_out(dve, GATES)
        chain(v.tensor_tensor(X.pre[0:n, :], X.g5[0:n, 0:8], X.gb[0:n, :], ALU.add))
        v.scalar_tensor_tensor(X.absf[0:n, :], X.pre[0:n, 4:8], -1.0, X.pre[0:n, 4:8], ALU.mult, ALU.max).then_inc(s["gate_abs_ready"], 1)
        self.t_landed(dve, T_SWA)
        v.tensor_copy(X.sqT[:, :, 0:n], X.ps_t[:, 0:2, 0:n])
        v.tensor_copy(X.skT[:, P:P + n], X.ps_t[:, 2, 0:n]).then_inc(s["t_free"], 1)
        self.on(dve, "lg_ready")
        v.scalar_tensor_tensor(X.lf[0:n, :], X.pre[0:n, 4:8], 0.0, X.lg[0:n, :], ALU.min, ALU.subtract)\
            .then_inc(s["lf_ready"], 1)
        self.z_landed(dve, VZ)
        v.tensor_copy(X.vz[0:n, :, :], X.ps_z[VZ % 2][0:n, :].rearrange("p (h d) -> p h d", h=MH))\
            .then_inc(s[f"zfree{VZ % 2}"], 1)
        self.on(dve, "b_full")
        v.tensor_copy(X.mb[0:n, 4:8], X.ps_m[0:n, 0:4])
        chain(v.tensor_tensor(X.w[0:n, :], X.pre[0:n, 0:4], X.ps_m[0:n, 0:4], ALU.subtract))
        v.tensor_tensor(X.diag[0:n, :, 0:n], repeat_mid(K["ident"][0:n, 0:n], MH), repeat_last(X.w[0:n, :], n), ALU.mult)\
            .then_inc(s["diag_ready"], 1)
        self.t_landed(dve, T_K)
        v.tensor_copy(X.kT[:, :, 0:n], X.ps_t[:, :, 0:n]).then_inc(s["t_free"], 1)
        self.on(dve, "wb_full")
        wb = X.ps_s[0:n, 1, :].rearrange("p (h s) -> p h s", h=MH)[:, :, 0:n]
        chain(v.tensor_tensor(X.dm[0:n, :, 0:n], wb, repeat_mid(self.mask, MH), ALU.add))
        chain(v.tensor_reduce(X.rowmax[0:n, :], X.dm[0:n, :, 0:n], AX, ALU.max))
        chain(v.tensor_tensor(X.mb[0:n, 0:4], X.rowmax[0:n, :], X.mprev[0:n, :], ALU.max))
        v.tensor_scalar(X.nmm[0:n, :], X.mb[0:n, 0:4], -1.0, None, ALU.mult)
        v.tensor_tensor(X.earg[0:n, 0:4], X.mprev[0:n, :], X.mb[0:n, 0:4], ALU.subtract)
        chain(v.tensor_tensor(X.mt[0:n, :], X.mb[0:n, 0:4], X.mb[0:n, 4:8], ALU.add))
        v.tensor_scalar(X.earg[0:n, 4:8], X.mt[0:n, :], -1.0, None, ALU.mult).then_inc(s["d_ready"], 1)
        self.z_landed(dve, CCCH)
        v.tensor_copy(X.g7[0:n, :], X.ps_z[CCCH % 2][0:n, :]).then_inc(s[f"zfree{CCCH % 2}"], 1)
        self.on(dve, "expw_ready")
        self.on(dve, "s_full")
        raw = X.ps_s[0:n, 0, :].rearrange("p (h s) -> p h s", h=MH)[:, :, 0:n]
        v.tensor_tensor(X.dm[0:n, :, 0:n], raw, X.dm[0:n, :, 0:n], ALU.mult).then_inc(s["p_ready"], 1)

    def dve_num(self, dve, chain, inter_den, inter_out):
        nc, X, s, n = self.nc, self.X, self.s, self.n
        v = nc.vector
        self.on(dve, "num_full")
        chain(v.tensor_tensor(X.den[0:n, 0:4], X.eval[0:n, 0:4], inter_den, ALU.mult))
        chain(v.tensor_tensor(X.den[0:n, 0:4], X.den[0:n, 0:4], X.ps_m[0:n, 12:16], ALU.add))
        chain(v.scalar_tensor_tensor(X.den[0:n, 4:8], X.den[0:n, 0:4], -1.0, X.den[0:n, 0:4], ALU.mult, ALU.max))
        chain(v.tensor_tensor(X.den[0:n, 4:8], X.den[0:n, 4:8], X.eval[0:n, 4:8], ALU.max))
        v.reciprocal(X.rden[0:n, :], X.den[0:n, 4:8])
        inter_out(dve)
        v.tensor_tensor(X.h[0:n, 0:MW], X.h[0:n, 0:MW], X.ps_n[0][0:n, :], ALU.add).then_inc(s["numf_ready"], 1)

    def dve_last(self, dve, chain):
        nc, X, s, n = self.nc, self.X, self.s, self.n
        v = nc.vector
        chain(v.tensor_copy(X.lastv[0:n, :], X.ps_m[0:n, 16:24]))
        v.tensor_tensor(X.larg[0:n, 0:4], X.w[0:n, :], X.lastv[0:n, 0:4], ALU.subtract)
        v.tensor_tensor(X.larg[0:n, 4:8], X.mprev[0:n, :], X.lastv[0:n, 0:4], ALU.subtract).then_inc(s["larg_ready"], 1)
        self.on(dve, "lval_ready")
        v.tensor_tensor(X.mprev[0:n, :], X.lastv[0:n, 0:4], X.lastv[0:n, 4:8], ALU.add)
        v.tensor_tensor(X.diag[0:n, :, :], X.vz[0:n, :, :], repeat_last(X.lval[0:n, 0:4], DH), ALU.mult)\
            .then_inc(s["vw_ready"], 1)

    def dve_norm(self, dve, chain):
        nc, X, s, n = self.nc, self.X, self.s, self.n
        v = nc.vector
        self.on(dve, "ss2_ready")
        chain(v.reciprocal(X.r2[0:n, :], X.r2[0:n, :]))
        chain(v.tensor_tensor(X.r2[0:n, :], X.r2[0:n, :], X.rden[0:n, :], ALU.mult))
        hm = X.h[0:n, 0:MW].rearrange("p (h d) -> p h d", h=MH)
        chain(v.tensor_tensor(hm, hm, repeat_last(X.r2[0:n, :], DH), ALU.mult))
        self.on(dve, "og_ready")
        v.tensor_tensor(X.h[0:n, 0:MW], X.h[0:n, 0:MW], X.oz[0:n, :], ALU.mult).then_inc(s["hm_ready"], 1)

    def dve_residual(self, dve, chain):
        nc, X, s, n = self.nc, self.X, self.s, self.n
        v = nc.vector
        self.on(dve, "o_full")
        v.tensor_tensor(X.h[0:n, 0:512], X.ps_z[0][0:n, :], X.row_g[0:n, 0:512], ALU.mult)
        chain(v.tensor_tensor(X.h[0:n, 512:D], X.ps_z[1][0:n, :], X.row_g[0:n, 512:D], ALU.mult))
        v.tensor_tensor(X.xt[0:n, :], X.xt[0:n, :], X.h[0:n, :], ALU.add).then_inc(s["x1_ready"], 1)

    def pool_gates(self, pool):
        nc, X, s, n = self.nc, self.X, self.s, self.n
        self.z_out(pool, CCCH)
        nc.gpsimd.tensor_tensor(X.u[0:n, :], X.g7[0:n, 0:CW], X.g7[0:n, CW:2 * CW], ALU.mult).then_inc(s["u_ready"], 1)
        self.z_out(pool, OZ)
        nc.gpsimd.tensor_tensor(X.oz[0:n, :], X.oz[0:n, :], X.mg[0:n, :], ALU.mult).then_inc(s["og_ready"], 1)


def load_mod_rows(sp, nc, I, mod, X, s, sample, extra=()):
    gain = I["norm_mix_g"][0]
    n = NS if sample else P
    for dst, k in ((X.row_a, 1), (X.row_s, 0), (X.row_g, 2)):
        if sample:
            for b in range(B):
                sp.dma_start(dst[b * TS:(b + 1) * TS, :], mod[1 + b, k * D:(k + 1) * D].partition_broadcast(TS)).then_inc(s["rows_in"], 16)
        else:
            sp.dma_start(dst[:, :], mod[0, k * D:(k + 1) * D].partition_broadcast(P)).then_inc(s["rows_in"], 16)
    sp.dma_start(X.h[0:n, :], gain.partition_broadcast(n)).then_inc(s["rows_in"], 16)
    return 16 * ((3 * B if sample else 3) + 1)


def dve_mod_rows(dve, nc, X, s, sample):
    n = NS if sample else P
    dve.wait_ge(s["rows_in"], 16 * ((3 * B if sample else 3) + 1))
    nc.vector.scalar_tensor_tensor(X.row_a[0:n, :], X.row_a[0:n, :], 1.0, X.h[0:n, :], ALU.add, ALU.mult)\
        .then_inc(s["rows_ready"], 1)
    dve.wait_ge(s["rows_ready"], 1)


def mix_prompt(nc, I, O, mod, x1_dram, X, K, s):

    def tile(t):
        T = Tile(nc, X, s, t, P, K["tri"][:, :], K["mask"][:, :], K["last"][:, :])
        T.per_t = TB
        return T

    with nc.Block() as block:
        @block.sync
        def _(sp):
            sp.dma_start(X.gb[:, :], I["mlstm_gate_b"][0].partition_broadcast(P)).then_inc(s["small_in"], 16)
            sp.dma_start(X.mg[:, :], I["mlstm_norm_g"][0].partition_broadcast(P)).then_inc(s["small_in"], 16)
            sp.dma_start(X.sink[:, :], I["swa_sinks"][0].partition_broadcast(P)).then_inc(s["small_in"], 16)
            for j in range(CK):
                sp.dma_start(X.cw[:, j, :], I["conv_w"][0, j].rearrange("(a p) -> p a", p=P),
                             allow_slow_non_contiguous=True).then_inc(s["small_in"], 16)
            load_mod_rows(sp, nc, I, mod, X, s, False)
            sp.dma_start(X.w_out[:, :, :], I["w_out"][0].rearrange("(kc p) n -> p kc n", p=P)).then_inc(s["w_out_in"], 16)
            sp.wait_ge(s["small_in"], 16 * (3 + CK))
            sp.wait_ge(s["init"], 1)
            sp.wait_ge(s["rows_ready"], 1)
            sp.dma_start(X.xt[:, :], I["x_prompt"][0, 0:P, :]).then_inc(s["x_in"], 16)

            def store(t):
                hold(sp, s["x1_ready"], t + 1)
                sp.dma_start(x1_dram[bass.ds(t * P, P), :], X.xt[:, :]).then_inc(s["x1_stored"], 16)

            with sp.Fori(0, NT - 1) as t:
                store(t)
                hold(sp, s["x1_stored"], t * 16 + 16)
                hold(sp, s["pool_done"], t + 1)
                sp.dma_start(X.xt[:, :], I["x_prompt"][0, bass.ds(t * P + P, P), :]).then_inc(s["x_in"], 16)
            store(NT - 1)
            out = []
            sp.dma_start(O["swa_k_p"].rearrange("l b w h d -> (l b w) (h d)"), X.g5[:, 264:392]).then_inc(s["x1_stored"], 16)
            sp.dma_start(O["swa_v_p"].rearrange("l b w h d -> (l b w) (h d)"), X.g6[:, 0:128]).then_inc(s["x1_stored"], 16)
            sp.dma_start(O["conv_p"].rearrange("l b w c -> (l b w) c"), X.u[P - 2:P, :]).then_inc(s["x1_stored"], 16)
            sp.dma_start(O["m_p"].rearrange("l b h -> (l b) h"), X.mprev[0:1, :]).then_inc(s["x1_stored"], 16)
            for h in range(MH):
                sp.dma_start(O["n_p"][0, 0, h].rearrange("(k o) -> k o", o=1), X.nT[:, h:h + 1],
                             allow_slow_non_contiguous=True).then_inc(s["x1_stored"], 16)
            sp.wait_ge(s["t_free"], NT * TB + 1)
            sp.dma_start(O["C_p"].rearrange("l b h v k -> v (l b h) k"), X.pT[:, :, :]).then_inc(s["x1_stored"], 16)
            sp.wait_ge(s["x1_stored"], 16 * (NT + 5 + MH))

        @block.gpsimd
        def _(pool):
            g = nc.gpsimd
            for m in (X.CT, X.nT, X.mprev, X.skT, X.sv_prev):
                g.memset(m[:], 0.0)
            g.memset(X.eps[:, :], EPS)
            g.memset(X.uT[:, :, 0:CK - 1], 0.0).then_inc(s["init"], 1)
            with pool.Fori(0, NT) as t:
                T = tile(t)
                T.pool_gates(pool)
                T.on(pool, "swa_full")
                g.tensor_copy(X.skT[:, 0:P], X.skT[:, P:2 * P])
                T.on(pool, "sc_ready")
                g.tensor_copy(K["live_bias"][:, :, 0:P], K["bias"][:, :, 0:P])
                T.on(pool, "pv_full")
                g.tensor_copy(X.sv_prev[:, :], X.g6[:, 0:P]).then_inc(s["pool_done"], 1)

        @block.scalar
        def _(act):
            chain = Chain(act, s["act_step"])
            a = nc.scalar.activation
            with act.Fori(0, NT) as t:
                chain.enter(t, 3)
                T = tile(t)
                T.act_front(act, chain)
                T.act_norm(act, chain, X.ps_n[1][:, :].rearrange("p (h d) -> p h d", h=MH),
                           lambda eng: T.on(eng, "num_full"), "inter_ready")
                T.on(act, "sc_ready")
                for h in range(AH):
                    a(X.sc[:, h, :], X.sc[:, h, :], ACT.Exp, bias=X.smx[:, AH + h:AH + h + 1],
                      accum_out=X.ssum[:, h:h + 1])
                a(X.ses[:, :], X.ses[:, :], ACT.Exp).then_inc(s["swa_exp"], 1)
                T.t_landed(act, T_A1)
                a(X.hT[:, 4:8, :], X.ps_t[:, :, :], ACT.Copy).then_inc(s["t_free"], 1)
                T.t_landed(act, T_CONV)
                a(X.uT[:, :, CK - 1:], X.ps_t[:, 0:2, :], ACT.Copy)
                a(X.cbT[:, :, :], X.ps_t[:, 2:4, :], ACT.Copy).then_inc(s["t_free"], 1)
                T.t_landed(act, T_OA)
                a(X.mixT[:, 4:6, :], X.ps_t[:, 0:2, :], ACT.Copy).then_inc(s["t_free"], 1)
            chain.leave(NT)
            act.wait_ge(s["t_full"], NT * TB + 1)
            a(X.pT[:, :, :], X.ps_t[:, :, :], ACT.Copy).then_inc(s["t_free"], 1)

        @block.vector
        def _(dve):
            chain = Chain(dve, s["dve_step"])
            v = nc.vector
            dve_mod_rows(dve, nc, X, s, False)
            with dve.Fori(0, NT) as t:
                chain.enter(t, 28)
                T = tile(t)
                T.dve_front(dve, chain, K)
                T.dve_num(dve, chain, X.ps_m[:, 8:12], lambda eng: T.on(eng, "inter_ready"))
                T.dve_last(dve, chain)
                T.dve_norm(dve, chain)
                T.on(dve, "upd_full")
                for h in range(MH):
                    v.scalar_tensor_tensor(X.CT[:, h, :], X.CT[:, h, :], X.lval[:, 4 + h:5 + h],
                                           X.ps_n[0][:, h * DH:(h + 1) * DH], ALU.mult, ALU.add)
                chain(v.tensor_tensor(X.nT[:, :], X.nT[:, :], X.lval[:, 4:8], ALU.mult))
                v.tensor_tensor(X.nT[:, :], X.nT[:, :], X.ps_m[:, 24:28], ALU.add).then_inc(s["state_ready"], 1)
                T.on(dve, "swa_full")
                chain(v.scalar_tensor_tensor(X.sc[:, :, :], X.ps_s[:, :, :].rearrange("p a (h k) -> p (a h) k", h=2),
                                             AD ** -0.5, K["live_bias"][:, :, :], ALU.mult, ALU.add))
                chain(v.tensor_reduce(X.smx[:, 0:AH], X.sc[:, :, :], AX, ALU.max))
                chain(v.tensor_tensor(X.smx[:, 0:AH], X.smx[:, 0:AH], X.sink[:, :], ALU.max))
                chain(v.tensor_tensor(X.ses[:, :], X.sink[:, :], X.smx[:, 0:AH], ALU.subtract))
                v.tensor_scalar(X.smx[:, AH:2 * AH], X.smx[:, 0:AH], -1.0, None, ALU.mult).then_inc(s["sc_ready"], 1)
                T.on(dve, "swa_exp")
                chain(v.tensor_tensor(X.ssum[:, :], X.ssum[:, :], X.ses[:, :], ALU.add))
                chain(v.reciprocal(X.ssum[:, :], X.ssum[:, :]))
                T.t_landed(dve, T_A0)
                v.tensor_copy(X.hT[:, 0:4, :], X.ps_t[:, :, :]).then_inc(s["t_free"], 1)
                T.on(dve, "pv_full")
                v.tensor_tensor(X.h[:, MW:MW + AH * AD].rearrange("p (h d) -> p h d", h=AH),
                                X.ps_m[:, 64:64 + AH * AD].rearrange("p (h d) -> p h d", h=AH),
                                repeat_last(X.ssum[:, :], AD), ALU.mult).then_inc(s["oa_ready"], 1)
                T.t_out(dve, T_CONV)
                y = X.diag[:, 0:2, :]
                for a in range(2):
                    last = v.tensor_scalar(y[:, a, :], X.uT[:, a, 0:P], X.cw[:, 0, a:a + 1], None, ALU.mult)
                chain(last)
                for j in range(1, CK):
                    for a in range(2):
                        last = v.scalar_tensor_tensor(y[:, a, :], X.uT[:, a, j:j + P], X.cw[:, j, a:a + 1], y[:, a, :],
                                                      ALU.mult, ALU.add)
                    chain(last)
                chain(v.tensor_tensor(X.mixT[:, 6:8, :], y, X.cbT[:, :, :], ALU.mult))
                v.tensor_copy(X.uT[:, :, 0:CK - 1], X.uT[:, :, P:P + CK - 1]).then_inc(s["yc_ready"], 1)
                T.t_landed(dve, T_HM)
                v.tensor_copy(X.mixT[:, 0:4, :], X.ps_t[:, :, :]).then_inc(s["t_free"], 1)
                T.dve_residual(dve, chain)
            chain.leave(NT)

        @block.tensor
        def _(pe):
            e = K["ident"]
            pe.wait_ge(s["w_in_in"], 16)
            with pe.Fori(0, NT) as t:
                T = tile(t)
                T.project(pe, K)
                for h in range(MH):
                    nc.tensor.matmul(X.ps_n[1][:, h * DH:(h + 1) * DH], X.qT[:, h, :], X.CT[:, h, :], start=True, stop=True)
                    nc.tensor.matmul(X.ps_m[:, 8 + h:9 + h], X.qT[:, h, :], X.nT[:, h:h + 1], start=True, stop=True)
                T.intra(pe, K)
                T.on(pe, "numf_ready")
                T.on(pe, "vw_ready")
                for h in range(MH):
                    nc.tensor.matmul(X.ps_n[0][:, h * DH:(h + 1) * DH], X.kz[:, h * DH:(h + 1) * DH], X.diag[:, h, :],
                                     start=True, stop=True)
                    mm = nc.tensor.matmul(X.ps_m[:, 24 + h:25 + h], X.kz[:, h * DH:(h + 1) * DH], X.lval[:, h:h + 1],
                                          start=True, stop=True)
                mm.then_inc(s["upd_full"], 1)
                for h in range(AH):
                    kv, g = h // 2, h % 2
                    mm = nc.tensor.matmul(X.ps_s[:, h // 2, (h % 2) * 2 * P:(h % 2 + 1) * 2 * P],
                                          X.sqT[kv * AD:(kv + 1) * AD, g, :], X.skT[kv * AD:(kv + 1) * AD, :],
                                          start=True, stop=True)
                mm.then_inc(s["swa_full"], 1)
                T.on(pe, "swa_exp")
                T.batch(pe, T_A0, [(X.sc[:, h, a * P:(a + 1) * P], P, P) for h in range(2) for a in range(2)], e)
                T.batch(pe, T_A1, [(X.sc[:, h, a * P:(a + 1) * P], P, P) for h in range(2, 4) for a in range(2)], e)
                T.t_out(pe, T_A1)
                for h in range(AH):
                    kv = h // 2
                    for a, vals in enumerate((X.sv_prev, X.g6)):
                        mm = nc.tensor.matmul(X.ps_m[:, 64 + h * AD:64 + (h + 1) * AD], X.hT[:, 2 * h + a, :],
                                              vals[:, kv * AD:(kv + 1) * AD], start=(a == 0), stop=(a == 1))
                mm.then_inc(s["pv_full"], 1)
                T.on(pe, "u_ready")
                T.batch(pe, T_CONV, [(X.u[:, 0:P], P, P), (X.u[:, P:], P, P), (X.g6[:, 128:256], P, P), (X.g6[:, 256:384], P, P)], e)
                T.on(pe, "hm_ready")
                T.batch(pe, T_HM, [(X.h[:, h * DH:(h + 1) * DH], P, DH) for h in range(MH)], e)
                T.on(pe, "oa_ready")
                T.batch(pe, T_OA, [(X.h[:, MW + a * P:MW + (a + 1) * P], P, P) for a in range(2)], e)
                T.t_out(pe, T_OA)
                T.out_product(pe)
            pe.wait_ge(s["state_ready"], NT)
            for h in range(MH):
                last = nc.tensor.transpose(X.ps_t[:, h, :], X.CT[:, h, :], e[:, :])
            last.then_inc(s["t_full"], 1)


S_C0 = T_P + 1
S_I = S_C0 + B
S_K0, S_K1, S_SC, S_P, S_CONV, S_ST, S_HM = range(S_I + 1, S_I + 8)
EXTRA = ("c_in kv_in small2_in si_full int_ready cu_full cu_out nu_full n_ready w8_full w8_out km_ready sw_full "
         "st_ready pn_ready y_stored").split()


def mix_sample(nc, I, O, mod, x1_dram, X, K, s):
    W = X.w_in[:, :, :].rearrange("p a b -> p (a b)")
    at = [0]

    def take(rows, n, pattern=None, **dims):
        ap = W[0:rows, at[0]:at[0] + n]
        at[0] += n
        return ap.rearrange(pattern, **dims) if pattern else ap

    Cs = take(P, B * MH * DH, "p (m k) -> p m k", k=DH)
    CTs = take(P, B * MH * DH, "p (m k) -> p m k", k=DH)
    Km = take(NS, MH * B * DH, "p (h b k) -> p h b k", h=MH, b=B)
    kc = take(P, B * P, "p (b c) -> p b c", b=B)
    vc = take(P, B * P, "p (b c) -> p b c", b=B)
    kcT = take(P, B * P, "p (b c) -> p b c", b=B)
    nq = take(NS, MW)
    nqz = take(NS, MW)
    n8 = take(B, MW)
    stc = take(2 * B, CW)
    intT = take(P, MH * NS)
    sT = take(P, AH * NS)
    sN = take(NS, AH * NS)
    sc = take(P, WIN + NS)
    pTc = take(P, AH * NS)
    pTn = take(NS, AH * NS)
    full = take(P, 2 * B * (TS + CK - 1), "p (a b w) -> p a b w", a=2, b=B)
    y = take(P, 2 * B * TS, "p (a b t) -> p a b t", a=2, b=B)
    lw = take(NS, MH * B, "p (h b) -> p h b", h=MH)
    wsel = take(NS, B * MH)
    lv8 = take(NS, 8)
    w8 = take(B, 8)
    wlib = take(P, B * MH)
    nden = take(NS, MH)

    T = Tile(nc, X, s, 0, NS, K["tri_s"][:, :], K["mask_s"][:, :], K["last_s"][:, :])
    T.per_t = 0
    last_of = K["last_s"][:, :].rearrange("p (b i) -> p b i", i=TS)[:, :, 0]

    with nc.Block() as block:
        @block.sync
        def _(sp):
            k_new, v_new = O["swa_k_s"][0], O["swa_v_s"][0]
            sp.dma_start(k_new[:, 0:WIN - TS], I["cache_swa_k"][0, :, TS:WIN]).then_inc(s["y_stored"], 16)
            sp.dma_start(v_new[:, 0:WIN - TS], I["cache_swa_v"][0, :, TS:WIN]).then_inc(s["y_stored"], 16)
            stored = 2
            load_mod_rows(sp, nc, I, mod, X, s, True)
            for b in range(B):
                sp.dma_start(X.mprev[b * TS:(b + 1) * TS, :], I["state_mlstm_m"][0, b].partition_broadcast(TS))\
                    .then_inc(s["small_in"], 16)
            for h in range(AH):
                sp.dma_start(X.sink[h * NS:(h + 1) * NS, 0:1], I["swa_sinks"][0, h:h + 1].partition_broadcast(NS))\
                    .then_inc(s["small_in"], 16)
            sp.wait_ge(s["small_in"], 16 * (B + AH))
            sp.wait_ge(s["rows_ready"], 1)
            sp.dma_start(X.xt[0:NS, :], I["x_sample"].rearrange("b t d -> (b t) d")).then_inc(s["x_in"], 16)
            T.z_landed(sp, OZ)
            sp.dma_start(Cs, I["state_mlstm_C"][0].rearrange("b h v k -> v (b h) k")).then_inc(s["c_in"], 16)
            sp.dma_start(kc, I["cache_swa_k"][0].rearrange("b w h d -> w b (h d)")).then_inc(s["kv_in"], 16)
            sp.dma_start(vc, I["cache_swa_v"][0].rearrange("b w h d -> w b (h d)")).then_inc(s["kv_in"], 16)
            for b in range(B):
                sp.dma_start(nq[b * TS:(b + 1) * TS, :], I["state_mlstm_n"][0, b].rearrange("h k -> (h k)")
                             .partition_broadcast(TS)).then_inc(s["small2_in"], 16)
            sp.dma_start(n8, I["state_mlstm_n"][0].rearrange("b h k -> b (h k)")).then_inc(s["small2_in"], 16)
            sp.dma_start(stc, I["state_conv"][0].rearrange("b w c -> (b w) c")).then_inc(s["small2_in"], 16)
            T.z_out(sp, GATES)
            T.z_out(sp, SVCB)
            for b in range(B):
                for new, rows in ((k_new, X.g5[b * TS:(b + 1) * TS, 264:392]), (v_new, X.g6[b * TS:(b + 1) * TS, 0:P])):
                    sp.dma_start(new[b, WIN - TS:WIN].rearrange("w h d -> w (h d)"), rows).then_inc(s["y_stored"], 16)
                    stored += 1
            T.on(sp, "u_ready")
            for j in range(CK - 1):
                sp.dma_start(O["conv_s"][0, :, j], X.u[TS - CK + 1 + j:NS:TS, :]).then_inc(s["y_stored"], 16)
                stored += 1
            sp.wait_ge(s["n_ready"], 1)
            sp.dma_start(O["n_s"][0].rearrange("b h k -> b (h k)"), n8).then_inc(s["y_stored"], 16)
            sp.dma_start(O["m_s"][0], w8[:, 4:8]).then_inc(s["y_stored"], 16)
            sp.wait_ge(s["cu_out"], 2 * MH)
            sp.dma_start(O["C_s"][0].rearrange("b h v k -> v (b h) k"), Cs).then_inc(s["y_stored"], 16)
            T.on(sp, "x1_ready")
            sp.dma_start(x1_dram[SEQ:SEQ + NS, :], X.xt[0:NS, :]).then_inc(s["y_stored"], 16)
            sp.wait_ge(s["y_stored"], 16 * (stored + 4))

        @block.gpsimd
        def _(pool):
            T.pool_gates(pool)

        @block.scalar
        def _(act):
            chain = Chain(act, s["act_step"])
            a = nc.scalar.activation
            T.act_front(act, chain)
            for i in range(0, B, 2):
                T.t_landed(act, S_C0 + i)
                a(CTs[:, 4 * i:4 * i + 4, :], X.ps_t[:, :, :], ACT.Copy).then_inc(s["t_free"], 1)
            act.wait_ge(s["si_full"], 1)
            a(intT, X.ps_n[1][:, 0:P], ACT.Copy).then_inc(s["int_ready"], 1)
            T.act_norm(act, chain, X.ps_t[0:NS, :, :], lambda eng: T.t_landed(eng, S_I), "t_free")
            for k, half in ((S_K0, 0), (S_K1, 4)):
                T.t_landed(act, k)
                a(kcT[:, half:half + 4, :], X.ps_t[:, :, :], ACT.Copy).then_inc(s["t_free"], 1)
            act.wait_ge(s["sw_full"], 1)
            for kv in range(KVH):
                a(sT[:, kv * 2 * NS:(kv + 1) * 2 * NS], X.ps_n[kv][:, 0:2 * NS], ACT.Copy)
                last = a(sN[:, kv * 2 * NS:(kv + 1) * 2 * NS], X.ps_n[kv][0:NS, P:P + 2 * NS], ACT.Copy)
            last.then_inc(s["st_ready"], 1)
            T.on(act, "sc_ready")
            a(sc, sc, ACT.Exp, bias=X.smx[:, 1:2], accum_out=X.ssum[:, 0:1])
            a(X.ses[:, 0:1], X.ses[:, 0:1], ACT.Exp).then_inc(s["swa_exp"], 1)
            T.on(act, "pv_full")
            a(X.mixT[:, 4:6, 0:NS], X.ps_m[:, P:P + 2 * NS].rearrange("p (a t) -> p a t", a=2), ACT.Copy)\
                .then_inc(s["oa_ready"], 1)

        @block.vector
        def _(dve):
            chain = Chain(dve, s["dve_step"])
            v = nc.vector
            dve_mod_rows(dve, nc, X, s, True)
            T.dve_front(dve, chain, K)
            for i in range(1, B, 2):
                T.t_landed(dve, S_C0 + i)
                v.tensor_copy(CTs[:, 4 * i:4 * i + 4, :], X.ps_t[:, :, :]).then_inc(s["t_free"], 1)
            dve.wait_ge(s["small2_in"], 16 * (B + 2))
            chain(v.tensor_tensor(nqz, X.qz[0:NS, :], nq, ALU.mult))
            chain(v.tensor_reduce(nden, nqz.rearrange("p (h k) -> p h k", h=MH), AX, ALU.add))
            T.dve_num(dve, chain, nden, lambda eng: T.t_out(eng, S_I))
            T.dve_last(dve, chain)
            same = K["same"][:, :]
            v.tensor_tensor(lw, repeat_mid(same, MH), repeat_last(X.lval[0:NS, 0:4], B), ALU.mult)
            v.tensor_tensor(wsel.rearrange("p (b h) -> p b h", b=B), repeat_last(last_of, MH),
                            repeat_mid(X.lval[0:NS, 4:8], B), ALU.mult)
            v.tensor_copy(lv8[:, 0:4], X.lval[0:NS, 4:8])
            v.tensor_copy(lv8[:, 4:8], X.mt[0:NS, :])
            for h in range(MH):
                last = v.tensor_tensor(Km[:, h], repeat_mid(X.kz[0:NS, h * DH:(h + 1) * DH], B), repeat_last(same, DH),
                                       ALU.mult)
            last.then_inc(s["km_ready"], 1)
            T.dve_norm(dve, chain)
            dve.wait_ge(s["w8_full"], 1)
            v.tensor_copy(w8, X.ps_m[0:B, 0:8])
            v.tensor_copy(wlib, X.ps_m[:, 32:32 + B * MH]).then_inc(s["w8_out"], 1)
            dve.wait_ge(s["w8_out"], 1)
            dve.wait_ge(s["nu_full"], 1)
            for h in range(MH):
                cols = slice(h * DH, (h + 1) * DH)
                last = v.scalar_tensor_tensor(n8[:, cols], n8[:, cols], w8[:, h:h + 1], X.ps_n[0][0:B, cols], ALU.mult, ALU.add)
            last.then_inc(s["n_ready"], 1)
            for i in range(2 * MH):
                h, half = i // 2, i % 2
                dve.wait_ge(s["cu_full"], i + 1)
                for j in range(B // 2):
                    m = (half * (B // 2) + j) * MH + h
                    last = v.scalar_tensor_tensor(Cs[:, m, :], Cs[:, m, :], wlib[:, m:m + 1],
                                                  X.ps_s[:, i % 2, j * DH:(j + 1) * DH], ALU.mult, ALU.add)
                last.then_inc(s["cu_out"], 1)
            T.t_landed(dve, S_SC)
            v.scalar_tensor_tensor(sc, X.ps_t[:, :, :].rearrange("p a b -> p (a b)")[:, 0:WIN + NS], AD ** -0.5,
                                   K["s_bias"][:, :], ALU.mult, ALU.add).then_inc(s["t_free"], 1)
            T.t_out(dve, S_SC)
            chain(v.tensor_reduce(X.smx[:, 0:1], sc, AX, ALU.max))
            chain(v.tensor_tensor(X.smx[:, 0:1], X.smx[:, 0:1], X.sink[:, 0:1], ALU.max))
            v.tensor_tensor(X.ses[:, 0:1], X.sink[:, 0:1], X.smx[:, 0:1], ALU.subtract)
            v.tensor_scalar(X.smx[:, 1:2], X.smx[:, 0:1], -1.0, None, ALU.mult).then_inc(s["sc_ready"], 1)
            T.on(dve, "swa_exp")
            chain(v.tensor_tensor(X.ssum[:, 0:1], X.ssum[:, 0:1], X.ses[:, 0:1], ALU.add))
            chain(v.reciprocal(X.ssum[:, 0:1], X.ssum[:, 0:1]))
            v.tensor_scalar(sc, sc, X.ssum[:, 0:1], None, ALU.mult).then_inc(s["pn_ready"], 1)
            T.t_landed(dve, S_P)
            v.tensor_copy(pTc, X.ps_t[:, 0, :])
            v.tensor_copy(pTn, X.ps_t[0:NS, 1, :]).then_inc(s["t_free"], 1)
            T.t_landed(dve, S_CONV)
            v.tensor_copy(full[:, :, :, CK - 1:], X.ps_t[:, 0:2, 0:NS].rearrange("p a (b t) -> p a b t", b=B))
            v.tensor_copy(X.cbT[:, :, 0:NS], X.ps_t[:, 2:4, 0:NS]).then_inc(s["t_free"], 1)
            T.t_landed(dve, S_ST)
            v.tensor_copy(full[:, :, :, 0:CK - 1], X.ps_t[:, 0:2, 0:2 * B].rearrange("p a (b w) -> p a b w", b=B))\
                .then_inc(s["t_free"], 1)
            T.t_out(dve, S_ST)
            for a in range(2):
                last = v.tensor_scalar(y[:, a], full[:, a, :, 0:TS], X.cw[:, 0, a:a + 1], None, ALU.mult)
            chain(last)
            for j in range(1, CK):
                for a in range(2):
                    last = v.scalar_tensor_tensor(y[:, a], full[:, a, :, j:j + TS], X.cw[:, j, a:a + 1], y[:, a],
                                                  ALU.mult, ALU.add)
                chain(last)
            v.tensor_tensor(X.mixT[:, 6:8, 0:NS], y.rearrange("p a b t -> p a (b t)"), X.cbT[:, :, 0:NS], ALU.mult)\
                .then_inc(s["yc_ready"], 1)
            T.t_landed(dve, S_HM)
            v.tensor_copy(X.mixT[:, 0:4, 0:NS], X.ps_t[:, :, 0:NS]).then_inc(s["t_free"], 1)
            T.dve_residual(dve, chain)

        @block.tensor
        def _(pe):
            e = K["ident"]
            T.project(pe, K)
            pe.wait_ge(s["c_in"], 16)
            for i in range(B):
                T.batch(pe, S_C0 + i, [(Cs[:, 4 * i + j, :], P, P) for j in range(4)], e)
            T.t_out(pe, S_I - 1)
            for b in range(B):
                for h in range(MH):
                    mm = nc.tensor.matmul(X.ps_n[1][:, h * NS + b * TS:h * NS + (b + 1) * TS], CTs[:, b * MH + h, :],
                                          X.qT[:, h, b * TS:(b + 1) * TS], start=True, stop=True)
            mm.then_inc(s["si_full"], 1)
            pe.wait_ge(s["int_ready"], 1)
            T.batch(pe, S_I, [(intT[:, h * NS:(h + 1) * NS], P, NS) for h in range(MH)], e)
            T.intra(pe, K)
            T.on(pe, "numf_ready")
            T.on(pe, "vw_ready")
            pe.wait_ge(s["km_ready"], 1)
            nc.tensor.matmul(X.ps_m[0:B, 0:8], last_of, lv8, start=True, stop=True)
            nc.tensor.matmul(X.ps_m[:, 32:32 + B * MH], K["ones"][0:NS, :], wsel, start=True, stop=True)\
                .then_inc(s["w8_full"], 1)
            for h in range(MH):
                mm = nc.tensor.matmul(X.ps_n[0][0:B, h * DH:(h + 1) * DH], lw[:, h, :], X.kz[0:NS, h * DH:(h + 1) * DH],
                                      start=True, stop=True)
            mm.then_inc(s["nu_full"], 1)
            for i in range(2 * MH):
                h, half = i // 2, i % 2
                if i >= 2:
                    pe.wait_ge(s["cu_out"], i - 1)
                nc.tensor.matmul(X.ps_s[:, i % 2, :], X.diag[0:NS, h, :], Km[:, h, half * (B // 2):(half + 1) * (B // 2), :],
                                 start=True, stop=True).then_inc(s["cu_full"], 1)
            pe.wait_ge(s["kv_in"], 32)
            T.batch(pe, S_K0, [(kc[:, b, :], P, P) for b in range(4)], e)
            T.batch(pe, S_K1, [(kc[:, b, :], P, P) for b in range(4, 8)], e)
            T.t_out(pe, S_K1)
            pe.wait_ge(s["n_ready"], 1)
            for h in range(AH):
                kv, g = h // 2, h % 2
                rows = slice(kv * AD, (kv + 1) * AD)
                for b in range(B):
                    nc.tensor.matmul(X.ps_n[kv][:, g * NS + b * TS:g * NS + (b + 1) * TS], kcT[rows, b, :],
                                     X.sqT[rows, g, b * TS:(b + 1) * TS], start=True, stop=True)
                mm = nc.tensor.matmul(X.ps_n[kv][0:NS, P + g * NS:P + (g + 1) * NS], X.skT[rows, P:P + NS],
                                      X.sqT[rows, g, 0:NS], start=True, stop=True)
            mm.then_inc(s["sw_full"], 1)
            pe.wait_ge(s["st_ready"], 1)
            T.batch(pe, S_SC, [(sT, P, P), (sN, NS, P)], e)
            pe.wait_ge(s["pn_ready"], 1)
            T.batch(pe, S_P, [(sc[:, 0:WIN], P, P), (sc[:, WIN:], P, NS)], e)
            T.t_out(pe, S_P)
            pe.wait_ge(s["w8_out"], 1)
            for h in range(AH):
                kv = h // 2
                vals = slice(kv * AD, (kv + 1) * AD)
                out = X.ps_m[(h % 2) * AD:(h % 2 + 1) * AD, P + (h // 2) * NS:P + (h // 2 + 1) * NS]
                nc.tensor.matmul(out, X.g6[0:NS, vals], pTn[:, h * NS:(h + 1) * NS], start=True, stop=False)
                for b in range(B):
                    mm = nc.tensor.matmul(out[:, b * TS:(b + 1) * TS], vc[:, b, vals],
                                          pTc[:, h * NS + b * TS:h * NS + (b + 1) * TS], start=False, stop=(b == B - 1))
            mm.then_inc(s["pv_full"], 1)
            T.on(pe, "u_ready")
            T.batch(pe, S_CONV, [(X.u[0:NS, 0:P], NS, P), (X.u[0:NS, P:], NS, P),
                                 (X.g6[0:NS, 128:256], NS, P), (X.g6[0:NS, 256:384], NS, P)], e)
            pe.wait_ge(s["small2_in"], 16 * (B + 2))
            T.batch(pe, S_ST, [(stc[:, 0:P], 2 * B, P), (stc[:, P:], 2 * B, P)], e)
            T.on(pe, "hm_ready")
            T.batch(pe, S_HM, [(X.h[0:NS, h * DH:(h + 1) * DH], NS, DH) for h in range(MH)], e)
            T.t_out(pe, S_HM)
            T.on(pe, "oa_ready")
            T.out_product(pe)


def second_norm(nc, I, mod, x1_dram, h2_dram, wq, wq_in, K):
    NTS = NT + 1
    with ExitStack() as ctx:
        def sb(name, shape):
            return ctx.enter_context(nc.sbuf_tensor(name, shape, F32))

        x, h = sb("n2_x", [P, NTS, D]), sb("n2_h", [P, NTS, D])
        scale, shift, gain = sb("n2_scale", [P, 2, D]), sb("n2_shift", [P, 2, D]), sb("n2_gain", [P, D])
        eps, ss, rt, r = sb("n2_eps", [P, 1]), sb("n2_ss", [P, NTS]), sb("n2_rt", [P, NTS]), sb("n2_r", [P, NTS])
        s = {n: ctx.enter_context(nc.semaphore("n2_" + n))
             for n in ["rows_in", "init", "ss_ready", "rt_ready", "a_ready", "step", "h_ready", "h_out"]}
        x_in = [ctx.enter_context(nc.semaphore(f"n2_x_in{t}")) for t in range(NTS)]

        with nc.Block() as block:
            @block.sync
            def _(sp):
                for t in range(NT):
                    sp.dma_start(x[:, t, :], x1_dram[t * P:(t + 1) * P, :]).then_inc(x_in[t], 16)
                sp.dma_start(x[0:NS, NT, :], x1_dram[SEQ:SEQ + NS, :]).then_inc(x_in[NT], 16)
                for dst, k in ((scale, 4), (shift, 3)):
                    sp.dma_start(dst[:, 0, :], mod[0, k * D:(k + 1) * D].partition_broadcast(P)).then_inc(s["rows_in"], 16)
                    for b in range(B):
                        sp.dma_start(dst[b * TS:(b + 1) * TS, 1, :],
                                     mod[1 + b, k * D:(k + 1) * D].partition_broadcast(TS)).then_inc(s["rows_in"], 16)
                sp.dma_start(gain[:, :], I["norm_ffn_g"][0].partition_broadcast(P)).then_inc(s["rows_in"], 16)
                sp.dma_start(wq[:, :, :], I["peer_wq"][0].rearrange("(kc p) n -> p kc n", p=P)).then_inc(wq_in, 16)
                for t in range(NTS):
                    sp.wait_ge(s["h_ready"], t + 1)
                    sp.dma_start(h2_dram[t * P:(t + 1) * P, :], h[:, t, :]).then_inc(s["h_out"], 16)
                sp.wait_ge(s["h_out"], 16 * NTS)

            @block.gpsimd
            def _(pool):
                nc.gpsimd.memset(eps[:, :], EPS)
                nc.gpsimd.memset(h[:, NT, :], 0.0).then_inc(s["init"], 1)

            @block.scalar
            def _(act):
                a = nc.scalar.activation
                act.wait_ge(s["init"], 1)
                for t in range(NTS):
                    n = P if t < NT else NS
                    act.wait_ge(x_in[t], 16)
                    a(h[0:n, t, :], x[0:n, t, :], ACT.Square, accum_out=ss[0:n, t:t + 1]).then_inc(s["ss_ready"], 1)
                act.wait_ge(s["ss_ready"], NTS)
                a(rt[:, 0:NT], ss[:, 0:NT], ACT.Sqrt, scale=1.0 / D, bias=eps[:, :])
                a(rt[0:NS, NT:], ss[0:NS, NT:], ACT.Sqrt, scale=1.0 / D, bias=eps[0:NS, :]).then_inc(s["rt_ready"], 1)

            @block.vector
            def _(dve):
                chain = Chain(dve, s["step"])
                v = nc.vector
                dve.wait_ge(s["rows_in"], 16 * (2 * (1 + B) + 1))
                v.scalar_tensor_tensor(scale[:, 0, :], scale[:, 0, :], 1.0, gain[:, :], ALU.add, ALU.mult)
                chain(v.scalar_tensor_tensor(scale[0:NS, 1, :], scale[0:NS, 1, :], 1.0, gain[0:NS, :], ALU.add, ALU.mult))
                dve.wait_ge(s["rt_ready"], 1)
                v.reciprocal(r[:, 0:NT], rt[:, 0:NT])
                chain(v.reciprocal(r[0:NS, NT:], rt[0:NS, NT:]))
                for t in range(NTS):
                    n, k = (P, 0) if t < NT else (NS, 1)
                    chain(v.scalar_tensor_tensor(h[0:n, t, :], x[0:n, t, :], r[0:n, t:t + 1], scale[0:n, k, :],
                                                 ALU.mult, ALU.mult))
                    v.tensor_tensor(h[0:n, t, :], h[0:n, t, :], shift[0:n, k, :], ALU.add).then_inc(s["h_ready"], 1)


NB = 8
GPT = PH * TOPK // NB
PPT = GPT // 2
NG = NT * GPT
QS = P // NS
SG = PH * TOPK // QS // NB


def experts(nc, I, O, mod, x1_dram, h2_dram, wq, wq_in, K):
    with ExitStack() as ctx:
        def sb(name, shape, dt=F32):
            return ctx.enter_context(nc.sbuf_tensor(name, shape, dt))

        def ps(name, shape):
            return ctx.enter_context(nc.psum_tensor(name, shape, F32))

        h_next, hT = sb("h_next", [P, D]), sb("hT_next", [P, KC, P])
        sub, subT = sb("subkeys", [PK, 2, P]), sb("subkeysT", [P, 2, PK])
        q, qT, sc, scw = sb("q", [P, 2, P]), sb("qT", [P, 2, P]), sb("key_scores", [P, 2, PK]), sb("key_scores_w", [P, 2, PK])
        top, topi, topf = sb("top", [P, 2, TOPK]), sb("top_i", [P, 2, TOPK], U32), sb("top_f", [P, 2, TOPK])
        cand, candw = sb("cand", [P, TOPK * TOPK]), sb("cand_w", [P, TOPK * TOPK])
        cs, ci = sb("cand_top", [P, TOPK]), sb("cand_i", [P, TOPK], U32)
        ab, abf = sb("sel_ab", [P, 2, TOPK], U32), sb("sel_abf", [P, 2, TOPK])
        hot, sel = sb("one_hot", [P, 2, TOPK, TOPK]), sb("selected", [P, 2, TOPK])
        iota = sb("iota_f", [P, TOPK])
        idx = sb("expert_idx", [P, (NT + 1) * PH * TOPK], U32)
        gate = sb("expert_gate", [P, (NT + 1) * PH * TOPK])
        gsum = sb("gate_sum", [P, PH])
        idx_s, gate_s = sb("sample_idx", [P, SG * NB], U32), sb("sample_gate", [P, SG * NB])
        h_cur = sb("h_cur", [P, D])
        u_rows, v_rows = sb("u_rows", [P, NB, D]), sb("v_rows", [P, NB, D])
        u_idx, v_idx = sb("u_idx", [P, 2, NB], U32), sb("v_idx", [P, 2, NB], U32)
        dots, act_val, wts = sb("dots", [P, 2, NB]), sb("act_val", [P, 2, NB]), sb("wts", [P, 2, NB])
        diag = sb("wt_diag", [P, 2, NB, P])
        x1, y, gate2, gate2_s, fin = sb("x1", [P, D]), sb("y", [P, D]), sb("gate2", [P, D]), sb("gate2_s", [NS, D]), sb("final_g", [P, D])
        fs, eps = sb("final_stat", [P, 4]), sb("eps2", [P, 1])
        fold = sb("fold", [P, NS])
        ps_y, ps_h, ps_r = ps("ps_y", [P, D]), ps("ps_h", [P, KC, P]), ps("ps_r", [P, 3, 512])
        names = ("sub_in small_in init subT_full subT_out hn_in hT_full hT_out copied q_full q_out qt_full qt_out sc_full "
                 "sc_out sc_free routed exp_ready normed spread_in hs_in u_staged v_staged u_used v_used "
                 "act_ready wts_ready diag_ready y_out x1_in ss_ready rt_ready done stored step "
                 "folded sub_step").split()
        s = {n: ctx.enter_context(nc.semaphore("ex_" + n)) for n in names}
        u_in = [ctx.enter_context(nc.semaphore(f"u_in{j}")) for j in range(NB)]
        v_in = [ctx.enter_context(nc.semaphore(f"v_in{j}")) for j in range(NB)]

        with nc.Block() as block:
            @block.sync
            def _(sp):
                sp.dma_start(sub[:, :, :], I["peer_subkeys"][0].rearrange("a k d -> k a d")).then_inc(s["sub_in"], 16)
                sp.dma_start(h_next[:, :], h2_dram[0:P, :]).then_inc(s["hn_in"], 16)
                sp.dma_start(gate2[:, :], mod[0, 5 * D:6 * D].partition_broadcast(P)).then_inc(s["small_in"], 16)
                for b in range(B):
                    sp.dma_start(gate2_s[b * TS:(b + 1) * TS, :], mod[1 + b, 5 * D:6 * D].partition_broadcast(TS))\
                        .then_inc(s["small_in"], 16)
                sp.dma_start(fin[:, :], I["final_g"].partition_broadcast(P)).then_inc(s["small_in"], 16)
                sp.dma_start(x1[:, :], x1_dram[0:P, :]).then_inc(s["x1_in"], 16)

                def next_rows(t):
                    hold(sp, s["copied"], t + 1)
                    hold(sp, s["hT_out"], t + 1)
                    sp.dma_start(h_next[:, :], h2_dram[bass.ds(t * P + P, P), :]).then_inc(s["hn_in"], 16)

                def finish(t, rows=P):
                    hold(sp, s["done"], t + 1)
                    sp.dma_start(O["y_p"][0, bass.ds(t * P, P), :], x1[:, :]).then_inc(s["stored"], 16)
                    hold(sp, s["stored"], t * 16 + 16)
                    sp.dma_start(x1[0:rows, :], x1_dram[bass.ds(t * P + P, rows), :]).then_inc(s["x1_in"], 16)

                next_rows(0)
                with sp.Fori(0, NT - 1) as t:
                    next_rows(t + 1)
                    finish(t)
                sp.wait_ge(s["normed"], NT + 1)
                for i in range(QS):
                    rows, cols = slice(i * NS, (i + 1) * NS), slice(NT * P + i * SG * NB, NT * P + (i + 1) * SG * NB)
                    sp.dma_start(idx_s[rows, :], idx[0:NS, cols]).then_inc(s["spread_in"], 16)
                    sp.dma_start(gate_s[rows, :], gate[0:NS, cols]).then_inc(s["spread_in"], 16)
                sp.wait_ge(s["u_used"], NG * NB)
                for i in range(QS):
                    sp.dma_start(h_cur[i * NS:(i + 1) * NS, :], h2_dram[SEQ:SEQ + NS, :]).then_inc(s["hs_in"], 16)
                finish(NT - 1, NS)
                sp.wait_ge(s["done"], NT + 1)
                sp.dma_start(O["y_s"].rearrange("b t d -> (b t) d"), x1[0:NS, :]).then_inc(s["stored"], 16)
                sp.wait_ge(s["stored"], 16 * (NT + 1))

            @block.gpsimd
            def _(pool):
                g = nc.gpsimd
                g.tensor_copy(iota[:, :], K["iota16"][:, :])
                g.memset(eps[:, :], EPS)
                g.memset(fold[:, :], 0.0).then_inc(s["init"], 1)
                pool.wait_ge(s["init"], 1)
                for i in range(QS):
                    g.affine_select(out=fold[:, :], in_=fold[:, :], compare_op=ALU.not_equal, fill=1.0, base=-i * NS,
                                    pattern=[[-1, NS]], channel_multiplier=1).then_inc(s["init"], 1)
                    pool.wait_ge(s["init"], 2 + i)

                def gather(rows, table, where, landed, used, i, j, first=False):
                    if not first:
                        hold(pool, used, i * NB + (j + 1 - NB))
                    g.indirect_dma_start(rows[:, j, :], None, table, bass.IndirectOffsetOnAxis(where[:, j:j + 1], 0))\
                        .then_inc(landed[j], 16)

                def stage(dst, src, signal, used, i, par, first=False):
                    if not first:
                        hold(pool, used, i * NB - NB)
                    g.tensor_copy(dst[:, par, :], src).then_inc(signal, 1)
                    hold(pool, signal, i + 1)

                U, V = I["peer_u"][0], I["peer_v"][0]

                def step(i, par, u_src, v_src, first=False):
                    stage(u_idx, u_src, s["u_staged"], s["u_used"], i, par, first)
                    stage(v_idx, v_src, s["v_staged"], s["v_used"], i - 1, 1 - par, first or (isinstance(i, int) and i == 2))
                    for j in range(NB):
                        gather(u_rows, U, u_idx[:, par], u_in, s["u_used"], i, j)
                        gather(v_rows, V, v_idx[:, 1 - par], v_in, s["v_used"], i - 1, j, first)

                def cols(i):
                    return idx[:, bass.ds(i * NB, NB)]

                pool.wait_ge(s["routed"], PH)
                stage(u_idx, cols(0), s["u_staged"], s["u_used"], 0, 0, True)
                for j in range(NB):
                    gather(u_rows, U, u_idx[:, 0], u_in, s["u_used"], 0, j, True)
                step(1, 1, cols(1), cols(0), True)
                step(2, 0, cols(2), cols(1))
                step(3, 1, cols(3), cols(2))
                with pool.Fori(2, NG // 2) as pair:
                    hold(pool, s["routed"], pair + 1)
                    first = pair * 2
                    for par in range(2):
                        step(first + par, par, idx[:, bass.ds(pair * (2 * NB) + par * NB, NB)],
                             idx[:, bass.ds(pair * (2 * NB) + (par - 1) * NB, NB)])
                pool.wait_ge(s["spread_in"], 2 * 16 * QS)
                for i in range(NG, NG + SG):
                    step(i, i % 2, idx_s[:, (i - NG) * NB:(i - NG + 1) * NB],
                         cols(i - 1) if i == NG else idx_s[:, (i - 1 - NG) * NB:(i - NG) * NB])
                i = NG + SG
                stage(v_idx, idx_s[:, (SG - 1) * NB:], s["v_staged"], s["v_used"], i - 1, (i - 1) % 2)
                for j in range(NB):
                    gather(v_rows, V, v_idx[:, (i - 1) % 2], v_in, s["v_used"], i - 1, j)

            @block.scalar
            def _(act):
                a = nc.scalar.activation

                def hT_copy(t):
                    hold(act, s["hT_full"], t + 1)
                    a(hT[:, 0:4, :], ps_h[:, 0:4, :], ACT.Copy)
                    a(hT[:, 4:8, :], ps_h[:, 4:8, :], ACT.Copy).then_inc(s["hT_out"], 1)

                def head(H):
                    hold(act, s["q_full"], H + 1)
                    a(q[:, :, :], ps_r[:, 0, 0:256], ACT.Copy).then_inc(s["q_out"], 1)
                    hold(act, s["qt_full"], H + 1)
                    a(qT[:, :, :], ps_r[:, 1, 0:256], ACT.Copy).then_inc(s["qt_out"], 1)
                    hold(act, s["sc_full"], H + 1)
                    hold(act, s["sc_free"], H + 1)
                    a(sc[:, :, :], ps_r[:, 2, 0:256], ACT.Copy).then_inc(s["sc_out"], 1)

                def group(i, par, first=False):
                    hold(act, s["u_used"], i * NB + NB)
                    a(act_val[:, par, :], dots[:, par, :], ACT.Gelu_apprx_tanh).then_inc(s["act_ready"], 1)
                    if not first:
                        hold(act, s["v_used"], i * NB - NB)
                    hold(act, s["wts_ready"], i + 1)
                    for j in range(NB):
                        a(diag[:, par, j, :], K["ident"][:, :], ACT.Copy, scale=wts[:, par, j:j + 1])\
                            .then_inc(s["diag_ready"], 1)

                def gate_exp(t):
                    hold(act, s["routed"], t * PH + PH)
                    cols = bass.ds(t * P, P)
                    a(gate[:, cols], gate[:, cols], ACT.Exp).then_inc(s["exp_ready"], 1)

                def y_copy(last_group):
                    hold(act, s["v_used"], last_group * NB + NB)
                    a(y[:, 0:512], ps_y[:, 0:512], ACT.Copy)
                    a(y[:, 512:D], ps_y[:, 512:D], ACT.Copy).then_inc(s["y_out"], 1)

                def root(t, n=P):
                    hold(act, s["ss_ready"], t + 1)
                    a(fs[0:n, 1:2], fs[0:n, 0:1], ACT.Sqrt, scale=1.0 / D, bias=eps[0:n, :]).then_inc(s["rt_ready"], 1)

                act.wait_ge(s["init"], 1 + QS)
                act.wait_ge(s["subT_full"], 1)
                a(subT[:, :, :], ps_r[:, 1, 0:256], ACT.Copy).then_inc(s["subT_out"], 1)
                hT_copy(0)
                with act.Fori(0, PH) as H:
                    head(H)
                gate_exp(0)
                group(0, 0, True)
                hT_copy(1)
                head(PH)
                group(1, 1, True)
                with act.Fori(0, NT - 1) as t:
                    with act.Fori(1, PPT) as p:
                        i = t * GPT + p * 2
                        group(i, 0)
                        head(t * PH + PH + p)
                        group(i + 1, 1)
                    i = t * GPT + GPT
                    gate_exp(t + 1)
                    group(i, 0)
                    y_copy(t * GPT + (GPT - 1))
                    hT_copy(t + 2)
                    head(t * PH + 2 * PH)
                    group(i + 1, 1)
                    root(t)
                with act.Fori(1, PPT) as p:
                    i = p * 2 + (NT - 1) * GPT
                    group(i, 0)
                    head(p + NT * PH)
                    group(i + 1, 1)
                gate_exp(NT)
                group(NG, 0)
                y_copy(NG - 1)
                group(NG + 1, 1)
                root(NT - 1)
                group(NG + 2, 0)
                group(NG + 3, 1)
                y_copy(NG + SG - 1)
                root(NT, NS)

            @block.vector
            def _(dve):
                chain = Chain(dve, s["step"])
                v = nc.vector

                def group(i, par, gates):
                    for j in range(NB):
                        hold(dve, u_in[j], i * 16 + 16)
                        v.tensor_tensor_reduce(u_rows[:, j, :], u_rows[:, j, :], h_cur[:, :], 1.0, 0.0, ALU.mult, ALU.add,
                                               dots[:, par, j:j + 1]).then_inc(s["u_used"], 1)
                    hold(dve, s["act_ready"], i + 1)
                    v.tensor_tensor(wts[:, par, :], act_val[:, par, :], gates, ALU.mult).then_inc(s["wts_ready"], 1)

                def top16(vals, where, scores, work):
                    chain(v.max(vals[:, 0:8], scores))
                    chain(v.match_replace(work, vals[:, 0:8], scores, NEG))
                    chain(v.max(vals[:, 8:16], work))
                    v.max_index(where[:, 0:8], vals[:, 0:8], scores)
                    return v.max_index(where[:, 8:16], vals[:, 8:16], work)

                def route(H):
                    hold(dve, s["sc_out"], H + 1)
                    top16(top[:, 0], topi[:, 0], sc[:, 0, :], scw[:, 0, :])
                    top16(top[:, 1], topi[:, 1], sc[:, 1, :], scw[:, 1, :]).then_inc(s["sc_free"], 1)
                    v.tensor_tensor(cand[:, :].rearrange("p (a b) -> p a b", a=TOPK), repeat_last(top[:, 0, :], TOPK),
                                    repeat_mid(top[:, 1, :], TOPK), ALU.add).then_inc(s["sub_step"], 1)
                    hold(dve, s["sub_step"], H + 1)
                    v.tensor_copy(topf[:, :, :], topi[:, :, :])
                    chain(top16(cs, ci, cand[:, :], candw[:, :]))
                    cols = bass.ds(H * TOPK, TOPK)
                    v.tensor_scalar(gate[:, cols], cs[:, :], cs[:, 0:1], None, ALU.subtract)
                    v.tensor_scalar(ab[:, 0, :], ci[:, :], 4, None, ALU.logical_shift_right)
                    chain(v.tensor_scalar(ab[:, 1, :], ci[:, :], 15, None, ALU.bitwise_and))
                    chain(v.tensor_copy(abf[:, :, :], ab[:, :, :]))
                    for k in range(2):
                        last = v.tensor_tensor(hot[:, k], repeat_last(abf[:, k, :], TOPK), repeat_mid(iota[:, :], TOPK),
                                               ALU.is_equal)
                    chain(last)
                    for k in range(2):
                        last = v.tensor_tensor(hot[:, k], hot[:, k], repeat_mid(topf[:, k, :], TOPK), ALU.mult)
                    chain(last)
                    chain(v.tensor_reduce(sel[:, :, :], hot[:, :, :, :], AX, ALU.add))
                    v.scalar_tensor_tensor(idx[:, cols], sel[:, 0, :], float(PK), sel[:, 1, :], ALU.mult, ALU.add)\
                        .then_inc(s["routed"], 1)

                ROUTE = 15

                def normalise(t):
                    hold(dve, s["exp_ready"], t + 1)
                    g3 = gate[:, bass.ds(t * P, P)].rearrange("p (h k) -> p h k", h=PH)
                    chain(v.tensor_reduce(gsum[:, :], g3, AX, ALU.add))
                    chain(v.reciprocal(gsum[:, :], gsum[:, :]))
                    v.tensor_tensor(g3, g3, repeat_last(gsum[:, :], TOPK), ALU.mult).then_inc(s["normed"], 1)
                    hold(dve, s["normed"], t + 1)

                def begin(t):
                    hold(dve, s["hn_in"], t * 16 + 16)
                    v.tensor_copy(h_cur[:, :], h_next[:, :]).then_inc(s["copied"], 1)
                    hold(dve, s["copied"], t + 1)
                    normalise(t)

                def finish(t, n, src, row):
                    hold(dve, s["x1_in"], t * 16 + 16)
                    chain(v.tensor_tensor(y[0:n, :], src, row, ALU.mult))
                    chain(v.tensor_tensor(x1[0:n, :], x1[0:n, :], y[0:n, :], ALU.add))
                    v.tensor_tensor_reduce(y[0:n, :], x1[0:n, :], x1[0:n, :], 1.0, 0.0, ALU.mult, ALU.add, fs[0:n, 0:1])\
                        .then_inc(s["ss_ready"], 1)
                    hold(dve, s["rt_ready"], t + 1)
                    chain(v.reciprocal(fs[0:n, 2:3], fs[0:n, 1:2]))
                    v.scalar_tensor_tensor(x1[0:n, :], x1[0:n, :], fs[0:n, 2:3], fin[0:n, :], ALU.mult, ALU.mult)\
                        .then_inc(s["done"], 1)

                def gates(i):
                    return gate[:, bass.ds(i * NB, NB)]

                dve.wait_ge(s["init"], 1 + QS)
                v.memset(fs[:, :], 0.0).then_inc(s["sc_free"], 1)
                with dve.Fori(0, PH) as H:
                    chain.enter(H, ROUTE)
                    route(H)
                chain.leave(PH)
                begin(0)
                group(0, 0, gates(0))
                group(1, 1, gates(1))
                route(PH)
                TILE = (PPT - 1) * ROUTE + ROUTE + 2 + 3
                outer = chain.base + chain.n
                with dve.Fori(0, NT - 1) as t:
                    chain.base, chain.n = t * TILE + outer, 0
                    with dve.Fori(1, PPT) as p:
                        chain.base, chain.n = t * TILE + p * ROUTE + (outer - ROUTE), 0
                        i = t * GPT + p * 2
                        group(i, 0, gate[:, bass.ds(t * P + p * TOPK, NB)])
                        group(i + 1, 1, gate[:, bass.ds(t * P + p * TOPK + NB, NB)])
                        route(t * PH + PH + p)
                        assert chain.n == ROUTE
                    chain.base, chain.n = t * TILE + outer + (PPT - 1) * ROUTE, 0
                    begin(t + 1)
                    i = t * GPT + GPT
                    group(i, 0, gates(i))
                    group(i + 1, 1, gates(i + 1))
                    route(t * PH + 2 * PH)
                    hold(dve, s["small_in"], 16 * (B + 2))
                    hold(dve, s["y_out"], t + 1)
                    finish(t, P, y[:, :], gate2[:, :])
                    assert chain.n == ROUTE + 2 + 3, chain.n
                base = outer + (NT - 1) * TILE
                with dve.Fori(1, PPT) as p:
                    chain.base, chain.n = p * ROUTE + (base - ROUTE), 0
                    i = p * 2 + (NT - 1) * GPT
                    group(i, 0, gate[:, bass.ds(p * TOPK + (NT - 1) * P, NB)])
                    group(i + 1, 1, gate[:, bass.ds(p * TOPK + ((NT - 1) * P + NB), NB)])
                    route(p + NT * PH)
                chain.base, chain.n = base + (PPT - 1) * ROUTE, 0
                normalise(NT)
                dve.wait_ge(s["hs_in"], 16 * QS)
                dve.wait_ge(s["spread_in"], 2 * 16 * QS)
                for i in range(SG):
                    group(NG + i, i % 2, gate_s[:, i * NB:(i + 1) * NB])
                    if i == 1:
                        dve.wait_ge(s["y_out"], NT)
                        finish(NT - 1, P, y[:, :], gate2[:, :])
                dve.wait_ge(s["folded"], 2)
                finish(NT, NS, ps_h[0:NS, :, :].rearrange("p a b -> p (a b)"), gate2_s[:, :])

            @block.tensor
            def _(pe):
                e = K["ident"]

                def rows_t(t):
                    hold(pe, s["hn_in"], t * 16 + 16)
                    for kc in range(KC):
                        last = nc.tensor.transpose(ps_h[:, kc, :], h_next[:, kc * P:(kc + 1) * P], e[:, :])
                    last.then_inc(s["hT_full"], 1)
                    hold(pe, s["hT_out"], t + 1)

                def head(H, h):
                    for kc in range(KC):
                        mm = nc.tensor.matmul(ps_r[:, 0, 0:256], hT[:, kc, :], wq[:, kc, bass.ds(h * 256, 256)],
                                              start=(kc == 0), stop=(kc == KC - 1))
                    mm.then_inc(s["q_full"], 1)
                    hold(pe, s["q_out"], H + 1)
                    for k in range(2):
                        last = nc.tensor.transpose(ps_r[:, 1, k * P:(k + 1) * P], q[:, k, :], e[:, :])
                    last.then_inc(s["qt_full"], 1)
                    hold(pe, s["qt_out"], H + 1)
                    hold(pe, s["sc_free"], H + 1)
                    for k in range(2):
                        mm = nc.tensor.matmul(ps_r[:, 2, k * PK:(k + 1) * PK], qT[:, k, :], subT[:, k, :], start=True, stop=True)
                    mm.then_inc(s["sc_full"], 1)

                def group(i, par, first=False):
                    for j in range(NB):
                        hold(pe, s["diag_ready"], i * NB + (j + 1))
                        hold(pe, v_in[j], i * 16 + 16)
                        for c in range(2):
                            mm = nc.tensor.matmul(ps_y[:, c * 512:(c + 1) * 512], diag[:, par, j, :],
                                                  v_rows[:, j, c * 512:(c + 1) * 512], start=(first and j == 0), stop=False,
                                                  skip_group_check=True)
                        mm.then_inc(s["v_used"], 1)

                pe.wait_ge(s["sub_in"], 16)
                for k in range(2):
                    last = nc.tensor.transpose(ps_r[:, 1, k * PK:(k + 1) * PK], sub[:, k, :], e[:, :])
                last.then_inc(s["subT_full"], 1)
                pe.wait_ge(s["subT_out"], 1)
                rows_t(0)
                pe.wait_ge(wq_in, 16)
                with pe.Fori(0, PH) as H:
                    head(H, H)
                rows_t(1)
                head(PH, 0)
                group(0, 0, True)
                group(1, 1)
                with pe.Fori(0, NT - 1) as t:
                    with pe.Fori(1, PPT) as p:
                        i = t * GPT + p * 2
                        head(t * PH + PH + p, p)
                        group(i, 0)
                        group(i + 1, 1)
                    i = t * GPT + GPT
                    rows_t(t + 2)
                    head(t * PH + 2 * PH, 0)
                    hold(pe, s["y_out"], t + 1)
                    group(i, 0, True)
                    group(i + 1, 1)
                with pe.Fori(1, PPT) as p:
                    i = p * 2 + (NT - 1) * GPT
                    head(p + NT * PH, p)
                    group(i, 0)
                    group(i + 1, 1)
                pe.wait_ge(s["y_out"], NT)
                for i in range(SG):
                    group(NG + i, i % 2, i == 0)
                pe.wait_ge(s["y_out"], NT + 1)
                for c in range(2):
                    nc.tensor.matmul(ps_h[0:NS, 4 * c:4 * c + 4, :], fold[:, :], y[:, c * 512:(c + 1) * 512],
                                     start=True, stop=True).then_inc(s["folded"], 1)


def trunk_step(nc, I, O):
    mod = nc.dram_tensor("mod_rows", (NC, 6 * D), F32, kind="Internal").ap()
    x1_dram = nc.dram_tensor("x1_rows", (SEQ + P, D), F32, kind="Internal").ap()
    with ExitStack() as ctx:
        def const(name, shape, dt=F32):
            return ctx.enter_context(nc.sbuf_tensor(name, shape, dt))

        K = {"ident": const("ident", [P, P]), "ones": const("ones", [P, P]), "iota16": const("iota16", [P, TOPK], I32)}
        with ExitStack() as mix:
            def mconst(name, shape):
                return mix.enter_context(nc.sbuf_tensor(name, shape, F32))

            K.update(tri=mconst("tri", [P, P]), mask=mconst("mask", [P, P]), last=mconst("last", [P, P]),
                     tri_s=mconst("tri_s", [NS, NS]), mask_s=mconst("mask_s", [NS, NS]), last_s=mconst("last_s", [NS, NS]),
                     same=mconst("same", [NS, B]), s_bias=mconst("s_bias", [P, WIN + NS]), bias=mconst("swa_bias", [P, AH, 2 * P]),
                     live_bias=mconst("swa_live_bias", [P, AH, 2 * P]))
            make_constants(nc, K)
            w_in = mix.enter_context(nc.sbuf_tensor("w_in", [P, KC, INW], F32))
            s = {n: nc.alloc_semaphore("mix_" + n) for n in SIGNALS}
            s["w_in_in"] = nc.alloc_semaphore("mix_w_in_in")
            modulation_rows(nc, I, mod, w_in, s["w_in_in"], K)
            X = Mixer(nc, mix, w_in)
            mix_prompt(nc, I, O, mod, x1_dram, X, K, s)
            s2 = {n: nc.alloc_semaphore("smp_" + n) for n in SIGNALS + EXTRA if n != "w_out_in"}
            s2["w_out_in"] = s["w_out_in"]
            mix_sample(nc, I, O, mod, x1_dram, X, K, s2)
        del s2["w_out_in"]
        nc.clear_and_free_semaphores([*s.values(), *s2.values()])
        nc.all_engine_barrier()
        h2_dram = nc.dram_tensor("h2_rows", (SEQ + P, D), F32, kind="Internal").ap()
        wq = ctx.enter_context(nc.sbuf_tensor("wq", [P, KC, PH * 2 * P], F32))
        wq_in = ctx.enter_context(nc.semaphore("wq_in"))
        second_norm(nc, I, mod, x1_dram, h2_dram, wq, wq_in, K)
        experts(nc, I, O, mod, x1_dram, h2_dram, wq, wq_in, K)


_OUTS = [("y_p", (1, SEQ, D)), ("y_s", (B, TS, D)),
         ("swa_k_p", (1, 1, WIN, KVH, AD)), ("swa_v_p", (1, 1, WIN, KVH, AD)), ("conv_p", (1, 1, CK - 1, CW)),
         ("C_p", (1, 1, MH, DH, DH)), ("n_p", (1, 1, MH, DH)), ("m_p", (1, 1, MH)),
         ("swa_k_s", (1, B, WIN, KVH, AD)), ("swa_v_s", (1, B, WIN, KVH, AD)), ("conv_s", (1, B, CK - 1, CW)),
         ("C_s", (1, B, MH, DH, DH)), ("n_s", (1, B, MH, DH)), ("m_s", (1, B, MH))]


def kernel(**inputs):
    import numpy as _np
    import concourse.bacc as _bacc
    from concourse import mybir as _mybir
    from concourse.bass_utils import run_bass_kernel_spmd as _run

    nc = _bacc.Bacc("TRN2", target_bir_lowering=False, num_devices=1)
    arrays, ins, outs = {}, {}, {}
    for name, a in inputs.items():
        a = _np.ascontiguousarray(a)
        arrays[f"in_{name}_dram"] = a
        ins[name] = nc.dram_tensor(f"in_{name}_dram", a.shape, _mybir.dt.from_np(a.dtype), kind="ExternalInput").ap()
    for name, shape in _OUTS:
        outs[name] = nc.dram_tensor(f"out_{name}_dram", shape, F32, kind="ExternalOutput").ap()
    trunk_step(nc, ins, outs)
    r = _run(nc, [arrays], core_ids=[0])
    return tuple(r.results[0][f"out_{name}_dram"] for name, _ in _OUTS)
```

```python
from contextlib import ExitStack

import concourse.bass as bass
from concourse import mybir

F32 = mybir.dt.float32
U32 = mybir.dt.uint32
I32 = mybir.dt.int32
ALU = mybir.AluOpType
ACT = mybir.ActivationFunctionType
AX = mybir.AxisListType.X

P = 128
D = 1024
KC = D // P
SEQ = 512
NT = SEQ // P
B = 8
TS = 4
NS = B * TS
NC = 1 + B
MH, DH = 4, 128
MW = MH * DH
AH, KVH, AD = 4, 2, 64
WIN = 128
CW, CK = 256, 3
INW = 3336
EPS = 1e-6
NEG = -1e30
KSCALE = DH ** -0.5
SLOPES = [2.0 ** (-8.0 * (h + 1) / AH) for h in range(AH)]
W_IN_LOADS = 4
PH, PK, TOPK, NEXP = 8, 128, 16, 16384

GATES, QZ, KZ, VZ, SVCB, CCCH, OZ = range(7)
CHUNKS = [(2048, 2440), (0, 512), (512, 1024), (1024, 1536), (2440, 2824), (2824, 3336), (1536, 2048)]


def hold(eng, sem, value):
    eng.wait_ge(sem, value)
    if not isinstance(value, int):
        eng.nop(nofuse=True)


class Chain:

    def __init__(self, eng, sem):
        self.eng, self.sem, self.base, self.n = eng, sem, 0, 0

    def __call__(self, ins):
        ins.then_inc(self.sem, 1)
        self.n += 1
        hold(self.eng, self.sem, self.base + self.n)

    def enter(self, t, per):
        self.start, self.per = self.base + self.n, per
        self.base, self.n = t * per + self.start, 0

    def leave(self, trips):
        assert self.n == self.per, (self.n, self.per)
        self.base, self.n = self.start + trips * self.per, 0


def same_cols(ap, n):
    return ap.rearrange("p (m o) -> p m o", o=1).to_broadcast([ap.shape[0], ap.shape[1], n])


def repeat_last(ap, n):
    return ap.unsqueeze(len(ap.shape)).broadcast_to([*ap.shape, n])


def repeat_mid(ap, n):
    return ap.unsqueeze(1).broadcast_to([ap.shape[0], n, *ap.shape[1:]])


class ConstantBuffers:

    def __init__(self, nc, ctx):
        def sb(name, shape, dt=F32):
            return ctx.enter_context(nc.sbuf_tensor(name, shape, dt))

        def sem(name):
            return ctx.enter_context(nc.semaphore(name))

        self.ident_ready, self.cleared, self.dist_ready = sem("const_ident"), sem("const_cleared"), sem("const_dist")
        self.bias_ready, self.sdist_ready, self.s_step = sem("const_bias"), sem("const_sdist"), sem("const_s_step")
        self.dist_i, self.dist = sb("dist_i", [P, 2 * P], I32), sb("dist", [P, 2 * P])
        self.sdist_i, self.sdist = sb("sdist_i", [P, WIN + NS], I32), sb("sdist", [P, WIN + NS])
        self.tpat_i, self.tpat = sb("tpat_i", [P, P], I32), sb("tpat", [P, P])
        self.cols = sb("row_cols", [P, 2])
        self.beyond = sb("beyond", [P, WIN + NS])


def constants_dve(nc, dve, K, C):
    v = nc.vector
    for h in range(AH):
        v.memset(C.cols[h * NS:(h + 1) * NS, 1:2], -SLOPES[h])
    dve.wait_ge(C.sdist_ready, 1)
    v.tensor_tensor(C.tpat[:, :], C.tpat[:, :], K["ident"][:, :], ALU.mult).then_inc(C.s_step, 1)
    dve.wait_ge(C.s_step, 1)
    v.tensor_reduce(C.cols[:, 0:1], C.tpat[:, :], AX, ALU.add).then_inc(C.s_step, 1)
    dve.wait_ge(C.s_step, 2)
    v.tensor_scalar(K["s_bias"][:, :], C.sdist[:, :], C.cols[:, 0:1], C.cols[:, 1:2], ALU.add, ALU.mult)
    v.tensor_scalar(C.beyond[:, :], C.sdist[:, :], C.cols[:, 0:1], float(WIN), ALU.add, ALU.is_gt).then_inc(C.s_step, 1)
    dve.wait_ge(C.s_step, 3)
    v.scalar_tensor_tensor(K["s_bias"][:, :], C.beyond[:, :], NEG, K["s_bias"][:, :], ALU.mult, ALU.add)\
        .then_inc(C.s_step, 1)
    dve.wait_ge(C.dist_ready, 1)
    for h in range(AH):
        last = v.tensor_copy(C.tpat[h * NS:(h + 1) * NS, 0:NS], K["mask_s"][:, :])
    last.then_inc(C.s_step, 1)
    dve.wait_ge(C.s_step, 5)
    v.tensor_tensor(K["s_bias"][:, WIN:], K["s_bias"][:, WIN:], C.tpat[:, 0:NS], ALU.add)


def constants_pool(nc, pool, K, C):
    g = nc.gpsimd
    g.memset(K["ident"][:, :], 0.0).then_inc(C.ident_ready, 1)
    pool.wait_ge(C.ident_ready, 1)
    g.affine_select(out=K["ident"][:, :], in_=K["ident"][:, :], compare_op=ALU.not_equal, fill=1.0, base=0,
                    pattern=[[-1, P]], channel_multiplier=1).then_inc(C.ident_ready, 1)
    g.iota(C.sdist_i[:, 0:WIN], pattern=[[-1, WIN]], base=WIN, channel_multiplier=0)
    g.iota(C.sdist_i[:, WIN:].rearrange("p (b i) -> p b i", i=TS), pattern=[[0, B], [-1, TS]], base=0, channel_multiplier=0)
    g.iota(C.tpat_i[:, :].rearrange("p (a i) -> p a i", i=TS), pattern=[[0, P // TS], [1, TS]], base=0,
           channel_multiplier=0)
    zero = [K["tri"], K["mask"], K["last"], K["tri_s"], K["mask_s"], K["last_s"], K["same"]]
    for m in zero:
        g.memset(m[:], 0.0)
    g.memset(K["ones"][:], 1.0)
    g.memset(K["live_bias"][:, :, 0:P], NEG)
    g.iota(C.dist_i[:, :], pattern=[[-1, 2 * P]], base=P, channel_multiplier=1)
    g.iota(K["iota16"][:, :], pattern=[[1, TOPK]], base=0, channel_multiplier=0).then_inc(C.cleared, 1)
    pool.wait_ge(C.cleared, 1)

    def fill(m, pattern, op, value, base, per_row):
        return g.affine_select(out=m, in_=m, compare_op=op, fill=value, base=base,
                               pattern=pattern, channel_multiplier=per_row)

    def blocks(m):
        return m.rearrange("p (b i) -> p b i", i=TS)

    fill(K["tri"][:, :], [[-1, P]], ALU.is_gt, 1.0, 0, 1)
    fill(K["mask"][:, :], [[-1, P]], ALU.is_ge, NEG, 0, 1)
    fill(K["last"][:, :], [[0, P]], ALU.not_equal, 1.0, -(P - 1), 1)
    fill(blocks(K["mask_s"][:, :]), [[-TS, B], [-1, TS]], ALU.is_ge, NEG, 0, 1)
    fill(K["tri_s"][:, :], [[-1, NS]], ALU.is_gt, 1.0, 0, 1)
    fill(blocks(K["last_s"][:, :]), [[-TS, B], [0, TS]], ALU.not_equal, 1.0, -(TS - 1), 1)
    fill(K["same"][:, :], [[TS, B]], ALU.is_gt, 1.0, 0, -1).then_inc(C.cleared, 1)
    pool.wait_ge(C.cleared, 2)
    fill(blocks(K["mask_s"][:, :]), [[TS, B], [0, TS]], ALU.is_ge, NEG, TS - 1, -1)
    fill(blocks(K["tri_s"][:, :]), [[-TS, B], [0, TS]], ALU.is_ge, 0.0, 0, 1)
    fill(K["same"][:, :], [[TS, B]], ALU.is_ge, 0.0, TS - 1, -1)
    g.tensor_copy(C.sdist[:, :], C.sdist_i[:, :])
    g.tensor_copy(C.tpat[:, :], C.tpat_i[:, :]).then_inc(C.sdist_ready, 1)
    g.tensor_copy(C.dist[:, :], C.dist_i[:, :]).then_inc(C.dist_ready, 1)
    pool.wait_ge(C.dist_ready, 1)
    for h in range(AH):
        g.tensor_scalar(K["bias"][:, h, :], C.dist[:, :], -SLOPES[h], None, ALU.mult).then_inc(C.bias_ready, 1)
    pool.wait_ge(C.bias_ready, AH)
    fill(K["bias"][:, :, :], [[0, AH], [1, 2 * P]], ALU.is_ge, NEG, 0, -1).then_inc(C.bias_ready, 1)
    pool.wait_ge(C.bias_ready, AH + 1)
    fill(K["bias"][:, :, :], [[0, AH], [-1, 2 * P]], ALU.is_ge, NEG, P, 1).then_inc(C.bias_ready, 1)
    pool.wait_ge(C.bias_ready, AH + 2)
    g.tensor_copy(K["live_bias"][:, :, P:2 * P], K["bias"][:, :, P:2 * P])


def modulation_rows(nc, I, mod, w_in, w_in_in, K):
    NCH = 6 * D // 512
    RING = 3
    with ExitStack() as ctx:
        def sb(name, shape, dt=F32):
            return ctx.enter_context(nc.sbuf_tensor(name, shape, dt))

        def sem(name):
            return ctx.enter_context(nc.semaphore(name))

        c_rows = sb("c_rows", [NC, D])
        c_sig = sb("c_sig", [NC, D])
        cT = sb("cT", [P, KC, NC])
        w = sb("ada_ring", [P, RING, KC, 512])
        bias = sb("ada_bias", [NC, RING, 512])
        row = sb("ada_row", [NC, RING, 512])
        ps_t = ctx.enter_context(nc.psum_tensor("ada_ps_t", [P, KC, NC], F32))
        ps = [ctx.enter_context(nc.psum_tensor(f"ada_ps{i}", [NC, 512], F32)) for i in range(RING)]
        c_in, c_silu, c_sgm, ct_ps, ct_ready = sem("c_in"), sem("c_silu"), sem("c_sgm"), sem("ct_ps"), sem("ct_ready")
        ring_in = [sem(f"ada_w_in{i}") for i in range(RING)]
        row_ps, row_ready = sem("ada_row_ps"), sem("ada_row_ready")
        row_out = [sem(f"ada_row_out{i}") for i in range(RING)]
        ada = I["ada_w"][0].rearrange("(kc p) n -> p kc n", p=P)
        w_in_dram = I["w_in"][0].rearrange("(kc p) n -> p kc n", p=P)
        C = ConstantBuffers(nc, ctx)
        block = ctx.enter_context(nc.Block())

        @block.sync
        def _(sp):
            sp.dma_start(c_rows[0:1, :], I["c_prompt"]).then_inc(c_in, 16)
            sp.dma_start(c_rows[1:NC, :], I["c_sample"]).then_inc(c_in, 16)

            def load(c, i, first=False):
                if not first:
                    hold(sp, row_ready, c - RING + 1)
                cols = bass.ds(c * 512, 512)
                sp.dma_start(w[:, i, :, :], ada[:, :, cols]).then_inc(ring_in[i], 16)
                sp.dma_start(bias[:, i, :], I["ada_b"][0, cols].partition_broadcast(NC)).then_inc(ring_in[i], 16)

            per = KC // (NCH // RING)
            for i in range(RING):
                load(i, i, first=True)
            sp.dma_start(w_in[:, 0:per, :], w_in_dram[:, 0:per, :]).then_inc(w_in_in, 16)
            with sp.Fori(1, NCH // RING) as r:
                for i in range(RING):
                    load(r * RING + i, i)
                blocks = bass.ds(r * per, per)
                sp.dma_start(w_in[:, blocks, :], w_in_dram[:, blocks, :]).then_inc(w_in_in, 16)

        @block.gpsimd
        def _(pool):
            constants_pool(nc, pool, K, C)

        @block.scalar
        def _(act):
            act.wait_ge(c_in, 32)
            nc.scalar.activation(c_sig[:, :], c_rows[:, :], ACT.Sigmoid).then_inc(c_sgm, 1)
            def store(c, i):
                hold(act, row_ready, c + 1)
                act.dma_start(mod[:, bass.ds(c * 512, 512)], row[:, i, :]).then_inc(row_out[i], 16)

            with act.Fori(0, NCH // RING) as r:
                for i in range(RING):
                    store(r * RING + i, i)
            for i in range(RING):
                act.wait_ge(row_out[i], 16 * (NCH // RING))

        @block.vector
        def _(dve):
            dve.wait_ge(c_sgm, 1)
            nc.vector.tensor_tensor(c_rows[:, :], c_rows[:, :], c_sig[:, :], ALU.mult).then_inc(c_silu, 1)
            dve.wait_ge(ct_ps, 1)
            nc.vector.tensor_copy(cT[:, :, :], ps_t[:, :, :]).then_inc(ct_ready, 1)
            constants_dve(nc, dve, K, C)

            def add_bias(c, r, i, first=False):
                hold(dve, ring_in[i], r * 32 + 32)
                if not first:
                    hold(dve, row_out[i], r * 16)
                hold(dve, row_ps, c + 1)
                nc.vector.tensor_tensor(row[:, i, :], ps[i][:, :], bias[:, i, :], ALU.add).then_inc(row_ready, 1)

            for i in range(RING):
                add_bias(i, 0, i, first=True)
            with dve.Fori(1, NCH // RING) as r:
                for i in range(RING):
                    add_bias(r * RING + i, r, i)

        @block.tensor
        def _(pe):
            pe.wait_ge(c_silu, 1)
            pe.wait_ge(C.ident_ready, 2)
            for kc in range(KC):
                last = nc.tensor.transpose(ps_t[:, kc, :], c_rows[:, kc * P:(kc + 1) * P], K["ident"][0:NC, 0:NC])
            last.then_inc(ct_ps, 1)
            pe.wait_ge(ct_ready, 1)

            def product(c, r, i, first=False):
                hold(pe, ring_in[i], r * 32 + 32)
                if not first:
                    hold(pe, row_ready, c - RING + 1)
                for kc in range(KC):
                    mm = nc.tensor.matmul(ps[i][:, :], cT[:, kc, :], w[:, i, kc, :], start=(kc == 0), stop=(kc == KC - 1))
                mm.then_inc(row_ps, 1)

            for i in range(RING):
                product(i, 0, i, first=True)
            with pe.Fori(1, NCH // RING) as r:
                for i in range(RING):
                    product(r * RING + i, r, i)


class Mixer:

    def __init__(self, nc, ctx, w_in):
        def sb(name, shape, dt=F32):
            return ctx.enter_context(nc.sbuf_tensor(name, shape, dt))

        def ps(name, shape):
            return ctx.enter_context(nc.psum_tensor(name, shape, F32))

        self.w_in = w_in
        self.w_out = sb("w_out", [P, KC, D])
        self.row_a, self.row_s, self.row_g = sb("mod_scale", [P, D]), sb("mod_shift", [P, D]), sb("mod_gate", [P, D])
        self.xt = sb("xt", [P, D])
        self.h = sb("h", [P, D])
        self.hT = sb("hT", [P, KC, P])
        self.g5 = sb("z_gates_sq_sk", [P, 392])
        self.qz, self.kz = sb("z_q", [P, MW]), sb("z_k", [P, MW])
        self.vz = sb("z_v", [P, MH, DH])
        self.g6, self.g7 = sb("z_sv_cb", [P, 384]), sb("z_cc_ch", [P, 512])
        self.oz = sb("z_o", [P, MW])
        self.stat = sb("mix_stat", [P, 4])
        self.eps = sb("eps", [P, 1])
        self.gb, self.mg, self.sink = sb("gate_b", [P, 2 * MH]), sb("mlstm_g", [P, MW]), sb("sinks", [P, AH])
        self.pre, self.absf = sb("gate_pre", [P, 8]), sb("gate_abs", [P, MH])
        self.lg, self.lf = sb("gate_log", [P, MH]), sb("gate_lf", [P, MH])
        self.mb = sb("mm_b", [P, 8])
        self.w, self.rowmax = sb("gate_w", [P, MH]), sb("d_max", [P, MH])
        self.mprev, self.nmm, self.mt = sb("m_prev", [P, MH]), sb("neg_mm", [P, MH]), sb("m_t", [P, MH])
        self.earg, self.eval = sb("exp_arg", [P, 8]), sb("exp_val", [P, 8])
        self.dm = sb("d_matrix", [P, MH, P])
        self.diag = sb("diag_w", [P, MH, P])
        self.qk = sb("qT_kT", [P, 2, MH, P])
        self.qT, self.kT = self.qk[:, 0], self.qk[:, 1]
        self.mixT = self.qk[:, :, :, :].rearrange("p a h t -> p (a h) t")
        self.pT = sb("pT", [P, MH, P])
        self.den, self.rden = sb("den", [P, 8]), sb("rden", [P, MH])
        self.ss2, self.r2 = sb("ss2", [P, MH]), sb("r2", [P, MH])
        self.lastv, self.larg, self.lval = sb("last_mm_b", [P, 8]), sb("last_arg", [P, 8]), sb("last_val", [P, 8])
        self.CT, self.nT = sb("CT", [P, MH, DH]), sb("nT", [P, MH])
        self.sqT, self.skT = sb("sqT", [P, 2, P]), sb("skT", [P, 2 * P])
        self.sv_prev = sb("sv_prev", [P, KVH * AD])
        self.sc = sb("swa_scores", [P, AH, 2 * P])
        self.nsq = self.dm
        self.xr = self.sc[:, :, :].rearrange("p h k -> p (h k)")
        self.smx, self.ssum, self.ses = sb("swa_max", [P, 2 * AH]), sb("swa_sum", [P, AH]), sb("swa_sink", [P, AH])
        self.ps_t, self.ps_m = ps("ps_t", [P, 4, P]), ps("ps_m", [P, 512])
        self.ps_z = [ps("ps_z0", [P, 512]), ps("ps_z1", [P, 512])]
        self.ps_s = ps("ps_s", [P, 2, 512])
        self.ps_n = [ps("ps_n0", [P, 512]), ps("ps_n1", [P, 512])]
        self.u = self.g7[:, 0:CW]
        self.uT = sb("conv_uT", [P, 2, P + CK - 1])
        self.cbT = self.pT[:, 2:4]
        self.cw = sb("conv_taps", [P, CK, 2])


TB = 11
T_H0, T_H1, T_SWA, T_Q, T_K, T_P, T_A0, T_A1, T_CONV, T_HM, T_OA = range(TB)
SIGNALS = ("w_out_in small_in rows_in rows_ready init x_in xr_in ss_ready h_ready t_full t_free zfull0 zfull1 zfree0 zfree1 "
           "gate_abs_ready lg_ready lf_ready b_full diag_ready wb_full d_ready expw_ready "
           "s_full p_ready num_full inter_ready numf_ready ss2_ready hm_ready larg_ready lval_ready vw_ready "
           "upd_full state_ready swa_full sc_ready swa_exp pv_full oa_ready u_ready yc_ready og_ready "
           "o_full x1_ready x1_stored pool_done act_step dve_step").split()


class Tile:

    def __init__(self, nc, X, s, t, rows, tri, mask, last):
        self.nc, self.X, self.s, self.t, self.n = nc, X, s, t, rows
        self.tri, self.mask, self.last = tri, mask, last

    def on(self, eng, name, per=1, k=None):
        hold(eng, self.s[name], self.t * per + (per if k is None else k))

    def z_landed(self, eng, i):
        self.on(eng, f"zfull{i % 2}", 4 - i % 2, i // 2 + 1)

    def z_out(self, eng, i):
        self.on(eng, f"zfree{i % 2}", 4 - i % 2, i // 2 + 1)

    def t_landed(self, eng, k):
        self.on(eng, "t_full", self.per_t, k + 1)

    def t_out(self, eng, k):
        self.on(eng, "t_free", self.per_t, k + 1)

    def batch(self, pe, k, blocks, ident):
        if k:
            self.t_out(pe, k - 1)
        for j, (src, rows, cols) in enumerate(blocks):
            last = self.nc.tensor.transpose(self.X.ps_t[0:cols, j, 0:rows], src, ident[0:rows, 0:rows])
        last.then_inc(self.s["t_full"], 1)

    def chunk(self, pe, i):
        a, b = CHUNKS[i]
        X, n = self.X, self.n
        if i >= 2:
            self.z_out(pe, i - 2)
        for kc in range(KC):
            mm = self.nc.tensor.matmul(X.ps_z[i % 2][0:n, 0:b - a], X.hT[:, kc, 0:n], X.w_in[:, kc, a:b],
                                       start=(kc == 0), stop=(kc == KC - 1))
        mm.then_inc(self.s[f"zfull{i % 2}"], 1)

    def transpose_rows(self, pe, K):
        X, n, e = self.X, self.n, K["ident"]
        self.on(pe, "h_ready")
        self.batch(pe, T_H0, [(X.h[0:n, j * P:(j + 1) * P], n, P) for j in range(4)], e)
        self.batch(pe, T_H1, [(X.h[0:n, j * P:(j + 1) * P], n, P) for j in range(4, 8)], e)

    def project(self, pe, K):
        nc, X, s, n, e = self.nc, self.X, self.s, self.n, K["ident"]
        self.t_out(pe, T_H1)
        self.chunk(pe, GATES)
        self.chunk(pe, QZ)
        self.z_out(pe, GATES)
        self.batch(pe, T_SWA, [(X.g5[0:n, 8 + j * P:8 + (j + 1) * P], n, P) for j in range(3)], e)
        self.chunk(pe, KZ)
        self.on(pe, "lf_ready")
        nc.tensor.matmul(X.ps_m[0:n, 0:4], self.tri, X.lf[0:n, :], start=True, stop=True).then_inc(s["b_full"], 1)
        self.chunk(pe, VZ)
        self.z_out(pe, QZ)
        self.batch(pe, T_Q, [(X.qz[0:n, h * DH:(h + 1) * DH], n, DH) for h in range(MH)], e)
        self.on(pe, "diag_ready")
        for h in range(MH):
            mm = nc.tensor.matmul(X.ps_s[0:n, 1, h * P:h * P + n], K["ones"][0:n, 0:n], X.diag[0:n, h, 0:n],
                                  start=True, stop=True)
        mm.then_inc(s["wb_full"], 1)
        self.chunk(pe, SVCB)
        self.z_out(pe, KZ)
        self.batch(pe, T_K, [(X.kz[0:n, h * DH:(h + 1) * DH], n, DH) for h in range(MH)], e)
        self.chunk(pe, CCCH)
        self.t_out(pe, T_K)
        for h in range(MH):
            mm = nc.tensor.matmul(X.ps_s[0:n, 0, h * P:h * P + n], X.qT[:, h, 0:n], X.kT[:, h, 0:n],
                                  start=True, stop=True)
        mm.then_inc(s["s_full"], 1)

    def transpose_weights(self, pe, K):
        X, n = self.X, self.n
        self.on(pe, "p_ready")
        self.batch(pe, T_P, [(X.dm[0:n, h, 0:n], n, n) for h in range(MH)], K["ident"])
        self.chunk(pe, OZ)

    def intra(self, pe, K):
        nc, X, s, n = self.nc, self.X, self.s, self.n
        self.t_out(pe, T_P)
        self.z_out(pe, VZ)
        nc.tensor.matmul(X.ps_m[0:n, 16:24], self.last, X.mb[0:n, :], start=True, stop=True)
        for h in range(MH):
            nc.tensor.matmul(X.ps_n[0][0:n, h * DH:(h + 1) * DH], X.pT[0:n, h, 0:n], X.vz[0:n, h, :],
                             start=True, stop=True)
            mm = nc.tensor.matmul(X.ps_m[0:n, 12 + h:13 + h], X.pT[0:n, h, 0:n], K["ones"][0:n, 0:1],
                                  start=True, stop=True)
        mm.then_inc(s["num_full"], 1)

    def out_product(self, pe):
        nc, X, s, n = self.nc, self.X, self.s, self.n
        pe.wait_ge(s["w_out_in"], 16)
        self.z_out(pe, CCCH)
        self.z_out(pe, OZ)
        self.on(pe, "yc_ready")
        for c in range(2):
            for kc in range(KC):
                mm = nc.tensor.matmul(X.ps_z[c][0:n, :], X.mixT[:, kc, 0:n], X.w_out[:, kc, c * 512:(c + 1) * 512],
                                      start=(kc == 0), stop=(kc == KC - 1))
        mm.then_inc(s["o_full"], 1)

    def act_rms(self, act, chain):
        nc, X, s, n = self.nc, self.X, self.s, self.n
        a = nc.scalar.activation
        self.on(act, "x_in", 16)
        chain(a(X.h[0:n, :], X.xt[0:n, :], ACT.Square, accum_out=X.stat[0:n, 0:1]))
        a(X.stat[0:n, 1:2], X.stat[0:n, 0:1], ACT.Sqrt, scale=1.0 / D, bias=X.eps[0:n, :]).then_inc(s["ss_ready"], 1)

    def act_front(self, act, chain):
        nc, X, s, n = self.nc, self.X, self.s, self.n
        a = nc.scalar.activation
        self.t_landed(act, T_H0)
        a(X.hT[:, 0:4, 0:n], X.ps_t[:, :, 0:n], ACT.Copy).then_inc(s["t_free"], 1)
        self.z_landed(act, QZ)
        a(X.qz[0:n, :], X.ps_z[QZ % 2][0:n, :], ACT.Copy).then_inc(s[f"zfree{QZ % 2}"], 1)
        self.on(act, "gate_abs_ready")
        chain(a(X.lg[0:n, :], X.absf[0:n, :], ACT.Exp, scale=-1.0))
        a(X.lg[0:n, :], X.lg[0:n, :], ACT.Ln, bias=1.0).then_inc(s["lg_ready"], 1)
        self.z_landed(act, KZ)
        a(X.kz[0:n, :], X.ps_z[KZ % 2][0:n, :], ACT.Copy, scale=KSCALE).then_inc(s[f"zfree{KZ % 2}"], 1)
        self.t_landed(act, T_Q)
        a(X.qT[:, :, 0:n], X.ps_t[:, :, 0:n], ACT.Copy).then_inc(s["t_free"], 1)
        self.on(act, "d_ready")
        for h in range(MH):
            a(X.dm[0:n, h, 0:n], X.dm[0:n, h, 0:n], ACT.Exp, bias=X.nmm[0:n, h:h + 1])
        a(X.eval[0:n, :], X.earg[0:n, :], ACT.Exp).then_inc(s["expw_ready"], 1)
        self.z_landed(act, SVCB)
        a(X.g6[0:n, :], X.ps_z[SVCB % 2][0:n, 0:384], ACT.Copy).then_inc(s[f"zfree{SVCB % 2}"], 1)
        self.t_landed(act, T_P)
        a(X.pT[0:n, :, 0:n], X.ps_t[0:n, :, 0:n], ACT.Copy).then_inc(s["t_free"], 1)

    def act_norm(self, act, chain, inter, landed, out):
        nc, X, s, n = self.nc, self.X, self.s, self.n
        a = nc.scalar.activation
        landed(act)
        for h in range(MH):
            last = a(X.h[0:n, h * DH:(h + 1) * DH], inter[:, h, :], ACT.Copy, scale=X.eval[0:n, h:h + 1])
        last.then_inc(s[out], 1)
        self.on(act, "larg_ready")
        a(X.lval[0:n, :], X.larg[0:n, :], ACT.Exp).then_inc(s["lval_ready"], 1)
        self.z_landed(act, OZ)
        a(X.oz[0:n, :], X.ps_z[OZ % 2][0:n, :], ACT.Sigmoid).then_inc(s[f"zfree{OZ % 2}"], 1)
        self.on(act, "numf_ready")
        for h in range(MH):
            last = a(X.nsq[0:n, h, :], X.h[0:n, h * DH:(h + 1) * DH], ACT.Square, scale=X.rden[0:n, h:h + 1],
                     accum_out=X.ss2[0:n, h:h + 1])
        chain(last)
        a(X.r2[0:n, :], X.ss2[0:n, :], ACT.Sqrt, scale=1.0 / DH, bias=X.eps[0:n, :]).then_inc(s["ss2_ready"], 1)

    def dve_rms(self, dve, chain):
        nc, X, s, n = self.nc, self.X, self.s, self.n
        v = nc.vector
        self.on(dve, "ss_ready")
        chain(v.reciprocal(X.stat[0:n, 2:3], X.stat[0:n, 1:2]))
        chain(v.scalar_tensor_tensor(X.h[0:n, :], X.xt[0:n, :], X.stat[0:n, 2:3], X.row_a[0:n, :], ALU.mult, ALU.mult))
        v.tensor_tensor(X.h[0:n, :], X.h[0:n, :], X.row_s[0:n, :], ALU.add).then_inc(s["h_ready"], 1)

    def dve_front(self, dve, chain, K):
        nc, X, s, n = self.nc, self.X, self.s, self.n
        v = nc.vector
        self.t_landed(dve, T_H1)
        v.tensor_copy(X.hT[:, 4:8, 0:n], X.ps_t[:, :, 0:n]).then_inc(s["t_free"], 1)
        self.z_landed(dve, GATES)
        zg = X.ps_z[GATES % 2][0:n, :]
        v.tensor_copy(X.g5[0:n, 0:8], zg[:, 0:8])
        v.tensor_copy(X.g5[0:n, 264:392], zg[:, 264:392])
        v.tensor_copy(X.g5[0:n, 8:264].rearrange("p (g kv d) -> p g kv d", g=2, kv=KVH),
                      zg[:, 8:264].rearrange("p (kv g d) -> p g kv d", kv=KVH, g=2)).then_inc(s[f"zfree{GATES % 2}"], 1)
        self.z_out(dve, GATES)
        chain(v.tensor_tensor(X.pre[0:n, :], X.g5[0:n, 0:8], X.gb[0:n, :], ALU.add))
        v.scalar_tensor_tensor(X.absf[0:n, :], X.pre[0:n, 4:8], -1.0, X.pre[0:n, 4:8], ALU.mult, ALU.max).then_inc(s["gate_abs_ready"], 1)
        self.t_landed(dve, T_SWA)
        v.tensor_copy(X.sqT[:, :, 0:n], X.ps_t[:, 0:2, 0:n])
        v.tensor_copy(X.skT[:, P:P + n], X.ps_t[:, 2, 0:n]).then_inc(s["t_free"], 1)
        self.on(dve, "lg_ready")
        v.scalar_tensor_tensor(X.lf[0:n, :], X.pre[0:n, 4:8], 0.0, X.lg[0:n, :], ALU.min, ALU.subtract)\
            .then_inc(s["lf_ready"], 1)
        self.z_landed(dve, VZ)
        v.tensor_copy(X.vz[0:n, :, :], X.ps_z[VZ % 2][0:n, :].rearrange("p (h d) -> p h d", h=MH))\
            .then_inc(s[f"zfree{VZ % 2}"], 1)
        self.on(dve, "b_full")
        v.tensor_copy(X.mb[0:n, 4:8], X.ps_m[0:n, 0:4])
        chain(v.tensor_tensor(X.w[0:n, :], X.pre[0:n, 0:4], X.ps_m[0:n, 0:4], ALU.subtract))
        v.tensor_tensor(X.diag[0:n, :, 0:n], repeat_mid(K["ident"][0:n, 0:n], MH), repeat_last(X.w[0:n, :], n), ALU.mult)\
            .then_inc(s["diag_ready"], 1)
        self.t_landed(dve, T_K)
        v.tensor_copy(X.kT[:, :, 0:n], X.ps_t[:, :, 0:n]).then_inc(s["t_free"], 1)
        self.on(dve, "wb_full")
        wb = X.ps_s[0:n, 1, :].rearrange("p (h s) -> p h s", h=MH)[:, :, 0:n]
        chain(v.tensor_tensor(X.dm[0:n, :, 0:n], wb, repeat_mid(self.mask, MH), ALU.add))
        chain(v.tensor_reduce(X.rowmax[0:n, :], X.dm[0:n, :, 0:n], AX, ALU.max))
        chain(v.tensor_tensor(X.mb[0:n, 0:4], X.rowmax[0:n, :], X.mprev[0:n, :], ALU.max))
        v.tensor_scalar(X.nmm[0:n, :], X.mb[0:n, 0:4], -1.0, None, ALU.mult)
        v.tensor_tensor(X.earg[0:n, 0:4], X.mprev[0:n, :], X.mb[0:n, 0:4], ALU.subtract)
        chain(v.tensor_tensor(X.mt[0:n, :], X.mb[0:n, 0:4], X.mb[0:n, 4:8], ALU.add))
        v.tensor_scalar(X.earg[0:n, 4:8], X.mt[0:n, :], -1.0, None, ALU.mult).then_inc(s["d_ready"], 1)
        self.z_landed(dve, CCCH)
        v.tensor_copy(X.g7[0:n, :], X.ps_z[CCCH % 2][0:n, :]).then_inc(s[f"zfree{CCCH % 2}"], 1)
        self.on(dve, "expw_ready")
        self.on(dve, "s_full")
        raw = X.ps_s[0:n, 0, :].rearrange("p (h s) -> p h s", h=MH)[:, :, 0:n]
        v.tensor_tensor(X.dm[0:n, :, 0:n], raw, X.dm[0:n, :, 0:n], ALU.mult).then_inc(s["p_ready"], 1)

    def dve_num(self, dve, chain, inter_den, inter_out):
        nc, X, s, n = self.nc, self.X, self.s, self.n
        v = nc.vector
        self.on(dve, "num_full")
        chain(v.tensor_tensor(X.den[0:n, 0:4], X.eval[0:n, 0:4], inter_den, ALU.mult))
        chain(v.tensor_tensor(X.den[0:n, 0:4], X.den[0:n, 0:4], X.ps_m[0:n, 12:16], ALU.add))
        chain(v.scalar_tensor_tensor(X.den[0:n, 4:8], X.den[0:n, 0:4], -1.0, X.den[0:n, 0:4], ALU.mult, ALU.max))
        chain(v.tensor_tensor(X.den[0:n, 4:8], X.den[0:n, 4:8], X.eval[0:n, 4:8], ALU.max))
        v.reciprocal(X.rden[0:n, :], X.den[0:n, 4:8])
        inter_out(dve)
        v.tensor_tensor(X.h[0:n, 0:MW], X.h[0:n, 0:MW], X.ps_n[0][0:n, :], ALU.add).then_inc(s["numf_ready"], 1)

    def dve_last(self, dve, chain):
        nc, X, s, n = self.nc, self.X, self.s, self.n
        v = nc.vector
        chain(v.tensor_copy(X.lastv[0:n, :], X.ps_m[0:n, 16:24]))
        v.tensor_tensor(X.larg[0:n, 0:4], X.w[0:n, :], X.lastv[0:n, 0:4], ALU.subtract)
        v.tensor_tensor(X.larg[0:n, 4:8], X.mprev[0:n, :], X.lastv[0:n, 0:4], ALU.subtract).then_inc(s["larg_ready"], 1)
        self.on(dve, "lval_ready")
        v.tensor_tensor(X.mprev[0:n, :], X.lastv[0:n, 0:4], X.lastv[0:n, 4:8], ALU.add)
        v.tensor_tensor(X.diag[0:n, :, :], X.vz[0:n, :, :], repeat_last(X.lval[0:n, 0:4], DH), ALU.mult)\
            .then_inc(s["vw_ready"], 1)

    def dve_norm(self, dve, chain):
        nc, X, s, n = self.nc, self.X, self.s, self.n
        v = nc.vector
        self.on(dve, "ss2_ready")
        chain(v.reciprocal(X.r2[0:n, :], X.r2[0:n, :]))
        chain(v.tensor_tensor(X.r2[0:n, :], X.r2[0:n, :], X.rden[0:n, :], ALU.mult))
        hm = X.h[0:n, 0:MW].rearrange("p (h d) -> p h d", h=MH)
        chain(v.tensor_tensor(hm, hm, repeat_last(X.r2[0:n, :], DH), ALU.mult))
        self.on(dve, "og_ready")
        v.tensor_tensor(X.h[0:n, 0:MW], X.h[0:n, 0:MW], X.oz[0:n, :], ALU.mult).then_inc(s["hm_ready"], 1)

    def dve_residual(self, dve, chain):
        nc, X, s, n = self.nc, self.X, self.s, self.n
        v = nc.vector
        self.on(dve, "o_full")
        v.tensor_tensor(X.qz[0:n, :], X.ps_z[0][0:n, :], X.row_g[0:n, 0:512], ALU.mult)
        chain(v.tensor_tensor(X.kz[0:n, :], X.ps_z[1][0:n, :], X.row_g[0:n, 512:D], ALU.mult))
        self.on(dve, "xr_in", 16)
        v.tensor_tensor(X.xr[0:n, 0:512], X.xr[0:n, 0:512], X.qz[0:n, :], ALU.add)
        v.tensor_tensor(X.xr[0:n, 512:D], X.xr[0:n, 512:D], X.kz[0:n, :], ALU.add).then_inc(s["x1_ready"], 1)

    def pool_gates(self, pool):
        nc, X, s, n = self.nc, self.X, self.s, self.n
        self.z_out(pool, CCCH)
        nc.gpsimd.tensor_tensor(X.u[0:n, :], X.g7[0:n, 0:CW], X.g7[0:n, CW:2 * CW], ALU.mult).then_inc(s["u_ready"], 1)
        self.z_out(pool, OZ)
        nc.gpsimd.tensor_tensor(X.oz[0:n, :], X.oz[0:n, :], X.mg[0:n, :], ALU.mult).then_inc(s["og_ready"], 1)


def load_mod_rows(sp, nc, I, mod, X, s, sample, extra=()):
    gain = I["norm_mix_g"][0]
    n = NS if sample else P
    for dst, k in ((X.row_a, 1), (X.row_s, 0), (X.row_g, 2)):
        if sample:
            for b in range(B):
                sp.dma_start(dst[b * TS:(b + 1) * TS, :], mod[1 + b, k * D:(k + 1) * D].partition_broadcast(TS)).then_inc(s["rows_in"], 16)
        else:
            sp.dma_start(dst[:, :], mod[0, k * D:(k + 1) * D].partition_broadcast(P)).then_inc(s["rows_in"], 16)
    sp.dma_start(X.h[0:n, :], gain.partition_broadcast(n)).then_inc(s["rows_in"], 16)
    return 16 * ((3 * B if sample else 3) + 1)


def dve_mod_rows(dve, nc, X, s, sample):
    n = NS if sample else P
    dve.wait_ge(s["rows_in"], 16 * ((3 * B if sample else 3) + 1))
    nc.vector.scalar_tensor_tensor(X.row_a[0:n, :], X.row_a[0:n, :], 1.0, X.h[0:n, :], ALU.add, ALU.mult)\
        .then_inc(s["rows_ready"], 1)
    dve.wait_ge(s["rows_ready"], 1)


def mix_prompt(nc, I, O, mod, x1_dram, X, K, s):

    def tile(t):
        T = Tile(nc, X, s, t, P, K["tri"][:, :], K["mask"][:, :], K["last"][:, :])
        T.per_t = TB
        return T

    with nc.Block() as block:
        @block.sync
        def _(sp):
            sp.dma_start(X.gb[:, :], I["mlstm_gate_b"][0].partition_broadcast(P)).then_inc(s["small_in"], 16)
            sp.dma_start(X.mg[:, :], I["mlstm_norm_g"][0].partition_broadcast(P)).then_inc(s["small_in"], 16)
            sp.dma_start(X.sink[:, :], I["swa_sinks"][0].partition_broadcast(P)).then_inc(s["small_in"], 16)
            for j in range(CK):
                sp.dma_start(X.cw[:, j, :], I["conv_w"][0, j].rearrange("(a p) -> p a", p=P),
                             allow_slow_non_contiguous=True).then_inc(s["small_in"], 16)
            load_mod_rows(sp, nc, I, mod, X, s, False)
            sp.dma_start(X.xt[:, :], I["x_prompt"][0, 0:P, :]).then_inc(s["x_in"], 16)
            sp.dma_start(X.w_out[:, :, :], I["w_out"][0].rearrange("(kc p) n -> p kc n", p=P)).then_inc(s["w_out_in"], 16)

            def residual(t):
                T = tile(t)
                T.t_landed(sp, T_A1)
                T.on(sp, "ss2_ready")
                sp.dma_start(X.xr[:, :], I["x_prompt"][0, bass.ds(t * P, P), :]).then_inc(s["xr_in"], 16)
                T.on(sp, "x1_ready")
                sp.dma_start(x1_dram[bass.ds(t * P, P), :], X.xr[:, :]).then_inc(s["x1_stored"], 16)

            with sp.Fori(0, NT - 1) as t:
                hold(sp, s["h_ready"], t + 1)
                sp.dma_start(X.xt[:, :], I["x_prompt"][0, bass.ds(t * P + P, P), :]).then_inc(s["x_in"], 16)
                residual(t)
            residual(NT - 1)
            out = []
            sp.dma_start(O["swa_k_p"].rearrange("l b w h d -> (l b w) (h d)"), X.g5[:, 264:392]).then_inc(s["x1_stored"], 16)
            sp.dma_start(O["swa_v_p"].rearrange("l b w h d -> (l b w) (h d)"), X.g6[:, 0:128]).then_inc(s["x1_stored"], 16)
            sp.dma_start(O["conv_p"].rearrange("l b w c -> (l b w) c"), X.u[P - 2:P, :]).then_inc(s["x1_stored"], 16)
            sp.dma_start(O["m_p"].rearrange("l b h -> (l b) h"), X.mprev[0:1, :]).then_inc(s["x1_stored"], 16)
            for h in range(MH):
                sp.dma_start(O["n_p"][0, 0, h].rearrange("(k o) -> k o", o=1), X.nT[:, h:h + 1],
                             allow_slow_non_contiguous=True).then_inc(s["x1_stored"], 16)
            sp.wait_ge(s["t_free"], NT * TB + 1)
            sp.dma_start(O["C_p"].rearrange("l b h v k -> v (l b h) k"), X.pT[:, :, :]).then_inc(s["x1_stored"], 16)
            sp.wait_ge(s["x1_stored"], 16 * (1 + NT + 5 + MH))

        @block.gpsimd
        def _(pool):
            g = nc.gpsimd
            for m in (X.CT, X.nT, X.mprev, X.skT, X.sv_prev):
                g.memset(m[:], 0.0)
            g.memset(X.eps[:, :], EPS)
            g.memset(X.uT[:, :, 0:CK - 1], 0.0).then_inc(s["init"], 1)
            g.memset(X.ses[:, :], 0.0).then_inc(s["x1_stored"], 16)
            with pool.Fori(0, NT) as t:
                T = tile(t)
                T.pool_gates(pool)
                T.on(pool, "swa_full")
                g.tensor_copy(X.skT[:, 0:P], X.skT[:, P:2 * P])
                T.on(pool, "sc_ready")
                g.tensor_copy(K["live_bias"][:, :, 0:P], K["bias"][:, :, 0:P])
                T.on(pool, "pv_full")
                g.tensor_copy(X.sv_prev[:, :], X.g6[:, 0:P]).then_inc(s["pool_done"], 1)

        @block.scalar
        def _(act):
            chain = Chain(act, s["act_step"])
            a = nc.scalar.activation
            act.wait_ge(s["init"], 1)
            act.wait_ge(s["rows_ready"], 1)

            def body(t, more=True):
                T = tile(t)
                T.act_front(act, chain)
                T.on(act, "sc_ready")
                for h in range(AH):
                    a(X.sc[:, h, :], X.sc[:, h, :], ACT.Exp, bias=X.smx[:, AH + h:AH + h + 1],
                      accum_out=X.ssum[:, h:h + 1])
                a(X.ses[:, :], X.ses[:, :], ACT.Exp).then_inc(s["swa_exp"], 1)
                T.t_landed(act, T_A0)
                a(X.hT[:, 0:4, :], X.ps_t[:, :, :], ACT.Copy).then_inc(s["t_free"], 1)
                T.act_norm(act, chain, X.ps_n[1][:, :].rearrange("p (h d) -> p h d", h=MH),
                           lambda eng: T.on(eng, "num_full"), "inter_ready")
                T.t_landed(act, T_CONV)
                a(X.uT[:, :, CK - 1:], X.ps_t[:, 0:2, :], ACT.Copy)
                a(X.cbT[:, :, :], X.ps_t[:, 2:4, :], ACT.Copy).then_inc(s["t_free"], 1)
                T.t_landed(act, T_OA)
                a(X.mixT[:, 4:6, :], X.ps_t[:, 0:2, :], ACT.Copy).then_inc(s["t_free"], 1)
                if more:
                    tile(t + 1).act_rms(act, chain)

            tile(0).act_rms(act, chain)
            with act.Fori(0, NT - 1) as t:
                chain.enter(t, 3)
                body(t)
            chain.leave(NT - 1)
            body(NT - 1, more=False)
            act.wait_ge(s["t_full"], NT * TB + 1)
            a(X.pT[:, :, :], X.ps_t[:, :, :], ACT.Copy).then_inc(s["t_free"], 1)

        @block.vector
        def _(dve):
            chain = Chain(dve, s["dve_step"])
            v = nc.vector
            dve_mod_rows(dve, nc, X, s, False)

            def body(t, more=True):
                T = tile(t)
                T.dve_front(dve, chain, K)
                T.on(dve, "swa_full")
                T.on(dve, "x1_stored", 16)
                chain(v.scalar_tensor_tensor(X.sc[:, :, :], X.ps_s[:, :, :].rearrange("p a (h k) -> p (a h) k", h=2),
                                             AD ** -0.5, K["live_bias"][:, :, :], ALU.mult, ALU.add))
                chain(v.tensor_reduce(X.smx[:, 0:AH], X.sc[:, :, :], AX, ALU.max))
                chain(v.tensor_tensor(X.smx[:, 0:AH], X.smx[:, 0:AH], X.sink[:, :], ALU.max))
                chain(v.tensor_tensor(X.ses[:, :], X.sink[:, :], X.smx[:, 0:AH], ALU.subtract))
                v.tensor_scalar(X.smx[:, AH:2 * AH], X.smx[:, 0:AH], -1.0, None, ALU.mult).then_inc(s["sc_ready"], 1)
                T.on(dve, "swa_exp")
                chain(v.tensor_tensor(X.ssum[:, :], X.ssum[:, :], X.ses[:, :], ALU.add))
                chain(v.reciprocal(X.ssum[:, :], X.ssum[:, :]))
                T.dve_num(dve, chain, X.ps_m[:, 8:12], lambda eng: T.on(eng, "inter_ready"))
                T.t_landed(dve, T_A1)
                v.tensor_copy(X.hT[:, 4:8, :], X.ps_t[:, :, :]).then_inc(s["t_free"], 1)
                T.dve_last(dve, chain)
                T.dve_norm(dve, chain)
                T.on(dve, "pv_full")
                v.tensor_tensor(X.h[:, MW:MW + AH * AD].rearrange("p (h d) -> p h d", h=AH),
                                X.ps_s[:, 0, 0:AH * AD].rearrange("p (h d) -> p h d", h=AH),
                                repeat_last(X.ssum[:, :], AD), ALU.mult).then_inc(s["oa_ready"], 1)
                T.on(dve, "upd_full")
                for h in range(MH):
                    v.scalar_tensor_tensor(X.CT[:, h, :], X.CT[:, h, :], X.lval[:, 4 + h:5 + h],
                                           X.ps_n[0][:, h * DH:(h + 1) * DH], ALU.mult, ALU.add)
                chain(v.tensor_tensor(X.nT[:, :], X.nT[:, :], X.lval[:, 4:8], ALU.mult))
                v.tensor_tensor(X.nT[:, :], X.nT[:, :], X.ps_m[:, 24:28], ALU.add).then_inc(s["state_ready"], 1)
                T.t_out(dve, T_CONV)
                y = X.diag[:, 0:2, :]
                for a in range(2):
                    last = v.tensor_scalar(y[:, a, :], X.uT[:, a, 0:P], X.cw[:, 0, a:a + 1], None, ALU.mult)
                chain(last)
                for j in range(1, CK):
                    for a in range(2):
                        last = v.scalar_tensor_tensor(y[:, a, :], X.uT[:, a, j:j + P], X.cw[:, j, a:a + 1], y[:, a, :],
                                                      ALU.mult, ALU.add)
                    chain(last)
                chain(v.tensor_tensor(X.mixT[:, 6:8, :], y, X.cbT[:, :, :], ALU.mult))
                v.tensor_copy(X.uT[:, :, 0:CK - 1], X.uT[:, :, P:P + CK - 1]).then_inc(s["yc_ready"], 1)
                T.t_landed(dve, T_HM)
                v.tensor_copy(X.mixT[:, 0:4, :], X.ps_t[:, :, :]).then_inc(s["t_free"], 1)
                if more:
                    tile(t + 1).dve_rms(dve, chain)
                T.dve_residual(dve, chain)

            dve.wait_ge(s["small_in"], 16 * (3 + CK))
            tile(0).dve_rms(dve, chain)
            with dve.Fori(0, NT - 1) as t:
                chain.enter(t, 28)
                body(t)
            chain.leave(NT - 1)
            body(NT - 1, more=False)

        @block.tensor
        def _(pe):
            e = K["ident"]
            pe.wait_ge(s["w_in_in"], W_IN_LOADS * 16)

            def body(t, more=True):
                T = tile(t)
                T.project(pe, K)
                for h in range(MH):
                    nc.tensor.matmul(X.ps_n[1][:, h * DH:(h + 1) * DH], X.qT[:, h, :], X.CT[:, h, :], start=True, stop=True)
                    nc.tensor.matmul(X.ps_m[:, 8 + h:9 + h], X.qT[:, h, :], X.nT[:, h:h + 1], start=True, stop=True)
                T.on(pe, "p_ready")
                for h in range(AH):
                    kv, g = h // 2, h % 2
                    mm = nc.tensor.matmul(X.ps_s[:, h // 2, (h % 2) * 2 * P:(h % 2 + 1) * 2 * P],
                                          X.sqT[kv * AD:(kv + 1) * AD, g, :], X.skT[kv * AD:(kv + 1) * AD, :],
                                          start=True, stop=True)
                mm.then_inc(s["swa_full"], 1)
                T.transpose_weights(pe, K)
                T.on(pe, "swa_exp")
                T.batch(pe, T_A0, [(X.sc[:, h, a * P:(a + 1) * P], P, P) for h in range(2) for a in range(2)], e)
                T.intra(pe, K)
                T.batch(pe, T_A1, [(X.sc[:, h, a * P:(a + 1) * P], P, P) for h in range(2, 4) for a in range(2)], e)
                T.t_out(pe, T_A1)
                for h in range(AH):
                    kv = h // 2
                    for a, vals in enumerate((X.sv_prev, X.g6)):
                        mm = nc.tensor.matmul(X.ps_s[:, 0, h * AD:(h + 1) * AD], X.hT[:, 2 * h + a, :],
                                              vals[:, kv * AD:(kv + 1) * AD], start=(a == 0), stop=(a == 1))
                mm.then_inc(s["pv_full"], 1)
                T.on(pe, "u_ready")
                T.batch(pe, T_CONV, [(X.u[:, 0:P], P, P), (X.u[:, P:], P, P), (X.g6[:, 128:256], P, P), (X.g6[:, 256:384], P, P)], e)
                T.on(pe, "numf_ready")
                T.on(pe, "vw_ready")
                for h in range(MH):
                    nc.tensor.matmul(X.ps_n[0][:, h * DH:(h + 1) * DH], X.kz[:, h * DH:(h + 1) * DH], X.diag[:, h, :],
                                     start=True, stop=True)
                    mm = nc.tensor.matmul(X.ps_m[:, 24 + h:25 + h], X.kz[:, h * DH:(h + 1) * DH], X.lval[:, h:h + 1],
                                          start=True, stop=True)
                mm.then_inc(s["upd_full"], 1)
                T.on(pe, "hm_ready")
                T.batch(pe, T_HM, [(X.h[:, h * DH:(h + 1) * DH], P, DH) for h in range(MH)], e)
                T.on(pe, "oa_ready")
                T.batch(pe, T_OA, [(X.h[:, MW + a * P:MW + (a + 1) * P], P, P) for a in range(2)], e)
                T.t_out(pe, T_OA)
                T.out_product(pe)
                if more:
                    tile(t + 1).transpose_rows(pe, K)
                    T.on(pe, "x1_ready")
                    T.on(pe, "pool_done")

            tile(0).transpose_rows(pe, K)
            with pe.Fori(0, NT - 1) as t:
                body(t)
            body(NT - 1, more=False)
            pe.wait_ge(s["state_ready"], NT)
            for h in range(MH):
                last = nc.tensor.transpose(X.ps_t[:, h, :], X.CT[:, h, :], e[:, :])
            last.then_inc(s["t_full"], 1)


S_C0 = T_P + 1
S_I = S_C0 + B
S_K0, S_K1, S_SC, S_P, S_CONV, S_ST, S_HM = range(S_I + 1, S_I + 8)
EXTRA = ("c_in kv_in small2_in si_full int_ready cu_full cu_out nu_full n_ready w8_full w8_out km_ready sw_full "
         "st_ready pn_ready y_stored").split()


def mix_sample(nc, I, O, mod, x1_dram, X, K, s):
    W = X.w_in[:, :, :].rearrange("p a b -> p (a b)")
    at = [0]

    def take(rows, n, pattern=None, **dims):
        ap = W[0:rows, at[0]:at[0] + n]
        at[0] += n
        return ap.rearrange(pattern, **dims) if pattern else ap

    Cs = take(P, B * MH * DH, "p (m k) -> p m k", k=DH)
    CTs = take(P, B * MH * DH, "p (m k) -> p m k", k=DH)
    Km = take(NS, MH * B * DH, "p (h b k) -> p h b k", h=MH, b=B)
    kc = take(P, B * P, "p (b c) -> p b c", b=B)
    vc = take(P, B * P, "p (b c) -> p b c", b=B)
    kcT = take(P, B * P, "p (b c) -> p b c", b=B)
    nq = take(NS, MW)
    nqz = take(NS, MW)
    n8 = take(B, MW)
    stc = take(2 * B, CW)
    intT = take(P, MH * NS)
    sT = take(P, AH * NS)
    sN = take(NS, AH * NS)
    sc = take(P, WIN + NS)
    pTc = take(P, AH * NS)
    pTn = take(NS, AH * NS)
    full = take(P, 2 * B * (TS + CK - 1), "p (a b w) -> p a b w", a=2, b=B)
    y = take(P, 2 * B * TS, "p (a b t) -> p a b t", a=2, b=B)
    lw = take(NS, MH * B, "p (h b) -> p h b", h=MH)
    wsel = take(NS, B * MH)
    lv8 = take(NS, 8)
    w8 = take(B, 8)
    wlib = take(P, B * MH)
    nden = take(NS, MH)

    T = Tile(nc, X, s, 0, NS, K["tri_s"][:, :], K["mask_s"][:, :], K["last_s"][:, :])
    T.per_t = 0
    last_of = K["last_s"][:, :].rearrange("p (b i) -> p b i", i=TS)[:, :, 0]

    with nc.Block() as block:
        @block.sync
        def _(sp):
            k_new, v_new = O["swa_k_s"][0], O["swa_v_s"][0]
            sp.dma_start(k_new[:, 0:WIN - TS], I["cache_swa_k"][0, :, TS:WIN]).then_inc(s["y_stored"], 16)
            sp.dma_start(v_new[:, 0:WIN - TS], I["cache_swa_v"][0, :, TS:WIN]).then_inc(s["y_stored"], 16)
            stored = 2
            load_mod_rows(sp, nc, I, mod, X, s, True)
            for b in range(B):
                sp.dma_start(X.mprev[b * TS:(b + 1) * TS, :], I["state_mlstm_m"][0, b].partition_broadcast(TS))\
                    .then_inc(s["small_in"], 16)
            for h in range(AH):
                sp.dma_start(X.sink[h * NS:(h + 1) * NS, 0:1], I["swa_sinks"][0, h:h + 1].partition_broadcast(NS))\
                    .then_inc(s["small_in"], 16)
            sp.wait_ge(s["small_in"], 16 * (B + AH))
            sp.wait_ge(s["rows_ready"], 1)
            sp.dma_start(X.xt[0:NS, :], I["x_sample"].rearrange("b t d -> (b t) d")).then_inc(s["x_in"], 16)
            T.on(sp, "h_ready")
            sp.dma_start(X.xr[0:NS, :], I["x_sample"].rearrange("b t d -> (b t) d")).then_inc(s["xr_in"], 16)
            T.z_landed(sp, OZ)
            sp.dma_start(Cs, I["state_mlstm_C"][0].rearrange("b h v k -> v (b h) k")).then_inc(s["c_in"], 16)
            sp.dma_start(kc, I["cache_swa_k"][0].rearrange("b w h d -> w b (h d)")).then_inc(s["kv_in"], 16)
            sp.dma_start(vc, I["cache_swa_v"][0].rearrange("b w h d -> w b (h d)")).then_inc(s["kv_in"], 16)
            for b in range(B):
                sp.dma_start(nq[b * TS:(b + 1) * TS, :], I["state_mlstm_n"][0, b].rearrange("h k -> (h k)")
                             .partition_broadcast(TS)).then_inc(s["small2_in"], 16)
            sp.dma_start(n8, I["state_mlstm_n"][0].rearrange("b h k -> b (h k)")).then_inc(s["small2_in"], 16)
            sp.dma_start(stc, I["state_conv"][0].rearrange("b w c -> (b w) c")).then_inc(s["small2_in"], 16)
            T.z_out(sp, GATES)
            T.z_out(sp, SVCB)
            for b in range(B):
                for new, rows in ((k_new, X.g5[b * TS:(b + 1) * TS, 264:392]), (v_new, X.g6[b * TS:(b + 1) * TS, 0:P])):
                    sp.dma_start(new[b, WIN - TS:WIN].rearrange("w h d -> w (h d)"), rows).then_inc(s["y_stored"], 16)
                    stored += 1
            T.on(sp, "u_ready")
            for j in range(CK - 1):
                sp.dma_start(O["conv_s"][0, :, j], X.u[TS - CK + 1 + j:NS:TS, :]).then_inc(s["y_stored"], 16)
                stored += 1
            sp.wait_ge(s["n_ready"], 1)
            sp.dma_start(O["n_s"][0].rearrange("b h k -> b (h k)"), n8).then_inc(s["y_stored"], 16)
            sp.dma_start(O["m_s"][0], w8[:, 4:8]).then_inc(s["y_stored"], 16)
            sp.wait_ge(s["cu_out"], 2 * MH)
            sp.dma_start(O["C_s"][0].rearrange("b h v k -> v (b h) k"), Cs).then_inc(s["y_stored"], 16)
            T.on(sp, "x1_ready")
            sp.dma_start(x1_dram[SEQ:SEQ + NS, :], X.xr[0:NS, :]).then_inc(s["y_stored"], 16)
            sp.wait_ge(s["y_stored"], 16 * (stored + 4))

        @block.gpsimd
        def _(pool):
            T.pool_gates(pool)

        @block.scalar
        def _(act):
            chain = Chain(act, s["act_step"])
            a = nc.scalar.activation
            T.act_rms(act, chain)
            T.act_front(act, chain)
            for i in range(0, B, 2):
                T.t_landed(act, S_C0 + i)
                a(CTs[:, 4 * i:4 * i + 4, :], X.ps_t[:, :, :], ACT.Copy).then_inc(s["t_free"], 1)
            act.wait_ge(s["si_full"], 1)
            a(intT, X.ps_n[1][:, 0:P], ACT.Copy).then_inc(s["int_ready"], 1)
            T.act_norm(act, chain, X.ps_t[0:NS, :, :], lambda eng: T.t_landed(eng, S_I), "t_free")
            for k, half in ((S_K0, 0), (S_K1, 4)):
                T.t_landed(act, k)
                a(kcT[:, half:half + 4, :], X.ps_t[:, :, :], ACT.Copy).then_inc(s["t_free"], 1)
            act.wait_ge(s["sw_full"], 1)
            for kv in range(KVH):
                a(sT[:, kv * 2 * NS:(kv + 1) * 2 * NS], X.ps_n[kv][:, 0:2 * NS], ACT.Copy)
                last = a(sN[:, kv * 2 * NS:(kv + 1) * 2 * NS], X.ps_n[kv][0:NS, P:P + 2 * NS], ACT.Copy)
            last.then_inc(s["st_ready"], 1)
            T.on(act, "sc_ready")
            a(sc, sc, ACT.Exp, bias=X.smx[:, 1:2], accum_out=X.ssum[:, 0:1])
            a(X.ses[:, 0:1], X.ses[:, 0:1], ACT.Exp).then_inc(s["swa_exp"], 1)
            T.on(act, "pv_full")
            a(X.mixT[:, 4:6, 0:NS], X.ps_m[:, P:P + 2 * NS].rearrange("p (a t) -> p a t", a=2), ACT.Copy)\
                .then_inc(s["oa_ready"], 1)

        @block.vector
        def _(dve):
            chain = Chain(dve, s["dve_step"])
            v = nc.vector
            dve_mod_rows(dve, nc, X, s, True)
            T.dve_rms(dve, chain)
            T.dve_front(dve, chain, K)
            for i in range(1, B, 2):
                T.t_landed(dve, S_C0 + i)
                v.tensor_copy(CTs[:, 4 * i:4 * i + 4, :], X.ps_t[:, :, :]).then_inc(s["t_free"], 1)
            dve.wait_ge(s["small2_in"], 16 * (B + 2))
            chain(v.tensor_tensor(nqz, X.qz[0:NS, :], nq, ALU.mult))
            chain(v.tensor_reduce(nden, nqz.rearrange("p (h k) -> p h k", h=MH), AX, ALU.add))
            T.dve_num(dve, chain, nden, lambda eng: T.t_out(eng, S_I))
            T.dve_last(dve, chain)
            same = K["same"][:, :]
            v.tensor_tensor(lw, repeat_mid(same, MH), repeat_last(X.lval[0:NS, 0:4], B), ALU.mult)
            v.tensor_tensor(wsel.rearrange("p (b h) -> p b h", b=B), repeat_last(last_of, MH),
                            repeat_mid(X.lval[0:NS, 4:8], B), ALU.mult)
            v.tensor_copy(lv8[:, 0:4], X.lval[0:NS, 4:8])
            v.tensor_copy(lv8[:, 4:8], X.mt[0:NS, :])
            for h in range(MH):
                last = v.tensor_tensor(Km[:, h], repeat_mid(X.kz[0:NS, h * DH:(h + 1) * DH], B), repeat_last(same, DH),
                                       ALU.mult)
            last.then_inc(s["km_ready"], 1)
            T.dve_norm(dve, chain)
            dve.wait_ge(s["w8_full"], 1)
            v.tensor_copy(w8, X.ps_m[0:B, 0:8])
            v.tensor_copy(wlib, X.ps_m[:, 32:32 + B * MH]).then_inc(s["w8_out"], 1)
            dve.wait_ge(s["w8_out"], 1)
            dve.wait_ge(s["nu_full"], 1)
            for h in range(MH):
                cols = slice(h * DH, (h + 1) * DH)
                last = v.scalar_tensor_tensor(n8[:, cols], n8[:, cols], w8[:, h:h + 1], X.ps_n[0][0:B, cols], ALU.mult, ALU.add)
            last.then_inc(s["n_ready"], 1)
            for i in range(2 * MH):
                h, half = i // 2, i % 2
                dve.wait_ge(s["cu_full"], i + 1)
                for j in range(B // 2):
                    m = (half * (B // 2) + j) * MH + h
                    last = v.scalar_tensor_tensor(Cs[:, m, :], Cs[:, m, :], wlib[:, m:m + 1],
                                                  X.ps_s[:, i % 2, j * DH:(j + 1) * DH], ALU.mult, ALU.add)
                last.then_inc(s["cu_out"], 1)
            T.t_landed(dve, S_SC)
            v.scalar_tensor_tensor(sc, X.ps_t[:, :, :].rearrange("p a b -> p (a b)")[:, 0:WIN + NS], AD ** -0.5,
                                   K["s_bias"][:, :], ALU.mult, ALU.add).then_inc(s["t_free"], 1)
            T.t_out(dve, S_SC)
            chain(v.tensor_reduce(X.smx[:, 0:1], sc, AX, ALU.max))
            chain(v.tensor_tensor(X.smx[:, 0:1], X.smx[:, 0:1], X.sink[:, 0:1], ALU.max))
            v.tensor_tensor(X.ses[:, 0:1], X.sink[:, 0:1], X.smx[:, 0:1], ALU.subtract)
            v.tensor_scalar(X.smx[:, 1:2], X.smx[:, 0:1], -1.0, None, ALU.mult).then_inc(s["sc_ready"], 1)
            T.on(dve, "swa_exp")
            chain(v.tensor_tensor(X.ssum[:, 0:1], X.ssum[:, 0:1], X.ses[:, 0:1], ALU.add))
            chain(v.reciprocal(X.ssum[:, 0:1], X.ssum[:, 0:1]))
            v.tensor_scalar(sc, sc, X.ssum[:, 0:1], None, ALU.mult).then_inc(s["pn_ready"], 1)
            T.t_landed(dve, S_P)
            v.tensor_copy(pTc, X.ps_t[:, 0, :])
            v.tensor_copy(pTn, X.ps_t[0:NS, 1, :]).then_inc(s["t_free"], 1)
            T.t_landed(dve, S_CONV)
            v.tensor_copy(full[:, :, :, CK - 1:], X.ps_t[:, 0:2, 0:NS].rearrange("p a (b t) -> p a b t", b=B))
            v.tensor_copy(X.cbT[:, :, 0:NS], X.ps_t[:, 2:4, 0:NS]).then_inc(s["t_free"], 1)
            T.t_landed(dve, S_ST)
            v.tensor_copy(full[:, :, :, 0:CK - 1], X.ps_t[:, 0:2, 0:2 * B].rearrange("p a (b w) -> p a b w", b=B))\
                .then_inc(s["t_free"], 1)
            T.t_out(dve, S_ST)
            for a in range(2):
                last = v.tensor_scalar(y[:, a], full[:, a, :, 0:TS], X.cw[:, 0, a:a + 1], None, ALU.mult)
            chain(last)
            for j in range(1, CK):
                for a in range(2):
                    last = v.scalar_tensor_tensor(y[:, a], full[:, a, :, j:j + TS], X.cw[:, j, a:a + 1], y[:, a],
                                                  ALU.mult, ALU.add)
                chain(last)
            v.tensor_tensor(X.mixT[:, 6:8, 0:NS], y.rearrange("p a b t -> p a (b t)"), X.cbT[:, :, 0:NS], ALU.mult)\
                .then_inc(s["yc_ready"], 1)
            T.t_landed(dve, S_HM)
            v.tensor_copy(X.mixT[:, 0:4, 0:NS], X.ps_t[:, :, 0:NS]).then_inc(s["t_free"], 1)
            T.dve_residual(dve, chain)

        @block.tensor
        def _(pe):
            e = K["ident"]
            T.transpose_rows(pe, K)
            T.project(pe, K)
            T.transpose_weights(pe, K)
            pe.wait_ge(s["c_in"], 16)
            for i in range(B):
                T.batch(pe, S_C0 + i, [(Cs[:, 4 * i + j, :], P, P) for j in range(4)], e)
            T.t_out(pe, S_I - 1)
            for b in range(B):
                for h in range(MH):
                    mm = nc.tensor.matmul(X.ps_n[1][:, h * NS + b * TS:h * NS + (b + 1) * TS], CTs[:, b * MH + h, :],
                                          X.qT[:, h, b * TS:(b + 1) * TS], start=True, stop=True)
            mm.then_inc(s["si_full"], 1)
            pe.wait_ge(s["int_ready"], 1)
            T.batch(pe, S_I, [(intT[:, h * NS:(h + 1) * NS], P, NS) for h in range(MH)], e)
            T.intra(pe, K)
            T.on(pe, "numf_ready")
            T.on(pe, "vw_ready")
            pe.wait_ge(s["km_ready"], 1)
            nc.tensor.matmul(X.ps_m[0:B, 0:8], last_of, lv8, start=True, stop=True)
            nc.tensor.matmul(X.ps_m[:, 32:32 + B * MH], K["ones"][0:NS, :], wsel, start=True, stop=True)\
                .then_inc(s["w8_full"], 1)
            for h in range(MH):
                mm = nc.tensor.matmul(X.ps_n[0][0:B, h * DH:(h + 1) * DH], lw[:, h, :], X.kz[0:NS, h * DH:(h + 1) * DH],
                                      start=True, stop=True)
            mm.then_inc(s["nu_full"], 1)
            for i in range(2 * MH):
                h, half = i // 2, i % 2
                if i >= 2:
                    pe.wait_ge(s["cu_out"], i - 1)
                nc.tensor.matmul(X.ps_s[:, i % 2, :], X.diag[0:NS, h, :], Km[:, h, half * (B // 2):(half + 1) * (B // 2), :],
                                 start=True, stop=True).then_inc(s["cu_full"], 1)
            pe.wait_ge(s["kv_in"], 32)
            T.batch(pe, S_K0, [(kc[:, b, :], P, P) for b in range(4)], e)
            T.batch(pe, S_K1, [(kc[:, b, :], P, P) for b in range(4, 8)], e)
            T.t_out(pe, S_K1)
            pe.wait_ge(s["n_ready"], 1)
            for h in range(AH):
                kv, g = h // 2, h % 2
                rows = slice(kv * AD, (kv + 1) * AD)
                for b in range(B):
                    nc.tensor.matmul(X.ps_n[kv][:, g * NS + b * TS:g * NS + (b + 1) * TS], kcT[rows, b, :],
                                     X.sqT[rows, g, b * TS:(b + 1) * TS], start=True, stop=True)
                mm = nc.tensor.matmul(X.ps_n[kv][0:NS, P + g * NS:P + (g + 1) * NS], X.skT[rows, P:P + NS],
                                      X.sqT[rows, g, 0:NS], start=True, stop=True)
            mm.then_inc(s["sw_full"], 1)
            pe.wait_ge(s["st_ready"], 1)
            T.batch(pe, S_SC, [(sT, P, P), (sN, NS, P)], e)
            pe.wait_ge(s["pn_ready"], 1)
            T.batch(pe, S_P, [(sc[:, 0:WIN], P, P), (sc[:, WIN:], P, NS)], e)
            T.t_out(pe, S_P)
            pe.wait_ge(s["w8_out"], 1)
            for h in range(AH):
                kv = h // 2
                vals = slice(kv * AD, (kv + 1) * AD)
                out = X.ps_m[(h % 2) * AD:(h % 2 + 1) * AD, P + (h // 2) * NS:P + (h // 2 + 1) * NS]
                nc.tensor.matmul(out, X.g6[0:NS, vals], pTn[:, h * NS:(h + 1) * NS], start=True, stop=False)
                for b in range(B):
                    mm = nc.tensor.matmul(out[:, b * TS:(b + 1) * TS], vc[:, b, vals],
                                          pTc[:, h * NS + b * TS:h * NS + (b + 1) * TS], start=False, stop=(b == B - 1))
            mm.then_inc(s["pv_full"], 1)
            T.on(pe, "u_ready")
            T.batch(pe, S_CONV, [(X.u[0:NS, 0:P], NS, P), (X.u[0:NS, P:], NS, P),
                                 (X.g6[0:NS, 128:256], NS, P), (X.g6[0:NS, 256:384], NS, P)], e)
            pe.wait_ge(s["small2_in"], 16 * (B + 2))
            T.batch(pe, S_ST, [(stc[:, 0:P], 2 * B, P), (stc[:, P:], 2 * B, P)], e)
            T.on(pe, "hm_ready")
            T.batch(pe, S_HM, [(X.h[0:NS, h * DH:(h + 1) * DH], NS, DH) for h in range(MH)], e)
            T.t_out(pe, S_HM)
            T.on(pe, "oa_ready")
            T.out_product(pe)


def second_norm(nc, I, mod, x1_dram, h2_dram, wq, wq_in, K):
    NTS = NT + 1
    with ExitStack() as ctx:
        def sb(name, shape):
            return ctx.enter_context(nc.sbuf_tensor(name, shape, F32))

        x, h = sb("n2_x", [P, NTS, D]), sb("n2_h", [P, NTS, D])
        scale, shift, gain = sb("n2_scale", [P, 2, D]), sb("n2_shift", [P, 2, D]), sb("n2_gain", [P, D])
        eps, ss, rt, r = sb("n2_eps", [P, 1]), sb("n2_ss", [P, NTS]), sb("n2_rt", [P, NTS]), sb("n2_r", [P, NTS])
        s = {n: ctx.enter_context(nc.semaphore("n2_" + n))
             for n in ["rows_in", "init", "ss_ready", "rt_ready", "a_ready", "step", "h_ready", "h_out"]}
        x_in = [ctx.enter_context(nc.semaphore(f"n2_x_in{t}")) for t in range(NTS)]

        with nc.Block() as block:
            @block.sync
            def _(sp):
                for t in range(NT):
                    sp.dma_start(x[:, t, :], x1_dram[t * P:(t + 1) * P, :]).then_inc(x_in[t], 16)
                sp.dma_start(x[0:NS, NT, :], x1_dram[SEQ:SEQ + NS, :]).then_inc(x_in[NT], 16)
                wq_dram = I["peer_wq"][0].rearrange("(kc p) n -> p kc n", p=P)
                for dst, k in ((scale, 4), (shift, 3)):
                    sp.dma_start(dst[:, 0, :], mod[0, k * D:(k + 1) * D].partition_broadcast(P)).then_inc(s["rows_in"], 16)
                    for b in range(B):
                        sp.dma_start(dst[b * TS:(b + 1) * TS, 1, :],
                                     mod[1 + b, k * D:(k + 1) * D].partition_broadcast(TS)).then_inc(s["rows_in"], 16)
                sp.dma_start(gain[:, :], I["norm_ffn_g"][0].partition_broadcast(P)).then_inc(s["rows_in"], 16)
                for i, landed in enumerate(wq_in):
                    cols = slice(i * 4 * P, (i + 1) * 4 * P)
                    sp.dma_start(wq[:, :, cols], wq_dram[:, :, cols]).then_inc(landed, 16)
                for t in range(NTS):
                    sp.wait_ge(s["h_ready"], t + 1)
                    sp.dma_start(h2_dram[t * P:(t + 1) * P, :], h[:, t, :]).then_inc(s["h_out"], 16)
                sp.wait_ge(s["h_out"], 16 * NTS)

            @block.gpsimd
            def _(pool):
                nc.gpsimd.memset(eps[:, :], EPS)
                nc.gpsimd.memset(h[:, NT, :], 0.0).then_inc(s["init"], 1)

            @block.scalar
            def _(act):
                a = nc.scalar.activation
                act.wait_ge(s["init"], 1)
                for t in range(NTS):
                    n = P if t < NT else NS
                    act.wait_ge(x_in[t], 16)
                    a(h[0:n, t, :], x[0:n, t, :], ACT.Square, accum_out=ss[0:n, t:t + 1]).then_inc(s["ss_ready"], 1)
                act.wait_ge(s["ss_ready"], NTS)
                a(rt[:, 0:NT], ss[:, 0:NT], ACT.Sqrt, scale=1.0 / D, bias=eps[:, :])
                a(rt[0:NS, NT:], ss[0:NS, NT:], ACT.Sqrt, scale=1.0 / D, bias=eps[0:NS, :]).then_inc(s["rt_ready"], 1)

            @block.vector
            def _(dve):
                chain = Chain(dve, s["step"])
                v = nc.vector
                dve.wait_ge(s["rows_in"], 16 * (2 * (1 + B) + 1))
                v.scalar_tensor_tensor(scale[:, 0, :], scale[:, 0, :], 1.0, gain[:, :], ALU.add, ALU.mult)
                chain(v.scalar_tensor_tensor(scale[0:NS, 1, :], scale[0:NS, 1, :], 1.0, gain[0:NS, :], ALU.add, ALU.mult))
                dve.wait_ge(s["rt_ready"], 1)
                v.reciprocal(r[:, 0:NT], rt[:, 0:NT])
                chain(v.reciprocal(r[0:NS, NT:], rt[0:NS, NT:]))
                for t in range(NTS):
                    n, k = (P, 0) if t < NT else (NS, 1)
                    chain(v.scalar_tensor_tensor(h[0:n, t, :], x[0:n, t, :], r[0:n, t:t + 1], scale[0:n, k, :],
                                                 ALU.mult, ALU.mult))
                    v.tensor_tensor(h[0:n, t, :], h[0:n, t, :], shift[0:n, k, :], ALU.add).then_inc(s["h_ready"], 1)


NB = 8
GPT = PH * TOPK // NB
PPT = GPT // 2
NG = NT * GPT
QS = P // NS
SG = PH * TOPK // QS // NB


def experts(nc, I, O, mod, x1_dram, h2_dram, wq, wq_in, K):
    with ExitStack() as ctx:
        def sb(name, shape, dt=F32):
            return ctx.enter_context(nc.sbuf_tensor(name, shape, dt))

        def ps(name, shape):
            return ctx.enter_context(nc.psum_tensor(name, shape, F32))

        h_next, hT = sb("h_next", [P, D]), sb("hT_next", [P, KC, P])
        sub, subT = sb("subkeys", [PK, 2, P]), sb("subkeysT", [P, 2, PK])
        q, qT, sc, scw = sb("q", [P, 2, P]), sb("qT", [P, 2, P]), sb("key_scores", [P, 2, PK]), sb("key_scores_w", [P, 2, PK])
        top, topi, topf = sb("top", [P, 2, TOPK]), sb("top_i", [P, 2, TOPK], U32), sb("top_f", [P, 2, TOPK])
        cand, candw = sb("cand", [P, TOPK * TOPK]), sb("cand_w", [P, TOPK * TOPK])
        cs, ci = sb("cand_top", [P, TOPK]), sb("cand_i", [P, TOPK], U32)
        ab, abf = sb("sel_ab", [P, 2, TOPK], U32), sb("sel_abf", [P, 2, TOPK])
        hot, sel = sb("one_hot", [P, 2, TOPK, TOPK]), sb("selected", [P, 2, TOPK])
        iota = sb("iota_f", [P, TOPK])
        idx = sb("expert_idx", [P, (NT + 1) * PH * TOPK], U32)
        gate = sb("expert_gate", [P, (NT + 1) * PH * TOPK])
        gsum = sb("gate_sum", [P, 2])
        idx_s, gate_s = sb("sample_idx", [P, SG * NB], U32), sb("sample_gate", [P, SG * NB])
        h_cur = sb("h_cur", [P, D])
        u_rows, v_rows = sb("u_rows", [P, NB, D]), sb("v_rows", [P, NB, D])
        u_idx, v_idx = sb("u_idx", [P, 2, NB], U32), sb("v_idx", [P, 2, NB], U32)
        dots, act_val, wts = sb("dots", [P, 2, NB]), sb("act_val", [P, 2, NB]), sb("wts", [P, 2, NB])
        diag = sb("wt_diag", [P, 2, NB, P])
        x1, y, gate2, gate2_s, fin = sb("x1", [P, D]), sb("y", [P, D]), sb("gate2", [P, D]), sb("gate2_s", [NS, D]), sb("final_g", [P, D])
        fs, eps = sb("final_stat", [P, 4]), sb("eps2", [P, 1])
        fold = sb("fold", [P, NS])
        ps_y, ps_h, ps_r = ps("ps_y", [P, D]), ps("ps_h", [P, KC, P]), ps("ps_r", [P, 3, 512])
        names = ("sub_in small_in init subT_full subT_out hn_in hT_full hT_out copied q_full q_out qt_full qt_out sc_full "
                 "sc_out sc_free routed gate_raw exp_ready normed hs_in u_staged v_staged u_used v_used "
                 "act_ready wts_ready diag_ready y_out x1_in ss_ready rt_ready done stored step "
                 "folded sub_step").split()
        spread_in = [ctx.enter_context(nc.semaphore(f"spread_in{g}")) for g in range(SG)]
        s = {n: ctx.enter_context(nc.semaphore("ex_" + n)) for n in names}
        u_in = [ctx.enter_context(nc.semaphore(f"u_in{j}")) for j in range(NB)]
        v_in = [ctx.enter_context(nc.semaphore(f"v_in{j}")) for j in range(NB)]

        with nc.Block() as block:
            @block.sync
            def _(sp):
                sp.dma_start(sub[:, :, :], I["peer_subkeys"][0].rearrange("a k d -> k a d")).then_inc(s["sub_in"], 16)
                sp.dma_start(h_next[:, :], h2_dram[0:P, :]).then_inc(s["hn_in"], 16)
                sp.dma_start(gate2[:, :], mod[0, 5 * D:6 * D].partition_broadcast(P)).then_inc(s["small_in"], 16)
                for b in range(B):
                    sp.dma_start(gate2_s[b * TS:(b + 1) * TS, :], mod[1 + b, 5 * D:6 * D].partition_broadcast(TS))\
                        .then_inc(s["small_in"], 16)
                sp.dma_start(fin[:, :], I["final_g"].partition_broadcast(P)).then_inc(s["small_in"], 16)
                sp.dma_start(x1[:, :], x1_dram[0:P, :]).then_inc(s["x1_in"], 16)

                def next_rows(t):
                    hold(sp, s["copied"], t + 1)
                    hold(sp, s["hT_out"], t + 1)
                    sp.dma_start(h_next[:, :], h2_dram[bass.ds(t * P + P, P), :]).then_inc(s["hn_in"], 16)

                def finish(t, rows=P):
                    hold(sp, s["done"], t + 1)
                    sp.dma_start(O["y_p"][0, bass.ds(t * P, P), :], x1[:, :]).then_inc(s["stored"], 16)
                    hold(sp, s["stored"], t * 16 + 16)
                    sp.dma_start(x1[0:rows, :], x1_dram[bass.ds(t * P + P, rows), :]).then_inc(s["x1_in"], 16)

                next_rows(0)
                with sp.Fori(0, NT - 1) as t:
                    next_rows(t + 1)
                    finish(t)
                for g in range(SG):
                    if g == SG - 1:
                        sp.wait_ge(s["u_used"], NG * NB)
                        for i in range(QS):
                            sp.dma_start(h_cur[i * NS:(i + 1) * NS, :], h2_dram[SEQ:SEQ + NS, :]).then_inc(s["hs_in"], 16)
                    sp.wait_ge(s["normed"], NT * PH + 2 * g + 2)
                    for i in range(QS):
                        rows, first = slice(i * NS, (i + 1) * NS), NT * P + (g * QS + i) * NB
                        for dst, src in ((idx_s, idx), (gate_s, gate)):
                            sp.dma_start(dst[rows, g * NB:(g + 1) * NB], src[0:NS, first:first + NB])\
                                .then_inc(spread_in[g], 16)
                finish(NT - 1, NS)
                sp.wait_ge(s["done"], NT + 1)
                sp.dma_start(O["y_s"].rearrange("b t d -> (b t) d"), x1[0:NS, :]).then_inc(s["stored"], 16)
                sp.wait_ge(s["stored"], 16 * (NT + 1))

            @block.gpsimd
            def _(pool):
                g = nc.gpsimd
                g.tensor_copy(iota[:, :], K["iota16"][:, :])
                g.memset(eps[:, :], EPS)
                g.memset(fold[:, :], 0.0).then_inc(s["init"], 1)
                pool.wait_ge(s["init"], 1)
                for i in range(QS):
                    g.affine_select(out=fold[:, :], in_=fold[:, :], compare_op=ALU.not_equal, fill=1.0, base=-i * NS,
                                    pattern=[[-1, NS]], channel_multiplier=1).then_inc(s["init"], 1)
                    pool.wait_ge(s["init"], 2 + i)

                def gather(rows, table, where, landed, used, i, j, first=False):
                    if not first:
                        hold(pool, used, i * NB + (j + 1 - NB))
                    g.indirect_dma_start(rows[:, j, :], None, table, bass.IndirectOffsetOnAxis(where[:, j:j + 1], 0))\
                        .then_inc(landed[j], 16)

                def stage(dst, src, signal, used, i, par, first=False):
                    if not first:
                        hold(pool, used, i * NB - NB)
                    g.tensor_copy(dst[:, par, :], src).then_inc(signal, 1)
                    hold(pool, signal, i + 1)

                U, V = I["peer_u"][0], I["peer_v"][0]

                def step(i, par, u_src, v_src, first=False):
                    stage(u_idx, u_src, s["u_staged"], s["u_used"], i, par, first)
                    stage(v_idx, v_src, s["v_staged"], s["v_used"], i - 1, 1 - par, first or (isinstance(i, int) and i == 2))
                    for j in range(NB):
                        gather(u_rows, U, u_idx[:, par], u_in, s["u_used"], i, j)
                        gather(v_rows, V, v_idx[:, 1 - par], v_in, s["v_used"], i - 1, j, first)

                def cols(i):
                    return idx[:, bass.ds(i * NB, NB)]

                pool.wait_ge(s["routed"], 1)
                stage(u_idx, cols(0), s["u_staged"], s["u_used"], 0, 0, True)
                for j in range(NB):
                    gather(u_rows, U, u_idx[:, 0], u_in, s["u_used"], 0, j, True)
                step(1, 1, cols(1), cols(0), True)
                pool.wait_ge(s["routed"], 2)
                step(2, 0, cols(2), cols(1))
                step(3, 1, cols(3), cols(2))
                with pool.Fori(2, NG // 2) as pair:
                    hold(pool, s["routed"], pair + 1)
                    first = pair * 2
                    for par in range(2):
                        step(first + par, par, idx[:, bass.ds(pair * (2 * NB) + par * NB, NB)],
                             idx[:, bass.ds(pair * (2 * NB) + (par - 1) * NB, NB)])
                for i in range(NG, NG + SG):
                    pool.wait_ge(spread_in[i - NG], 2 * 16 * QS)
                    step(i, i % 2, idx_s[:, (i - NG) * NB:(i - NG + 1) * NB],
                         cols(i - 1) if i == NG else idx_s[:, (i - 1 - NG) * NB:(i - NG) * NB])
                i = NG + SG
                stage(v_idx, idx_s[:, (SG - 1) * NB:], s["v_staged"], s["v_used"], i - 1, (i - 1) % 2)
                for j in range(NB):
                    gather(v_rows, V, v_idx[:, (i - 1) % 2], v_in, s["v_used"], i - 1, j)

            @block.scalar
            def _(act):
                a = nc.scalar.activation

                def hT_copy(t):
                    hold(act, s["hT_full"], t + 1)
                    a(hT[:, 0:4, :], ps_h[:, 0:4, :], ACT.Copy)
                    a(hT[:, 4:8, :], ps_h[:, 4:8, :], ACT.Copy).then_inc(s["hT_out"], 1)

                def head(H):
                    hold(act, s["q_full"], H + 1)
                    a(q[:, :, :], ps_r[:, 0, 0:256], ACT.Copy).then_inc(s["q_out"], 1)
                    hold(act, s["qt_full"], H + 1)
                    a(qT[:, :, :], ps_r[:, 1, 0:256], ACT.Copy).then_inc(s["qt_out"], 1)
                    hold(act, s["sc_full"], H + 1)
                    hold(act, s["sc_free"], H + 1)
                    a(sc[:, :, :], ps_r[:, 2, 0:256], ACT.Copy).then_inc(s["sc_out"], 1)

                def group(i, par, first=False):
                    hold(act, s["u_used"], i * NB + NB)
                    a(act_val[:, par, :], dots[:, par, :], ACT.Gelu_apprx_tanh).then_inc(s["act_ready"], 1)
                    if not first:
                        hold(act, s["v_used"], i * NB - NB)
                    hold(act, s["wts_ready"], i + 1)
                    for j in range(NB):
                        a(diag[:, par, j, :], K["ident"][:, :], ACT.Copy, scale=wts[:, par, j:j + 1])\
                            .then_inc(s["diag_ready"], 1)

                def gate_exp(H):
                    hold(act, s["gate_raw"], H + 1)
                    cols = bass.ds(H * TOPK, TOPK)
                    a(gate[:, cols], gate[:, cols], ACT.Exp, accum_out=gsum[:, 0:1]).then_inc(s["exp_ready"], 1)

                def pair(i, H, two=False, first=False, between=None):
                    head(H)
                    group(i, 0, first)
                    if between:
                        between()
                    if two:
                        gate_exp(H)
                        head(H + 1)
                    group(i + 1, 1, first)
                    gate_exp(H + 1 if two else H)

                def y_copy(last_group):
                    hold(act, s["v_used"], last_group * NB + NB)
                    a(y[:, 0:512], ps_y[:, 0:512], ACT.Copy)
                    a(y[:, 512:D], ps_y[:, 512:D], ACT.Copy).then_inc(s["y_out"], 1)

                def root(t, n=P):
                    hold(act, s["ss_ready"], t + 1)
                    a(fs[0:n, 1:2], fs[0:n, 0:1], ACT.Sqrt, scale=1.0 / D, bias=eps[0:n, :]).then_inc(s["rt_ready"], 1)

                act.wait_ge(s["init"], 1 + QS)
                act.wait_ge(s["subT_full"], 1)
                a(subT[:, :, :], ps_r[:, 1, 0:256], ACT.Copy).then_inc(s["subT_out"], 1)
                hT_copy(0)
                for H in range(2):
                    head(H)
                    gate_exp(H)
                pair(0, 2, first=True)
                with act.Fori(0, NT - 1) as t:
                    with act.Fori(1, PPT - 2) as p:
                        pair(t * GPT + p * 2, t * PH + p + 2)
                    hT_copy(t + 1)
                    with act.Fori(PPT - 2, PPT) as p:
                        pair(t * GPT + p * 2, t * PH + p + 2)
                    pair(t * GPT + GPT, t * PH + (PH + 2), between=lambda: y_copy(t * GPT + (GPT - 1)))
                    root(t)
                with act.Fori(1, 3) as p:
                    pair(p * 2 + (NT - 1) * GPT, p * 2 + ((NT - 1) * PH + 1), two=True)
                pair((NT - 1) * GPT + 6, NT * PH - 1)
                hT_copy(NT)
                with act.Fori(4, PPT) as p:
                    pair(p * 2 + (NT - 1) * GPT, p * 2 + (NT * PH - 8), two=True)
                group(NG, 0)
                y_copy(NG - 1)
                group(NG + 1, 1)
                root(NT - 1)
                group(NG + 2, 0)
                group(NG + 3, 1)
                y_copy(NG + SG - 1)
                root(NT, NS)

            @block.vector
            def _(dve):
                chain = Chain(dve, s["step"])
                v = nc.vector

                def group(i, par, gates):
                    for j in range(NB):
                        hold(dve, u_in[j], i * 16 + 16)
                        v.tensor_tensor_reduce(u_rows[:, j, :], u_rows[:, j, :], h_cur[:, :], 1.0, 0.0, ALU.mult, ALU.add,
                                               dots[:, par, j:j + 1]).then_inc(s["u_used"], 1)
                    hold(dve, s["act_ready"], i + 1)
                    v.tensor_tensor(wts[:, par, :], act_val[:, par, :], gates, ALU.mult).then_inc(s["wts_ready"], 1)

                def top16(vals, where, scores, work):
                    chain(v.max(vals[:, 0:8], scores))
                    chain(v.match_replace(work, vals[:, 0:8], scores, NEG))
                    chain(v.max(vals[:, 8:16], work))
                    v.max_index(where[:, 0:8], vals[:, 0:8], scores)
                    return v.max_index(where[:, 8:16], vals[:, 8:16], work)

                def route(H):
                    hold(dve, s["sc_out"], H + 1)
                    top16(top[:, 0], topi[:, 0], sc[:, 0, :], scw[:, 0, :])
                    top16(top[:, 1], topi[:, 1], sc[:, 1, :], scw[:, 1, :]).then_inc(s["sc_free"], 1)
                    v.tensor_tensor(cand[:, :].rearrange("p (a b) -> p a b", a=TOPK), repeat_last(top[:, 0, :], TOPK),
                                    repeat_mid(top[:, 1, :], TOPK), ALU.add).then_inc(s["sub_step"], 1)
                    hold(dve, s["sub_step"], H + 1)
                    v.tensor_copy(topf[:, :, :], topi[:, :, :])
                    chain(top16(cs, ci, cand[:, :], candw[:, :]))
                    cols = bass.ds(H * TOPK, TOPK)
                    v.tensor_scalar(gate[:, cols], cs[:, :], cs[:, 0:1], None, ALU.subtract).then_inc(s["gate_raw"], 1)
                    v.tensor_scalar(ab[:, 0, :], ci[:, :], 4, None, ALU.logical_shift_right)
                    chain(v.tensor_scalar(ab[:, 1, :], ci[:, :], 15, None, ALU.bitwise_and))
                    chain(v.tensor_copy(abf[:, :, :], ab[:, :, :]))
                    for k in range(2):
                        last = v.tensor_tensor(hot[:, k], repeat_last(abf[:, k, :], TOPK), repeat_mid(iota[:, :], TOPK),
                                               ALU.is_equal)
                    chain(last)
                    for k in range(2):
                        last = v.tensor_tensor(hot[:, k], hot[:, k], repeat_mid(topf[:, k, :], TOPK), ALU.mult)
                    chain(last)
                    chain(v.tensor_reduce(sel[:, :, :], hot[:, :, :, :], AX, ALU.add))
                    v.scalar_tensor_tensor(idx[:, cols], sel[:, 0, :], float(PK), sel[:, 1, :], ALU.mult, ALU.add)\
                        .then_inc(s["routed"], 1)
                    hold(dve, s["exp_ready"], H + 1)
                    chain(v.reciprocal(gsum[:, 1:2], gsum[:, 0:1]))
                    v.tensor_scalar(gate[:, cols], gate[:, cols], gsum[:, 1:2], None, ALU.mult).then_inc(s["normed"], 1)
                    hold(dve, s["normed"], H + 1)

                ROUTE = 16

                def begin(t):
                    hold(dve, s["hn_in"], t * 16 + 16)
                    v.tensor_copy(h_cur[:, :], h_next[:, :]).then_inc(s["copied"], 1)
                    hold(dve, s["copied"], t + 1)

                def pair(i, first, H, two=False):
                    group(i, 0, gate[:, bass.ds(first, NB)])
                    if two:
                        route(H)
                    group(i + 1, 1, gate[:, bass.ds(first + NB, NB)])
                    route(H + 1 if two else H)

                def finish(t, n, src, row):
                    hold(dve, s["x1_in"], t * 16 + 16)
                    chain(v.tensor_tensor(y[0:n, :], src, row, ALU.mult))
                    chain(v.tensor_tensor(x1[0:n, :], x1[0:n, :], y[0:n, :], ALU.add))
                    v.tensor_tensor_reduce(y[0:n, :], x1[0:n, :], x1[0:n, :], 1.0, 0.0, ALU.mult, ALU.add, fs[0:n, 0:1])\
                        .then_inc(s["ss_ready"], 1)
                    hold(dve, s["rt_ready"], t + 1)
                    chain(v.reciprocal(fs[0:n, 2:3], fs[0:n, 1:2]))
                    v.scalar_tensor_tensor(x1[0:n, :], x1[0:n, :], fs[0:n, 2:3], fin[0:n, :], ALU.mult, ALU.mult)\
                        .then_inc(s["done"], 1)

                dve.wait_ge(s["init"], 1 + QS)
                v.memset(fs[:, :], 0.0).then_inc(s["sc_free"], 1)
                route(0)
                route(1)
                begin(0)
                pair(0, 0, 2)
                TILE = PPT * ROUTE + 3
                outer = chain.n
                with dve.Fori(0, NT - 1) as t:
                    with dve.Fori(1, PPT) as p:
                        chain.base, chain.n = t * TILE + p * ROUTE + (outer - ROUTE), 0
                        pair(t * GPT + p * 2, t * P + p * TOPK, t * PH + p + 2)
                        assert chain.n == ROUTE
                    chain.base, chain.n = t * TILE + outer + (PPT - 1) * ROUTE, 0
                    begin(t + 1)
                    pair(t * GPT + GPT, t * P + P, t * PH + (PH + 2))
                    hold(dve, s["small_in"], 16 * (B + 2))
                    hold(dve, s["y_out"], t + 1)
                    finish(t, P, y[:, :], gate2[:, :])
                    assert chain.n == ROUTE + 3, chain.n
                base = outer + (NT - 1) * TILE
                last_tile = (NT - 1) * P
                with dve.Fori(1, 3) as p:
                    chain.base, chain.n = p * (2 * ROUTE) + (base - 2 * ROUTE), 0
                    pair(p * 2 + (NT - 1) * GPT, p * TOPK + last_tile, p * 2 + ((NT - 1) * PH + 1), two=True)
                base += 4 * ROUTE
                chain.base, chain.n = base, 0
                pair((NT - 1) * GPT + 6, last_tile + 3 * TOPK, NT * PH - 1)
                base += ROUTE
                with dve.Fori(4, PPT) as p:
                    chain.base, chain.n = p * (2 * ROUTE) + (base - 8 * ROUTE), 0
                    pair(p * 2 + (NT - 1) * GPT, p * TOPK + last_tile, p * 2 + (NT * PH - 8), two=True)
                chain.base, chain.n = base + 8 * ROUTE, 0
                dve.wait_ge(s["hs_in"], 16 * QS)
                for i in range(SG):
                    dve.wait_ge(spread_in[i], 2 * 16 * QS)
                    group(NG + i, i % 2, gate_s[:, i * NB:(i + 1) * NB])
                    if i == 1:
                        dve.wait_ge(s["y_out"], NT)
                        finish(NT - 1, P, y[:, :], gate2[:, :])
                dve.wait_ge(s["folded"], 2)
                finish(NT, NS, ps_h[0:NS, :, :].rearrange("p a b -> p (a b)"), gate2_s[:, :])

            @block.tensor
            def _(pe):
                e = K["ident"]

                def rows_t(t):
                    hold(pe, s["hn_in"], t * 16 + 16)
                    for kc in range(KC):
                        last = nc.tensor.transpose(ps_h[:, kc, :], h_next[:, kc * P:(kc + 1) * P], e[:, :])
                    last.then_inc(s["hT_full"], 1)
                    hold(pe, s["hT_out"], t + 1)

                def head(H, h, first=False):
                    for kc in range(KC):
                        mm = nc.tensor.matmul(ps_r[:, 0, 0:256], hT[:, kc, :], wq[:, kc, bass.ds(h * 256, 256)],
                                              start=(kc == 0), stop=(kc == KC - 1))
                    mm.then_inc(s["q_full"], 1)
                    hold(pe, s["q_out"], H + 1)
                    for k in range(2):
                        last = nc.tensor.transpose(ps_r[:, 1, k * P:(k + 1) * P], q[:, k, :], e[:, :])
                    last.then_inc(s["qt_full"], 1)
                    hold(pe, s["qt_out"], H + 1)
                    if not first:
                        hold(pe, s["sc_out"], H)
                    for k in range(2):
                        mm = nc.tensor.matmul(ps_r[:, 2, k * PK:(k + 1) * PK], qT[:, k, :], subT[:, k, :], start=True, stop=True)
                    mm.then_inc(s["sc_full"], 1)

                def group(i, par, first=False):
                    for j in range(NB):
                        hold(pe, s["diag_ready"], i * NB + (j + 1))
                        hold(pe, v_in[j], i * 16 + 16)
                        for c in range(2):
                            mm = nc.tensor.matmul(ps_y[:, c * 512:(c + 1) * 512], diag[:, par, j, :],
                                                  v_rows[:, j, c * 512:(c + 1) * 512], start=(first and j == 0), stop=False,
                                                  skip_group_check=True)
                        mm.then_inc(s["v_used"], 1)

                def pair(i, H, h, two=False, first=False, new_tile=None):
                    head(H, h)
                    if new_tile is not None:
                        hold(pe, s["y_out"], new_tile)
                    group(i, 0, first)
                    if two:
                        head(H + 1, h + 1)
                    group(i + 1, 1)

                pe.wait_ge(s["sub_in"], 16)
                for k in range(2):
                    last = nc.tensor.transpose(ps_r[:, 1, k * PK:(k + 1) * PK], sub[:, k, :], e[:, :])
                last.then_inc(s["subT_full"], 1)
                pe.wait_ge(s["subT_out"], 1)
                rows_t(0)
                pe.wait_ge(wq_in[0], 16)
                head(0, 0, True)
                head(1, 1)
                for landed in wq_in[1:]:
                    pe.wait_ge(landed, 16)
                pair(0, 2, 2, first=True)
                with pe.Fori(0, NT - 1) as t:
                    with pe.Fori(1, PPT - 2) as p:
                        pair(t * GPT + p * 2, t * PH + p + 2, p + 2)
                    rows_t(t + 1)
                    with pe.Fori(PPT - 2, PPT) as p:
                        pair(t * GPT + p * 2, t * PH + p + 2, p + (2 - PPT))
                    pair(t * GPT + GPT, t * PH + (PH + 2), 2, first=True, new_tile=t + 1)
                with pe.Fori(1, 3) as p:
                    pair(p * 2 + (NT - 1) * GPT, p * 2 + ((NT - 1) * PH + 1), p * 2 + 1, two=True)
                pair((NT - 1) * GPT + 6, NT * PH - 1, PH - 1)
                rows_t(NT)
                with pe.Fori(4, PPT) as p:
                    pair(p * 2 + (NT - 1) * GPT, p * 2 + (NT * PH - 8), p * 2 - 8, two=True)
                pe.wait_ge(s["y_out"], NT)
                for i in range(SG):
                    group(NG + i, i % 2, i == 0)
                pe.wait_ge(s["y_out"], NT + 1)
                for c in range(2):
                    nc.tensor.matmul(ps_h[0:NS, 4 * c:4 * c + 4, :], fold[:, :], y[:, c * 512:(c + 1) * 512],
                                     start=True, stop=True).then_inc(s["folded"], 1)


def trunk_step(nc, I, O):
    mod = nc.dram_tensor("mod_rows", (NC, 6 * D), F32, kind="Internal").ap()
    x1_dram = nc.dram_tensor("x1_rows", (SEQ + P, D), F32, kind="Internal").ap()
    with ExitStack() as ctx:
        def const(name, shape, dt=F32):
            return ctx.enter_context(nc.sbuf_tensor(name, shape, dt))

        K = {"ident": const("ident", [P, P]), "ones": const("ones", [P, P]), "iota16": const("iota16", [P, TOPK], I32)}
        with ExitStack() as mix:
            def mconst(name, shape):
                return mix.enter_context(nc.sbuf_tensor(name, shape, F32))

            K.update(tri=mconst("tri", [P, P]), mask=mconst("mask", [P, P]), last=mconst("last", [P, P]),
                     tri_s=mconst("tri_s", [NS, NS]), mask_s=mconst("mask_s", [NS, NS]), last_s=mconst("last_s", [NS, NS]),
                     same=mconst("same", [NS, B]), s_bias=mconst("s_bias", [P, WIN + NS]), bias=mconst("swa_bias", [P, AH, 2 * P]),
                     live_bias=mconst("swa_live_bias", [P, AH, 2 * P]))
            w_in = mix.enter_context(nc.sbuf_tensor("w_in", [P, KC, INW], F32))
            s = {n: nc.alloc_semaphore("mix_" + n) for n in SIGNALS}
            s["w_in_in"] = nc.alloc_semaphore("mix_w_in_in")
            modulation_rows(nc, I, mod, w_in, s["w_in_in"], K)
            X = Mixer(nc, mix, w_in)
            mix_prompt(nc, I, O, mod, x1_dram, X, K, s)
            s2 = {n: nc.alloc_semaphore("smp_" + n) for n in SIGNALS + EXTRA if n != "w_out_in"}
            s2["w_out_in"] = s["w_out_in"]
            mix_sample(nc, I, O, mod, x1_dram, X, K, s2)
        del s2["w_out_in"]
        nc.clear_and_free_semaphores([*s.values(), *s2.values()])
        nc.all_engine_barrier()
        h2_dram = nc.dram_tensor("h2_rows", (SEQ + P, D), F32, kind="Internal").ap()
        wq = ctx.enter_context(nc.sbuf_tensor("wq", [P, KC, PH * 2 * P], F32))
        wq_in = [ctx.enter_context(nc.semaphore(f"wq_in{i}")) for i in range(PH // 2)]
        second_norm(nc, I, mod, x1_dram, h2_dram, wq, wq_in, K)
        experts(nc, I, O, mod, x1_dram, h2_dram, wq, wq_in, K)


_OUTS = [("y_p", (1, SEQ, D)), ("y_s", (B, TS, D)),
         ("swa_k_p", (1, 1, WIN, KVH, AD)), ("swa_v_p", (1, 1, WIN, KVH, AD)), ("conv_p", (1, 1, CK - 1, CW)),
         ("C_p", (1, 1, MH, DH, DH)), ("n_p", (1, 1, MH, DH)), ("m_p", (1, 1, MH)),
         ("swa_k_s", (1, B, WIN, KVH, AD)), ("swa_v_s", (1, B, WIN, KVH, AD)), ("conv_s", (1, B, CK - 1, CW)),
         ("C_s", (1, B, MH, DH, DH)), ("n_s", (1, B, MH, DH)), ("m_s", (1, B, MH))]


def kernel(**inputs):
    import numpy as _np
    import concourse.bacc as _bacc
    from concourse import mybir as _mybir
    from concourse.bass_utils import run_bass_kernel_spmd as _run

    nc = _bacc.Bacc("TRN2", target_bir_lowering=False, num_devices=1)
    arrays, ins, outs = {}, {}, {}
    for name, a in inputs.items():
        a = _np.ascontiguousarray(a)
        arrays[f"in_{name}_dram"] = a
        ins[name] = nc.dram_tensor(f"in_{name}_dram", a.shape, _mybir.dt.from_np(a.dtype), kind="ExternalInput").ap()
    for name, shape in _OUTS:
        outs[name] = nc.dram_tensor(f"out_{name}_dram", shape, F32, kind="ExternalOutput").ap()
    trunk_step(nc, ins, outs)
    r = _run(nc, [arrays], core_ids=[0])
    return tuple(r.results[0][f"out_{name}_dram"] for name, _ in _OUTS)
```

```python
from contextlib import ExitStack

import concourse.bass as bass
from concourse import mybir

F32 = mybir.dt.float32
U32 = mybir.dt.uint32
I32 = mybir.dt.int32
ALU = mybir.AluOpType
ACT = mybir.ActivationFunctionType
AX = mybir.AxisListType.X

P = 128
D = 1024
KC = D // P
SEQ = 512
NT = SEQ // P
B = 8
TS = 4
NS = B * TS
NC = 1 + B
MH, DH = 4, 128
MW = MH * DH
AH, KVH, AD = 4, 2, 64
WIN = 128
CW, CK = 256, 3
INW = 3336
EPS = 1e-6
NEG = -1e30
KSCALE = DH ** -0.5
SLOPES = [2.0 ** (-8.0 * (h + 1) / AH) for h in range(AH)]
W_IN_LOADS = 6
W_IN_LATE = 2
PH, PK, TOPK, NEXP = 8, 128, 16, 16384

GATES, QZ, KZ, VZ, SVCB, CCCH, OZ = range(7)
CHUNKS = [(2048, 2440), (0, 512), (512, 1024), (1024, 1536), (2440, 2824), (2824, 3336), (1536, 2048)]


def hold(eng, sem, value):
    eng.wait_ge(sem, value)
    if not isinstance(value, int):
        eng.nop(nofuse=True)


class Chain:

    def __init__(self, eng, sem):
        self.eng, self.sem, self.base, self.n = eng, sem, 0, 0

    def __call__(self, ins):
        ins.then_inc(self.sem, 1)
        self.n += 1
        hold(self.eng, self.sem, self.base + self.n)

    def enter(self, t, per):
        self.start, self.per = self.base + self.n, per
        self.base, self.n = t * per + self.start, 0

    def leave(self, trips):
        assert self.n == self.per, (self.n, self.per)
        self.base, self.n = self.start + trips * self.per, 0


def repeat_last(ap, n):
    return ap.unsqueeze(len(ap.shape)).broadcast_to([*ap.shape, n])


def for_tokens(ap):
    return ap.unsqueeze(1).broadcast_to([B, TS, ap.shape[1]])


def repeat_mid(ap, n):
    return ap.unsqueeze(1).broadcast_to([ap.shape[0], n, *ap.shape[1:]])


class ConstantBuffers:

    def __init__(self, nc, ctx):
        def sb(name, shape, dt=F32):
            return ctx.enter_context(nc.sbuf_tensor(name, shape, dt))

        def sem(name):
            return ctx.enter_context(nc.semaphore(name))

        self.ident_ready, self.cleared, self.dist_ready = sem("const_ident"), sem("const_cleared"), sem("const_dist")
        self.bias_ready, self.sdist_ready, self.s_step = sem("const_bias"), sem("const_sdist"), sem("const_s_step")
        self.dist_i, self.dist = sb("dist_i", [P, 2 * P], I32), sb("dist", [P, 2 * P])
        self.sdist_i, self.sdist = sb("sdist_i", [P, WIN + NS], I32), sb("sdist", [P, WIN + NS])
        self.tpat_i, self.tpat = sb("tpat_i", [P, P], I32), sb("tpat", [P, P])
        self.cols = sb("row_cols", [P, 2])
        self.beyond = sb("beyond", [P, WIN + NS])


def constants_dve(nc, dve, K, C):
    v = nc.vector
    for h in range(AH):
        v.memset(C.cols[h * NS:(h + 1) * NS, 1:2], -SLOPES[h])
    dve.wait_ge(C.sdist_ready, 1)
    v.tensor_tensor(C.tpat[:, :], C.tpat[:, :], K["ident"][:, :], ALU.mult).then_inc(C.s_step, 1)
    dve.wait_ge(C.s_step, 1)
    v.tensor_reduce(C.cols[:, 0:1], C.tpat[:, :], AX, ALU.add).then_inc(C.s_step, 1)
    dve.wait_ge(C.s_step, 2)
    v.tensor_scalar(K["s_bias"][:, :], C.sdist[:, :], C.cols[:, 0:1], C.cols[:, 1:2], ALU.add, ALU.mult)
    v.tensor_scalar(C.beyond[:, :], C.sdist[:, :], C.cols[:, 0:1], float(WIN), ALU.add, ALU.is_gt).then_inc(C.s_step, 1)
    dve.wait_ge(C.s_step, 3)
    v.scalar_tensor_tensor(K["s_bias"][:, :], C.beyond[:, :], NEG, K["s_bias"][:, :], ALU.mult, ALU.add)\
        .then_inc(C.s_step, 1)
    dve.wait_ge(C.dist_ready, 1)
    for h in range(AH):
        last = v.tensor_copy(C.tpat[h * NS:(h + 1) * NS, 0:NS], K["mask_s"][:, :])
    last.then_inc(C.s_step, 1)
    dve.wait_ge(C.s_step, 5)
    v.tensor_tensor(K["s_bias"][:, WIN:], K["s_bias"][:, WIN:], C.tpat[:, 0:NS], ALU.add)


def constants_pool(nc, pool, K, C):
    g = nc.gpsimd
    g.memset(K["ident"][:, :], 0.0).then_inc(C.ident_ready, 1)
    pool.wait_ge(C.ident_ready, 1)
    g.affine_select(out=K["ident"][:, :], in_=K["ident"][:, :], compare_op=ALU.not_equal, fill=1.0, base=0,
                    pattern=[[-1, P]], channel_multiplier=1).then_inc(C.ident_ready, 1)
    g.iota(C.sdist_i[:, 0:WIN], pattern=[[-1, WIN]], base=WIN, channel_multiplier=0)
    g.iota(C.sdist_i[:, WIN:].rearrange("p (b i) -> p b i", i=TS), pattern=[[0, B], [-1, TS]], base=0, channel_multiplier=0)
    g.iota(C.tpat_i[:, :].rearrange("p (a i) -> p a i", i=TS), pattern=[[0, P // TS], [1, TS]], base=0,
           channel_multiplier=0)
    zero = [K["tri"], K["mask"], K["last"], K["tri_s"], K["mask_s"], K["last_s"], K["same"]]
    for m in zero:
        g.memset(m[:], 0.0)
    g.memset(K["ones"][:], 1.0)
    g.memset(K["live_bias"][:, :, 0:P], NEG)
    g.iota(C.dist_i[:, :], pattern=[[-1, 2 * P]], base=P, channel_multiplier=1)
    g.iota(K["iota16"][:, :], pattern=[[1, TOPK]], base=0, channel_multiplier=0).then_inc(C.cleared, 1)
    pool.wait_ge(C.cleared, 1)

    def fill(m, pattern, op, value, base, per_row):
        return g.affine_select(out=m, in_=m, compare_op=op, fill=value, base=base,
                               pattern=pattern, channel_multiplier=per_row)

    def blocks(m):
        return m.rearrange("p (b i) -> p b i", i=TS)

    fill(K["tri"][:, :], [[-1, P]], ALU.is_gt, 1.0, 0, 1)
    fill(K["mask"][:, :], [[-1, P]], ALU.is_ge, NEG, 0, 1)
    fill(K["last"][:, :], [[0, P]], ALU.not_equal, 1.0, -(P - 1), 1)
    fill(blocks(K["mask_s"][:, :]), [[-TS, B], [-1, TS]], ALU.is_ge, NEG, 0, 1)
    fill(K["tri_s"][:, :], [[-1, NS]], ALU.is_gt, 1.0, 0, 1)
    fill(blocks(K["last_s"][:, :]), [[-TS, B], [0, TS]], ALU.not_equal, 1.0, -(TS - 1), 1)
    fill(K["same"][:, :], [[TS, B]], ALU.is_gt, 1.0, 0, -1).then_inc(C.cleared, 1)
    pool.wait_ge(C.cleared, 2)
    fill(blocks(K["mask_s"][:, :]), [[TS, B], [0, TS]], ALU.is_ge, NEG, TS - 1, -1)
    fill(blocks(K["tri_s"][:, :]), [[-TS, B], [0, TS]], ALU.is_ge, 0.0, 0, 1)
    fill(K["same"][:, :], [[TS, B]], ALU.is_ge, 0.0, TS - 1, -1)
    g.tensor_copy(C.sdist[:, :], C.sdist_i[:, :])
    g.tensor_copy(C.tpat[:, :], C.tpat_i[:, :]).then_inc(C.sdist_ready, 1)
    g.tensor_copy(C.dist[:, :], C.dist_i[:, :]).then_inc(C.dist_ready, 1)
    pool.wait_ge(C.dist_ready, 1)
    for h in range(AH):
        g.tensor_scalar(K["bias"][:, h, :], C.dist[:, :], -SLOPES[h], None, ALU.mult).then_inc(C.bias_ready, 1)
    pool.wait_ge(C.bias_ready, AH)
    fill(K["bias"][:, :, :], [[0, AH], [1, 2 * P]], ALU.is_ge, NEG, 0, -1).then_inc(C.bias_ready, 1)
    pool.wait_ge(C.bias_ready, AH + 1)
    fill(K["bias"][:, :, :], [[0, AH], [-1, 2 * P]], ALU.is_ge, NEG, P, 1).then_inc(C.bias_ready, 1)
    pool.wait_ge(C.bias_ready, AH + 2)
    g.tensor_copy(K["live_bias"][:, :, P:2 * P], K["bias"][:, :, P:2 * P])


def modulation_rows(nc, I, mod, w_in, w_in_in, K):
    NCH = 6 * D // 512
    RING = 3
    with ExitStack() as ctx:
        def sb(name, shape, dt=F32):
            return ctx.enter_context(nc.sbuf_tensor(name, shape, dt))

        def sem(name):
            return ctx.enter_context(nc.semaphore(name))

        c_rows = sb("c_rows", [NC, D])
        c_sig = sb("c_sig", [NC, D])
        cT = sb("cT", [P, KC, NC])
        w = sb("ada_ring", [P, RING, KC, 512])
        bias = sb("ada_bias", [NC, RING, 512])
        row = sb("ada_row", [NC, RING, 512])
        ps_t = ctx.enter_context(nc.psum_tensor("ada_ps_t", [P, KC, NC], F32))
        ps = [ctx.enter_context(nc.psum_tensor(f"ada_ps{i}", [NC, 512], F32)) for i in range(RING)]
        c_in, c_silu, c_sgm, ct_ps, ct_ready = sem("c_in"), sem("c_silu"), sem("c_sgm"), sem("ct_ps"), sem("ct_ready")
        ring_in = [sem(f"ada_w_in{i}") for i in range(RING)]
        row_ps, row_ready = sem("ada_row_ps"), sem("ada_row_ready")
        row_out = [sem(f"ada_row_out{i}") for i in range(RING)]
        ada = I["ada_w"][0].rearrange("(kc p) n -> p kc n", p=P)
        w_in_dram = I["w_in"][0].rearrange("(kc p) n -> p kc n", p=P)
        C = ConstantBuffers(nc, ctx)
        block = ctx.enter_context(nc.Block())

        @block.sync
        def _(sp):
            sp.dma_start(c_rows[0:1, :], I["c_prompt"]).then_inc(c_in, 16)
            sp.dma_start(c_rows[1:NC, :], I["c_sample"]).then_inc(c_in, 16)

            def load(c, i, first=False):
                if not first:
                    hold(sp, row_ready, c - RING + 1)
                cols = bass.ds(c * 512, 512)
                sp.dma_start(w[:, i, :, :], ada[:, :, cols]).then_inc(ring_in[i], 16)
                sp.dma_start(bias[:, i, :], I["ada_b"][0, cols].partition_broadcast(NC)).then_inc(ring_in[i], 16)

            per = 1
            for i in range(RING):
                load(i, i, first=True)
            sp.dma_start(w_in[:, 0:per, :], w_in_dram[:, 0:per, :]).then_inc(w_in_in, 16)
            with sp.Fori(1, NCH // RING) as r:
                for i in range(RING):
                    load(r * RING + i, i)
                blocks = bass.ds(r * per, per)
                sp.dma_start(w_in[:, blocks, :], w_in_dram[:, blocks, :]).then_inc(w_in_in, 16)
            rest = slice(NCH // RING * per, KC - W_IN_LATE)
            sp.dma_start(w_in[:, rest, :], w_in_dram[:, rest, :]).then_inc(w_in_in, 16)

        @block.gpsimd
        def _(pool):
            constants_pool(nc, pool, K, C)

        @block.scalar
        def _(act):
            act.wait_ge(c_in, 32)
            nc.scalar.activation(c_sig[:, :], c_rows[:, :], ACT.Sigmoid).then_inc(c_sgm, 1)
            def store(c, i):
                hold(act, row_ready, c + 1)
                act.dma_start(mod[:, bass.ds(c * 512, 512)], row[:, i, :]).then_inc(row_out[i], 16)

            with act.Fori(0, NCH // RING) as r:
                for i in range(RING):
                    store(r * RING + i, i)
            for i in range(RING):
                act.wait_ge(row_out[i], 16 * (NCH // RING))

        @block.vector
        def _(dve):
            dve.wait_ge(c_sgm, 1)
            nc.vector.tensor_tensor(c_rows[:, :], c_rows[:, :], c_sig[:, :], ALU.mult).then_inc(c_silu, 1)
            dve.wait_ge(ct_ps, 1)
            nc.vector.tensor_copy(cT[:, :, :], ps_t[:, :, :]).then_inc(ct_ready, 1)
            constants_dve(nc, dve, K, C)

            def add_bias(c, r, i, first=False):
                hold(dve, ring_in[i], r * 32 + 32)
                if not first:
                    hold(dve, row_out[i], r * 16)
                hold(dve, row_ps, c + 1)
                nc.vector.tensor_tensor(row[:, i, :], ps[i][:, :], bias[:, i, :], ALU.add).then_inc(row_ready, 1)

            for i in range(RING):
                add_bias(i, 0, i, first=True)
            with dve.Fori(1, NCH // RING) as r:
                for i in range(RING):
                    add_bias(r * RING + i, r, i)

        @block.tensor
        def _(pe):
            pe.wait_ge(c_silu, 1)
            pe.wait_ge(C.ident_ready, 2)
            for kc in range(KC):
                last = nc.tensor.transpose(ps_t[:, kc, :], c_rows[:, kc * P:(kc + 1) * P], K["ident"][0:NC, 0:NC])
            last.then_inc(ct_ps, 1)
            pe.wait_ge(ct_ready, 1)

            def product(c, r, i, first=False):
                hold(pe, ring_in[i], r * 32 + 32)
                if not first:
                    hold(pe, row_ready, c - RING + 1)
                for kc in range(KC):
                    mm = nc.tensor.matmul(ps[i][:, :], cT[:, kc, :], w[:, i, kc, :], start=(kc == 0), stop=(kc == KC - 1))
                mm.then_inc(row_ps, 1)

            for i in range(RING):
                product(i, 0, i, first=True)
            with pe.Fori(1, NCH // RING) as r:
                for i in range(RING):
                    product(r * RING + i, r, i)


class Mixer:

    def __init__(self, nc, ctx, w_in):
        def sb(name, shape, dt=F32):
            return ctx.enter_context(nc.sbuf_tensor(name, shape, dt))

        def ps(name, shape):
            return ctx.enter_context(nc.psum_tensor(name, shape, F32))

        self.w_in = w_in
        self.w_out = sb("w_out", [P, KC, D])
        self.row_a, self.row_s, self.row_g = sb("mod_scale", [P, D]), sb("mod_shift", [P, D]), sb("mod_gate", [P, D])
        self.xt = sb("xt", [P, D])
        self.h = sb("h", [P, D])
        self.hT = sb("hT", [P, KC, P])
        self.g5 = sb("z_gates_sq_sk", [P, 392])
        self.qz, self.kz = sb("z_q", [P, MW]), sb("z_k", [P, MW])
        self.vz = sb("z_v", [P, MH, DH])
        self.g6, self.g7 = sb("z_sv_cb", [P, 384]), sb("z_cc_ch", [P, 512])
        self.oz = sb("z_o", [P, MW])
        self.stat = sb("mix_stat", [P, 4])
        self.eps = sb("eps", [P, 1])
        self.gb, self.mg, self.sink = sb("gate_b", [P, 2 * MH]), sb("mlstm_g", [P, MW]), sb("sinks", [P, AH])
        self.pre, self.absf = sb("gate_pre", [P, 8]), sb("gate_abs", [P, MH])
        self.lg, self.lf = sb("gate_log", [P, MH]), sb("gate_lf", [P, MH])
        self.mb = sb("mm_b", [P, 8])
        self.w, self.rowmax = sb("gate_w", [P, MH]), sb("d_max", [P, MH])
        self.mprev, self.nmm, self.mt = sb("m_prev", [P, MH]), sb("neg_mm", [P, MH]), sb("m_t", [P, MH])
        self.earg, self.eval = sb("exp_arg", [P, 8]), sb("exp_val", [P, 8])
        self.dm = sb("d_matrix", [P, MH, P])
        self.diag = sb("diag_w", [P, MH, P])
        self.qk = sb("qT_kT", [P, 2, MH, P])
        self.qT, self.kT = self.qk[:, 0], self.qk[:, 1]
        self.mixT = self.qk[:, :, :, :].rearrange("p a h t -> p (a h) t")
        self.pT = sb("pT", [P, MH, P])
        self.den, self.rden = sb("den", [P, 8]), sb("rden", [P, MH])
        self.ss2, self.r2 = sb("ss2", [P, MH]), sb("r2", [P, MH])
        self.lastv, self.larg, self.lval = sb("last_mm_b", [P, 8]), sb("last_arg", [P, 8]), sb("last_val", [P, 8])
        self.CT, self.nT = sb("CT", [P, MH, DH]), sb("nT", [P, MH])
        self.sqT, self.skT = sb("sqT", [P, 2, P]), sb("skT", [P, 2 * P])
        self.sv_prev = sb("sv_prev", [P, KVH * AD])
        self.sc = sb("swa_scores", [P, AH, 2 * P])
        self.nsq = self.dm
        self.xr = self.sc[:, :, :].rearrange("p h k -> p (h k)")
        self.smx, self.ssum, self.ses = sb("swa_max", [P, 2 * AH]), sb("swa_sum", [P, AH]), sb("swa_sink", [P, AH])
        self.ps_t, self.ps_m = ps("ps_t", [P, 4, P]), ps("ps_m", [P, 512])
        self.ps_z = [ps("ps_z0", [P, 512]), ps("ps_z1", [P, 512])]
        self.ps_s = ps("ps_s", [P, 2, 512])
        self.ps_n = [ps("ps_n0", [P, 512]), ps("ps_n1", [P, 512])]
        self.u = self.g7[:, 0:CW]
        self.uT = sb("conv_uT", [P, 2, P + CK - 1])
        self.cbT = self.pT[:, 2:4]
        self.cT_out = self.hT[:, 0:4, :]
        self.cw = sb("conv_taps", [P, CK, 2])


TB = 11
T_H0, T_H1, T_SWA, T_Q, T_K, T_P, T_A0, T_A1, T_CONV, T_OA, T_HM = range(TB)
SIGNALS = ("w_out_in small_in rows_in rows_ready init x_in xr_in ss_ready h_ready t_full t_free zfull0 zfull1 zfree0 zfree1 "
           "gate_abs_ready lg_ready lf_ready b_full diag_ready wb_full d_ready expw_ready "
           "s_full p_ready num_full inter_ready numf_ready ss2_ready hm_ready larg_ready lval_ready vw_ready "
           "upd_full state_ready swa_full sc_ready swa_exp pv_full oa_ready u_ready yc_ready og_ready "
           "o_full x1_ready x1_stored state_out pool_done act_step dve_step").split()


class Tile:

    def __init__(self, nc, X, s, t, rows, tri, mask, last):
        self.nc, self.X, self.s, self.t, self.n = nc, X, s, t, rows
        self.tri, self.mask, self.last = tri, mask, last

    def on(self, eng, name, per=1, k=None):
        hold(eng, self.s[name], self.t * per + (per if k is None else k))

    def z_landed(self, eng, i):
        self.on(eng, f"zfull{i % 2}", 4 - i % 2, i // 2 + 1)

    def z_out(self, eng, i):
        self.on(eng, f"zfree{i % 2}", 4 - i % 2, i // 2 + 1)

    def t_landed(self, eng, k):
        self.on(eng, "t_full", self.per_t, k + 1)

    def t_out(self, eng, k):
        self.on(eng, "t_free", self.per_t, k + 1)

    def batch(self, pe, k, blocks, ident):
        if k:
            self.t_out(pe, k - 1)
        for j, (src, rows, cols) in enumerate(blocks):
            last = self.nc.tensor.transpose(self.X.ps_t[0:cols, j, 0:rows], src, ident[0:rows, 0:rows])
        last.then_inc(self.s["t_full"], 1)

    def chunk(self, pe, i):
        a, b = CHUNKS[i]
        X, n = self.X, self.n
        if i >= 2:
            self.z_out(pe, i - 2)
        for kc in range(KC):
            mm = self.nc.tensor.matmul(X.ps_z[i % 2][0:n, 0:b - a], X.hT[:, kc, 0:n], X.w_in[:, kc, a:b],
                                       start=(kc == 0), stop=(kc == KC - 1))
        mm.then_inc(self.s[f"zfull{i % 2}"], 1)

    def transpose_rows(self, pe, K):
        X, n, e = self.X, self.n, K["ident"]
        self.on(pe, "h_ready")
        self.batch(pe, T_H0, [(X.h[0:n, j * P:(j + 1) * P], n, P) for j in range(4)], e)
        self.batch(pe, T_H1, [(X.h[0:n, j * P:(j + 1) * P], n, P) for j in range(4, 8)], e)

    def project(self, pe, K):
        nc, X, s, n, e = self.nc, self.X, self.s, self.n, K["ident"]
        self.t_out(pe, T_H1)
        self.chunk(pe, GATES)
        self.chunk(pe, QZ)
        self.z_out(pe, GATES)
        self.batch(pe, T_SWA, [(X.g5[0:n, 8 + j * P:8 + (j + 1) * P], n, P) for j in range(3)], e)
        self.chunk(pe, KZ)
        self.on(pe, "lf_ready")
        nc.tensor.matmul(X.ps_m[0:n, 0:4], self.tri, X.lf[0:n, :], start=True, stop=True).then_inc(s["b_full"], 1)
        self.chunk(pe, VZ)
        self.z_out(pe, QZ)
        self.batch(pe, T_Q, [(X.qz[0:n, h * DH:(h + 1) * DH], n, DH) for h in range(MH)], e)
        self.on(pe, "diag_ready")
        for h in range(MH):
            mm = nc.tensor.matmul(X.ps_s[0:n, 1, h * P:h * P + n], K["ones"][0:n, 0:n], X.diag[0:n, h, 0:n],
                                  start=True, stop=True)
        mm.then_inc(s["wb_full"], 1)
        self.chunk(pe, SVCB)
        self.z_out(pe, KZ)
        self.batch(pe, T_K, [(X.kz[0:n, h * DH:(h + 1) * DH], n, DH) for h in range(MH)], e)
        self.chunk(pe, CCCH)
        self.t_out(pe, T_K)
        for h in range(MH):
            mm = nc.tensor.matmul(X.ps_s[0:n, 0, h * P:h * P + n], X.qT[:, h, 0:n], X.kT[:, h, 0:n],
                                  start=True, stop=True)
        mm.then_inc(s["s_full"], 1)

    def transpose_weights(self, pe, K):
        X, n = self.X, self.n
        self.on(pe, "p_ready")
        self.batch(pe, T_P, [(X.dm[0:n, h, 0:n], n, n) for h in range(MH)], K["ident"])
        self.chunk(pe, OZ)

    def intra(self, pe, K):
        nc, X, s, n = self.nc, self.X, self.s, self.n
        self.t_out(pe, T_P)
        self.z_out(pe, VZ)
        nc.tensor.matmul(X.ps_m[0:n, 16:24], self.last, X.mb[0:n, :], start=True, stop=True)
        for h in range(MH):
            nc.tensor.matmul(X.ps_n[0][0:n, h * DH:(h + 1) * DH], X.pT[0:n, h, 0:n], X.vz[0:n, h, :],
                             start=True, stop=True)
            mm = nc.tensor.matmul(X.ps_m[0:n, 12 + h:13 + h], X.pT[0:n, h, 0:n], K["ones"][0:n, 0:1],
                                  start=True, stop=True)
        mm.then_inc(s["num_full"], 1)

    def out_product(self, pe, oa_out, hm_out, halfway=None):
        nc, X, s, n = self.nc, self.X, self.s, self.n
        pe.wait_ge(s["w_out_in"], 32)
        self.z_out(pe, CCCH)
        self.z_out(pe, OZ)
        oa_out(pe)
        order = (4, 5, 0, 1, 2, 3, 6, 7)
        for c in range(2):
            for i, kc in enumerate(order):
                if c == 0 and kc == 0:
                    hm_out(pe)
                if c == 0 and kc == 6:
                    self.on(pe, "yc_ready")
                mm = nc.tensor.matmul(X.ps_z[c][0:n, :], X.mixT[:, kc, 0:n], X.w_out[:, kc, c * 512:(c + 1) * 512],
                                      start=(i == 0), stop=(i == KC - 1))
            if c == 0 and halfway:
                halfway(pe)
        mm.then_inc(s["o_full"], 1)

    def act_rms(self, act, chain):
        nc, X, s, n = self.nc, self.X, self.s, self.n
        a = nc.scalar.activation
        self.on(act, "x_in", 16)
        chain(a(X.h[0:n, :], X.xt[0:n, :], ACT.Square, accum_out=X.stat[0:n, 0:1]))
        a(X.stat[0:n, 1:2], X.stat[0:n, 0:1], ACT.Sqrt, scale=1.0 / D, bias=X.eps[0:n, :]).then_inc(s["ss_ready"], 1)

    def act_front(self, act, chain):
        nc, X, s, n = self.nc, self.X, self.s, self.n
        a = nc.scalar.activation
        self.t_landed(act, T_H0)
        a(X.hT[:, 0:4, 0:n], X.ps_t[:, :, 0:n], ACT.Copy).then_inc(s["t_free"], 1)
        self.z_landed(act, QZ)
        a(X.qz[0:n, :], X.ps_z[QZ % 2][0:n, :], ACT.Copy).then_inc(s[f"zfree{QZ % 2}"], 1)
        self.on(act, "gate_abs_ready")
        chain(a(X.lg[0:n, :], X.absf[0:n, :], ACT.Exp, scale=-1.0))
        a(X.lg[0:n, :], X.lg[0:n, :], ACT.Ln, bias=1.0).then_inc(s["lg_ready"], 1)
        self.z_landed(act, KZ)
        a(X.kz[0:n, :], X.ps_z[KZ % 2][0:n, :], ACT.Copy, scale=KSCALE).then_inc(s[f"zfree{KZ % 2}"], 1)
        self.t_landed(act, T_Q)
        a(X.qT[:, :, 0:n], X.ps_t[:, :, 0:n], ACT.Copy).then_inc(s["t_free"], 1)
        self.on(act, "d_ready")
        for h in range(MH):
            a(X.dm[0:n, h, 0:n], X.dm[0:n, h, 0:n], ACT.Exp, bias=X.nmm[0:n, h:h + 1])
        a(X.eval[0:n, :], X.earg[0:n, :], ACT.Exp).then_inc(s["expw_ready"], 1)
        self.z_landed(act, SVCB)
        a(X.g6[0:n, :], X.ps_z[SVCB % 2][0:n, 0:384], ACT.Copy).then_inc(s[f"zfree{SVCB % 2}"], 1)
        self.t_landed(act, T_P)
        a(X.pT[0:n, :, 0:n], X.ps_t[0:n, :, 0:n], ACT.Copy).then_inc(s["t_free"], 1)

    def act_norm(self, act, chain, inter, landed, out, also=None):
        nc, X, s, n = self.nc, self.X, self.s, self.n
        a = nc.scalar.activation
        landed(act)
        for h in range(MH):
            last = a(X.h[0:n, h * DH:(h + 1) * DH], inter[:, h, :], ACT.Copy, scale=X.eval[0:n, h:h + 1])
        last.then_inc(s[out], 1)
        if also:
            also(act)
        self.on(act, "larg_ready")
        a(X.lval[0:n, :], X.larg[0:n, :], ACT.Exp).then_inc(s["lval_ready"], 1)
        self.z_landed(act, OZ)
        a(X.oz[0:n, :], X.ps_z[OZ % 2][0:n, :], ACT.Sigmoid).then_inc(s[f"zfree{OZ % 2}"], 1)
        self.on(act, "numf_ready")
        for h in range(MH):
            last = a(X.nsq[0:n, h, :], X.h[0:n, h * DH:(h + 1) * DH], ACT.Square, scale=X.rden[0:n, h:h + 1],
                     accum_out=X.ss2[0:n, h:h + 1])
        chain(last)
        a(X.r2[0:n, :], X.ss2[0:n, :], ACT.Sqrt, scale=1.0 / DH, bias=X.eps[0:n, :]).then_inc(s["ss2_ready"], 1)

    def dve_rms(self, dve, chain):
        nc, X, s, n = self.nc, self.X, self.s, self.n
        v = nc.vector
        self.on(dve, "ss_ready")
        chain(v.reciprocal(X.stat[0:n, 2:3], X.stat[0:n, 1:2]))
        chain(v.scalar_tensor_tensor(X.h[0:n, :], X.xt[0:n, :], X.stat[0:n, 2:3], X.row_a[0:n, :], ALU.mult, ALU.mult))
        v.tensor_tensor(X.h[0:n, :], X.h[0:n, :], X.row_s[0:n, :], ALU.add).then_inc(s["h_ready"], 1)

    def dve_front(self, dve, chain, K):
        nc, X, s, n = self.nc, self.X, self.s, self.n
        v = nc.vector
        self.t_landed(dve, T_H1)
        v.tensor_copy(X.hT[:, 4:8, 0:n], X.ps_t[:, :, 0:n]).then_inc(s["t_free"], 1)
        self.z_landed(dve, GATES)
        zg = X.ps_z[GATES % 2][0:n, :]
        v.tensor_copy(X.g5[0:n, 0:8], zg[:, 0:8])
        v.tensor_copy(X.g5[0:n, 264:392], zg[:, 264:392])
        v.tensor_copy(X.g5[0:n, 8:264].rearrange("p (g kv d) -> p g kv d", g=2, kv=KVH),
                      zg[:, 8:264].rearrange("p (kv g d) -> p g kv d", kv=KVH, g=2)).then_inc(s[f"zfree{GATES % 2}"], 1)
        self.z_out(dve, GATES)
        chain(v.tensor_tensor(X.pre[0:n, :], X.g5[0:n, 0:8], X.gb[0:n, :], ALU.add))
        v.scalar_tensor_tensor(X.absf[0:n, :], X.pre[0:n, 4:8], -1.0, X.pre[0:n, 4:8], ALU.mult, ALU.max).then_inc(s["gate_abs_ready"], 1)
        self.t_landed(dve, T_SWA)
        v.tensor_copy(X.sqT[:, :, 0:n], X.ps_t[:, 0:2, 0:n])
        v.tensor_copy(X.skT[:, P:P + n], X.ps_t[:, 2, 0:n]).then_inc(s["t_free"], 1)
        self.on(dve, "lg_ready")
        v.scalar_tensor_tensor(X.lf[0:n, :], X.pre[0:n, 4:8], 0.0, X.lg[0:n, :], ALU.min, ALU.subtract)\
            .then_inc(s["lf_ready"], 1)
        self.z_landed(dve, VZ)
        v.tensor_copy(X.vz[0:n, :, :], X.ps_z[VZ % 2][0:n, :].rearrange("p (h d) -> p h d", h=MH))\
            .then_inc(s[f"zfree{VZ % 2}"], 1)
        self.on(dve, "b_full")
        v.tensor_copy(X.mb[0:n, 4:8], X.ps_m[0:n, 0:4])
        chain(v.tensor_tensor(X.w[0:n, :], X.pre[0:n, 0:4], X.ps_m[0:n, 0:4], ALU.subtract))
        v.tensor_tensor(X.diag[0:n, :, 0:n], repeat_mid(K["ident"][0:n, 0:n], MH), repeat_last(X.w[0:n, :], n), ALU.mult)\
            .then_inc(s["diag_ready"], 1)
        self.t_landed(dve, T_K)
        v.tensor_copy(X.kT[:, :, 0:n], X.ps_t[:, :, 0:n]).then_inc(s["t_free"], 1)
        self.on(dve, "wb_full")
        wb = X.ps_s[0:n, 1, :].rearrange("p (h s) -> p h s", h=MH)[:, :, 0:n]
        chain(v.tensor_tensor(X.dm[0:n, :, 0:n], wb, repeat_mid(self.mask, MH), ALU.add))
        chain(v.tensor_reduce(X.rowmax[0:n, :], X.dm[0:n, :, 0:n], AX, ALU.max))
        chain(v.tensor_tensor(X.mb[0:n, 0:4], X.rowmax[0:n, :], X.mprev[0:n, :], ALU.max))
        v.tensor_scalar(X.nmm[0:n, :], X.mb[0:n, 0:4], -1.0, None, ALU.mult)
        v.tensor_tensor(X.earg[0:n, 0:4], X.mprev[0:n, :], X.mb[0:n, 0:4], ALU.subtract)
        chain(v.tensor_tensor(X.mt[0:n, :], X.mb[0:n, 0:4], X.mb[0:n, 4:8], ALU.add))
        v.tensor_scalar(X.earg[0:n, 4:8], X.mt[0:n, :], -1.0, None, ALU.mult).then_inc(s["d_ready"], 1)
        self.z_landed(dve, CCCH)
        v.tensor_copy(X.g7[0:n, :], X.ps_z[CCCH % 2][0:n, :]).then_inc(s[f"zfree{CCCH % 2}"], 1)
        self.on(dve, "expw_ready")
        self.on(dve, "s_full")
        raw = X.ps_s[0:n, 0, :].rearrange("p (h s) -> p h s", h=MH)[:, :, 0:n]
        v.tensor_tensor(X.dm[0:n, :, 0:n], raw, X.dm[0:n, :, 0:n], ALU.mult).then_inc(s["p_ready"], 1)

    def dve_num(self, dve, chain, inter_den, inter_out):
        nc, X, s, n = self.nc, self.X, self.s, self.n
        v = nc.vector
        self.on(dve, "num_full")
        chain(v.tensor_tensor(X.den[0:n, 0:4], X.eval[0:n, 0:4], inter_den, ALU.mult))
        chain(v.tensor_tensor(X.den[0:n, 0:4], X.den[0:n, 0:4], X.ps_m[0:n, 12:16], ALU.add))
        chain(v.scalar_tensor_tensor(X.den[0:n, 4:8], X.den[0:n, 0:4], -1.0, X.den[0:n, 0:4], ALU.mult, ALU.max))
        chain(v.tensor_tensor(X.den[0:n, 4:8], X.den[0:n, 4:8], X.eval[0:n, 4:8], ALU.max))
        v.reciprocal(X.rden[0:n, :], X.den[0:n, 4:8])
        inter_out(dve)
        v.tensor_tensor(X.h[0:n, 0:MW], X.h[0:n, 0:MW], X.ps_n[0][0:n, :], ALU.add).then_inc(s["numf_ready"], 1)

    def dve_last(self, dve, chain):
        nc, X, s, n = self.nc, self.X, self.s, self.n
        v = nc.vector
        chain(v.tensor_copy(X.lastv[0:n, :], X.ps_m[0:n, 16:24]))
        v.tensor_tensor(X.larg[0:n, 0:4], X.w[0:n, :], X.lastv[0:n, 0:4], ALU.subtract)
        v.tensor_tensor(X.larg[0:n, 4:8], X.mprev[0:n, :], X.lastv[0:n, 0:4], ALU.subtract).then_inc(s["larg_ready"], 1)
        self.on(dve, "lval_ready")
        v.tensor_tensor(X.mprev[0:n, :], X.lastv[0:n, 0:4], X.lastv[0:n, 4:8], ALU.add)
        v.tensor_tensor(X.diag[0:n, :, :], X.vz[0:n, :, :], repeat_last(X.lval[0:n, 0:4], DH), ALU.mult)\
            .then_inc(s["vw_ready"], 1)

    def dve_norm(self, dve, chain):
        nc, X, s, n = self.nc, self.X, self.s, self.n
        v = nc.vector
        self.on(dve, "ss2_ready")
        chain(v.reciprocal(X.r2[0:n, :], X.r2[0:n, :]))
        chain(v.tensor_tensor(X.r2[0:n, :], X.r2[0:n, :], X.rden[0:n, :], ALU.mult))
        hm = X.h[0:n, 0:MW].rearrange("p (h d) -> p h d", h=MH)
        chain(v.tensor_tensor(hm, hm, repeat_last(X.r2[0:n, :], DH), ALU.mult))
        self.on(dve, "og_ready")
        v.tensor_tensor(X.h[0:n, 0:MW], X.h[0:n, 0:MW], X.oz[0:n, :], ALU.mult).then_inc(s["hm_ready"], 1)

    def dve_residual(self, dve, chain):
        nc, X, s, n = self.nc, self.X, self.s, self.n
        v = nc.vector
        self.on(dve, "o_full")
        v.tensor_tensor(X.qz[0:n, :], X.ps_z[0][0:n, :], X.row_g[0:n, 0:512], ALU.mult)
        chain(v.tensor_tensor(X.kz[0:n, :], X.ps_z[1][0:n, :], X.row_g[0:n, 512:D], ALU.mult))
        self.on(dve, "xr_in", 16)
        v.tensor_tensor(X.xr[0:n, 0:512], X.xr[0:n, 0:512], X.qz[0:n, :], ALU.add)
        v.tensor_tensor(X.xr[0:n, 512:D], X.xr[0:n, 512:D], X.kz[0:n, :], ALU.add).then_inc(s["x1_ready"], 1)

    def pool_gates(self, pool):
        nc, X, s, n = self.nc, self.X, self.s, self.n
        self.z_out(pool, CCCH)
        nc.gpsimd.tensor_tensor(X.u[0:n, :], X.g7[0:n, 0:CW], X.g7[0:n, CW:2 * CW], ALU.mult).then_inc(s["u_ready"], 1)
        self.z_out(pool, OZ)
        nc.gpsimd.tensor_tensor(X.oz[0:n, :], X.oz[0:n, :], X.mg[0:n, :], ALU.mult).then_inc(s["og_ready"], 1)


def load_row(eng, nc, mod, dst, k, sample, landed):
    if sample:
        eng.dma_start(dst[0:NS, :], for_tokens(mod[1:NC, k * D:(k + 1) * D])).then_inc(landed, 16)
    else:
        eng.dma_start(dst[:, :], mod[0, k * D:(k + 1) * D].partition_broadcast(P)).then_inc(landed, 16)


def dve_mod_rows(dve, nc, X, s, sample):
    n = NS if sample else P
    dve.wait_ge(s["rows_in"], 16 * 3)
    nc.vector.scalar_tensor_tensor(X.row_a[0:n, :], X.row_a[0:n, :], 1.0, X.h[0:n, :], ALU.add, ALU.mult)\
        .then_inc(s["rows_ready"], 1)
    dve.wait_ge(s["rows_ready"], 1)


def mix_prompt(nc, I, O, mod, x1_dram, X, K, s, S):

    def tile(t):
        T = Tile(nc, X, s, t, P, K["tri"][:, :], K["mask"][:, :], K["last"][:, :])
        T.per_t = TB
        return T

    with nc.Block() as block:
        @block.sync
        def _(sp):
            gain = I["norm_mix_g"][0]
            sp.wait_ge(s["x_in"], 16)
            sp.dma_start(X.w_in[:, KC - W_IN_LATE:, :], I["w_in"][0].rearrange("(kc p) n -> p kc n", p=P)
                         [:, KC - W_IN_LATE:, :]).then_inc(s["w_in_in"], 16)
            sp.dma_start(X.gb[:, :], I["mlstm_gate_b"][0].partition_broadcast(P)).then_inc(s["small_in"], 16)
            sp.dma_start(X.mg[:, :], I["mlstm_norm_g"][0].partition_broadcast(P)).then_inc(s["small_in"], 16)
            sp.dma_start(X.sink[:, :], I["swa_sinks"][0].partition_broadcast(P)).then_inc(s["small_in"], 16)
            for j in range(CK):
                sp.dma_start(X.cw[:, j, :], I["conv_w"][0, j].rearrange("(a p) -> p a", p=P),
                             allow_slow_non_contiguous=True).then_inc(s["small_in"], 16)
            load_row(sp, nc, mod, X.row_g, 2, False, s["w_out_in"])
            sp.dma_start(X.w_out[:, :, :], I["w_out"][0].rearrange("(kc p) n -> p kc n", p=P)).then_inc(s["w_out_in"], 16)

            def x_again(t):
                T = tile(t)
                T.t_landed(sp, T_A1)
                sp.dma_start(X.xr[:, :], I["x_prompt"][0, bass.ds(t * P, P), :]).then_inc(s["xr_in"], 16)

            def store(t):
                hold(sp, s["x1_ready"], t + 1)
                sp.dma_start(x1_dram[bass.ds(t * P, P), :], X.xr[:, :]).then_inc(s["x1_stored"], 16)

            with sp.Fori(0, NT - 1) as t:
                hold(sp, s["h_ready"], t + 1)
                sp.dma_start(X.xt[:, :], I["x_prompt"][0, bass.ds(t * P + P, P), :]).then_inc(s["x_in"], 16)
                x_again(t)
                store(t)
            sp.wait_ge(s["h_ready"], NT)
            sp.dma_start(X.xt[0:NS, :], I["x_sample"].rearrange("b t d -> (b t) d")).then_inc(S.s["x_in"], 16)
            load_row(sp, nc, mod, X.row_a, 1, True, S.s["rows_in"])
            load_row(sp, nc, mod, X.row_s, 0, True, S.s["rows_in"])
            x_again(NT - 1)
            done = s["state_out"]
            sp.wait_ge(s["state_ready"], NT)
            sp.dma_start(O["swa_k_p"].rearrange("l b w h d -> (l b w) (h d)"), X.g5[:, 264:392]).then_inc(done, 16)
            sp.dma_start(O["swa_v_p"].rearrange("l b w h d -> (l b w) (h d)"), X.g6[:, 0:128]).then_inc(done, 16)
            sp.dma_start(O["conv_p"].rearrange("l b w c -> (l b w) c"), X.u[P - 2:P, :]).then_inc(done, 16)
            sp.dma_start(O["m_p"].rearrange("l b h -> (l b) h"), X.mprev[0:1, :]).then_inc(done, 16)
            for h in range(MH):
                sp.dma_start(O["n_p"][0, 0, h].rearrange("(k o) -> k o", o=1), X.nT[:, h:h + 1],
                             allow_slow_non_contiguous=True).then_inc(done, 16)
            tile(NT - 1).t_landed(sp, T_HM)
            sp.dma_start(X.h[0:NS, :], gain.partition_broadcast(NS)).then_inc(S.s["rows_in"], 16)
            sp.wait_ge(s["t_free"], NT * TB + 1)
            sp.dma_start(O["C_p"].rearrange("l b h v k -> v (l b h) k"), X.cT_out).then_inc(done, 16)
            store(NT - 1)
            load_row(sp, nc, mod, X.row_g, 2, True, S.s["small_in"])
            sp.wait_ge(done, 16 * (5 + MH))
            sp.wait_ge(s["x1_stored"], 16 * (1 + NT))

        @block.gpsimd
        def _(pool):
            g = nc.gpsimd
            for m in (X.CT, X.nT, X.mprev, X.skT, X.sv_prev):
                g.memset(m[:], 0.0)
            g.memset(X.eps[:, :], EPS)
            g.memset(X.uT[:, :, 0:CK - 1], 0.0).then_inc(s["init"], 1)
            g.memset(X.ses[:, :], 0.0).then_inc(s["x1_stored"], 16)
            with pool.Fori(0, NT) as t:
                T = tile(t)
                T.pool_gates(pool)
                T.on(pool, "swa_full")
                g.tensor_copy(X.skT[:, 0:P], X.skT[:, P:2 * P])
                T.on(pool, "sc_ready")
                g.tensor_copy(K["live_bias"][:, :, 0:P], K["bias"][:, :, 0:P])
                T.on(pool, "pv_full")
                g.tensor_copy(X.sv_prev[:, :], X.g6[:, 0:P]).then_inc(s["pool_done"], 1)

        @block.scalar
        def _(act):
            chain = Chain(act, s["act_step"])
            a = nc.scalar.activation
            act.dma_start(X.xt[:, :], I["x_prompt"][0, 0:P, :]).then_inc(s["x_in"], 16)
            act.dma_start(X.h[:, :], I["norm_mix_g"][0].partition_broadcast(P)).then_inc(s["rows_in"], 16)
            load_row(act, nc, mod, X.row_a, 1, False, s["rows_in"])
            load_row(act, nc, mod, X.row_s, 0, False, s["rows_in"])
            act.wait_ge(s["init"], 1)
            act.wait_ge(s["rows_ready"], 1)

            def body(t, more=True):
                T = tile(t)
                T.act_front(act, chain)
                T.on(act, "sc_ready")
                for h in range(AH):
                    a(X.sc[:, h, :], X.sc[:, h, :], ACT.Exp, bias=X.smx[:, AH + h:AH + h + 1],
                      accum_out=X.ssum[:, h:h + 1])
                a(X.ses[:, :], X.ses[:, :], ACT.Exp).then_inc(s["swa_exp"], 1)
                T.t_landed(act, T_A0)
                a(X.hT[:, 0:4, :], X.ps_t[:, :, :], ACT.Copy).then_inc(s["t_free"], 1)

                def a1_copy(eng):
                    T.t_landed(eng, T_A1)
                    a(X.hT[:, 4:8, :], X.ps_t[:, :, :], ACT.Copy).then_inc(s["t_free"], 1)

                T.act_norm(act, chain, X.ps_n[1][:, :].rearrange("p (h d) -> p h d", h=MH),
                           lambda eng: T.on(eng, "num_full"), "inter_ready", also=a1_copy)
                T.t_landed(act, T_CONV)
                a(X.uT[:, :, CK - 1:], X.ps_t[:, 0:2, :], ACT.Copy)
                a(X.cbT[:, :, :], X.ps_t[:, 2:4, :], ACT.Copy).then_inc(s["t_free"], 1)
                T.t_landed(act, T_OA)
                a(X.mixT[:, 4:6, :], X.ps_t[:, 0:2, :], ACT.Copy).then_inc(s["t_free"], 1)
                T.t_landed(act, T_HM)
                if more:
                    tile(t + 1).act_rms(act, chain)
                else:
                    T.t_landed(act, TB)
                    a(X.cT_out, X.ps_t[:, :, :], ACT.Copy).then_inc(s["t_free"], 1)
                    act.wait_ge(S.s["rows_ready"], 1)
                    S.act_rms(act, Chain(act, S.s["act_step"]))

            tile(0).act_rms(act, chain)
            with act.Fori(0, NT - 1) as t:
                chain.enter(t, 3)
                body(t)
            chain.leave(NT - 1)
            body(NT - 1, more=False)

        @block.vector
        def _(dve):
            chain = Chain(dve, s["dve_step"])
            v = nc.vector
            dve_mod_rows(dve, nc, X, s, False)

            def body(t, more=True):
                T = tile(t)
                T.dve_front(dve, chain, K)
                T.on(dve, "swa_full")
                T.on(dve, "x1_stored", 16)
                chain(v.scalar_tensor_tensor(X.sc[:, :, :], X.ps_s[:, :, :].rearrange("p a (h k) -> p (a h) k", h=2),
                                             AD ** -0.5, K["live_bias"][:, :, :], ALU.mult, ALU.add))
                chain(v.tensor_reduce(X.smx[:, 0:AH], X.sc[:, :, :], AX, ALU.max))
                chain(v.tensor_tensor(X.smx[:, 0:AH], X.smx[:, 0:AH], X.sink[:, :], ALU.max))
                chain(v.tensor_tensor(X.ses[:, :], X.sink[:, :], X.smx[:, 0:AH], ALU.subtract))
                v.tensor_scalar(X.smx[:, AH:2 * AH], X.smx[:, 0:AH], -1.0, None, ALU.mult).then_inc(s["sc_ready"], 1)
                T.on(dve, "swa_exp")
                chain(v.tensor_tensor(X.ssum[:, :], X.ssum[:, :], X.ses[:, :], ALU.add))
                chain(v.reciprocal(X.ssum[:, :], X.ssum[:, :]))
                T.dve_num(dve, chain, X.ps_m[:, 8:12], lambda eng: T.on(eng, "inter_ready"))
                T.dve_last(dve, chain)
                T.on(dve, "pv_full")
                v.tensor_tensor(X.h[:, MW:MW + AH * AD].rearrange("p (h d) -> p h d", h=AH),
                                X.ps_s[:, 0, 0:AH * AD].rearrange("p (h d) -> p h d", h=AH),
                                repeat_last(X.ssum[:, :], AD), ALU.mult).then_inc(s["oa_ready"], 1)
                T.dve_norm(dve, chain)
                T.t_landed(dve, T_HM)
                v.tensor_copy(X.mixT[:, 0:4, :], X.ps_t[:, :, :]).then_inc(s["t_free"], 1)
                T.t_out(dve, T_CONV)
                y = X.diag[:, 0:2, :]
                for a in range(2):
                    last = v.tensor_scalar(y[:, a, :], X.uT[:, a, 0:P], X.cw[:, 0, a:a + 1], None, ALU.mult)
                chain(last)
                for j in range(1, CK):
                    for a in range(2):
                        last = v.scalar_tensor_tensor(y[:, a, :], X.uT[:, a, j:j + P], X.cw[:, j, a:a + 1], y[:, a, :],
                                                      ALU.mult, ALU.add)
                    chain(last)
                chain(v.tensor_tensor(X.mixT[:, 6:8, :], y, X.cbT[:, :, :], ALU.mult))
                v.tensor_copy(X.uT[:, :, 0:CK - 1], X.uT[:, :, P:P + CK - 1]).then_inc(s["yc_ready"], 1)
                T.on(dve, "upd_full")
                for h in range(MH):
                    v.scalar_tensor_tensor(X.CT[:, h, :], X.CT[:, h, :], X.lval[:, 4 + h:5 + h],
                                           X.ps_n[0][:, h * DH:(h + 1) * DH], ALU.mult, ALU.add)
                chain(v.tensor_tensor(X.nT[:, :], X.nT[:, :], X.lval[:, 4:8], ALU.mult))
                v.tensor_tensor(X.nT[:, :], X.nT[:, :], X.ps_m[:, 24:28], ALU.add).then_inc(s["state_ready"], 1)
                if more:
                    tile(t + 1).dve_rms(dve, chain)
                else:
                    dve_mod_rows(dve, nc, X, S.s, True)
                    S.dve_rms(dve, Chain(dve, S.s["dve_step"]))
                T.dve_residual(dve, chain)

            tile(0).dve_rms(dve, chain)
            dve.wait_ge(s["small_in"], 16 * (3 + CK))
            with dve.Fori(0, NT - 1) as t:
                chain.enter(t, 28)
                body(t)
            chain.leave(NT - 1)
            body(NT - 1, more=False)

        @block.tensor
        def _(pe):
            e = K["ident"]
            pe.wait_ge(s["w_in_in"], W_IN_LOADS * 16)

            def body(t, more=True):
                T = tile(t)
                T.project(pe, K)
                for h in range(MH):
                    nc.tensor.matmul(X.ps_n[1][:, h * DH:(h + 1) * DH], X.qT[:, h, :], X.CT[:, h, :], start=True, stop=True)
                    nc.tensor.matmul(X.ps_m[:, 8 + h:9 + h], X.qT[:, h, :], X.nT[:, h:h + 1], start=True, stop=True)
                T.on(pe, "p_ready")
                for h in range(AH):
                    kv, g = h // 2, h % 2
                    mm = nc.tensor.matmul(X.ps_s[:, h // 2, (h % 2) * 2 * P:(h % 2 + 1) * 2 * P],
                                          X.sqT[kv * AD:(kv + 1) * AD, g, :], X.skT[kv * AD:(kv + 1) * AD, :],
                                          start=True, stop=True)
                mm.then_inc(s["swa_full"], 1)
                T.transpose_weights(pe, K)
                T.on(pe, "swa_exp")
                T.batch(pe, T_A0, [(X.sc[:, h, a * P:(a + 1) * P], P, P) for h in range(2) for a in range(2)], e)
                T.intra(pe, K)
                T.batch(pe, T_A1, [(X.sc[:, h, a * P:(a + 1) * P], P, P) for h in range(2, 4) for a in range(2)], e)
                T.t_out(pe, T_A1)
                for h in range(AH):
                    kv = h // 2
                    for a, vals in enumerate((X.sv_prev, X.g6)):
                        mm = nc.tensor.matmul(X.ps_s[:, 0, h * AD:(h + 1) * AD], X.hT[:, 2 * h + a, :],
                                              vals[:, kv * AD:(kv + 1) * AD], start=(a == 0), stop=(a == 1))
                mm.then_inc(s["pv_full"], 1)
                T.on(pe, "u_ready")
                T.batch(pe, T_CONV, [(X.u[:, 0:P], P, P), (X.u[:, P:], P, P), (X.g6[:, 128:256], P, P), (X.g6[:, 256:384], P, P)], e)
                T.on(pe, "numf_ready")
                T.on(pe, "vw_ready")
                for h in range(MH):
                    nc.tensor.matmul(X.ps_n[0][:, h * DH:(h + 1) * DH], X.kz[:, h * DH:(h + 1) * DH], X.diag[:, h, :],
                                     start=True, stop=True)
                    mm = nc.tensor.matmul(X.ps_m[:, 24 + h:25 + h], X.kz[:, h * DH:(h + 1) * DH], X.lval[:, h:h + 1],
                                          start=True, stop=True)
                mm.then_inc(s["upd_full"], 1)
                T.on(pe, "oa_ready")
                T.batch(pe, T_OA, [(X.h[:, MW + a * P:MW + (a + 1) * P], P, P) for a in range(2)], e)
                T.on(pe, "hm_ready")
                T.batch(pe, T_HM, [(X.h[:, h * DH:(h + 1) * DH], P, DH) for h in range(MH)], e)

                def state_back(eng):
                    T.on(eng, "state_ready")
                    T.t_out(eng, T_HM)
                    for h in range(MH):
                        last = nc.tensor.transpose(X.ps_t[:, h, :], X.CT[:, h, :], e[:, :])
                    last.then_inc(s["t_full"], 1)

                T.out_product(pe, lambda eng: T.t_out(eng, T_OA), lambda eng: T.t_out(eng, T_HM),
                              halfway=None if more else state_back)
                if more:
                    tile(t + 1).transpose_rows(pe, K)
                    T.on(pe, "x1_ready")
                    T.on(pe, "pool_done")

            tile(0).transpose_rows(pe, K)
            with pe.Fori(0, NT - 1) as t:
                body(t)
            body(NT - 1, more=False)


S_CONV, S_K0, S_K1, S_ST, S_SC, S_P, S_I, S_HM = range(T_P + 1, T_P + 9)
EXTRA = ("c_in ct_full ct_even_out ct_odd_out k_in kv_in small2_in si_full int_ready cu_full cu_out nu_full n_ready w8_full w8_out km_ready sw_full "
         "st_ready pn_ready y_stored").split()


def sample_tile(nc, X, K, s):
    T = Tile(nc, X, s, 0, NS, K["tri_s"][:, :], K["mask_s"][:, :], K["last_s"][:, :])
    T.per_t = 0
    return T


def mix_sample(nc, I, O, mod, x1_dram, X, K, s, T):
    W = X.w_in[:, :, :].rearrange("p a b -> p (a b)")
    at = [0]

    def take(rows, n, pattern=None, **dims):
        ap = W[0:rows, at[0]:at[0] + n]
        at[0] += n
        return ap.rearrange(pattern, **dims) if pattern else ap

    Cs = take(P, B * MH * DH, "p (m k) -> p m k", k=DH)
    CTs = take(P, B * MH * DH, "p (m k) -> p m k", k=DH)
    Km = take(NS, MH * B * DH, "p (h b k) -> p h b k", h=MH, b=B)
    kc = take(P, B * P, "p (b c) -> p b c", b=B)
    vc = take(P, B * P, "p (b c) -> p b c", b=B)
    kcT = take(P, B * P, "p (b c) -> p b c", b=B)
    nq = take(NS, MW)
    nqz = take(NS, MW)
    n8 = take(B, MW)
    stc = take(2 * B, CW)
    intT = take(P, MH * NS)
    sT = take(P, AH * NS)
    sN = take(NS, AH * NS)
    sc = take(P, WIN + NS)
    pTc = take(P, AH * NS)
    pTn = take(NS, AH * NS)
    full = take(P, 2 * B * (TS + CK - 1), "p (a b w) -> p a b w", a=2, b=B)
    y = take(P, 2 * B * TS, "p (a b t) -> p a b t", a=2, b=B)
    lw = take(NS, MH * B, "p (h b) -> p h b", h=MH)
    wsel = take(NS, B * MH)
    lv8 = take(NS, 8)
    w8 = take(B, 8)
    wlib = take(P, B * MH)
    nden = take(NS, MH)
    cb = take(P, 2 * NS, "p (a t) -> p a t", a=2)

    last_of = K["last_s"][:, :].rearrange("p (b i) -> p b i", i=TS)[:, :, 0]

    with nc.Block() as block:
        @block.sync
        def _(sp):
            k_new, v_new = O["swa_k_s"][0], O["swa_v_s"][0]
            sp.dma_start(k_new[:, 0:WIN - TS], I["cache_swa_k"][0, :, TS:WIN]).then_inc(s["y_stored"], 16)
            sp.dma_start(v_new[:, 0:WIN - TS], I["cache_swa_v"][0, :, TS:WIN]).then_inc(s["y_stored"], 16)
            stored = 2
            sp.dma_start(X.mprev[0:NS, :], for_tokens(I["state_mlstm_m"][0])).then_inc(s["small_in"], 16)
            for h in range(AH):
                sp.dma_start(X.sink[h * NS:(h + 1) * NS, 0:1], I["swa_sinks"][0, h:h + 1].partition_broadcast(NS))\
                    .then_inc(s["small_in"], 16)
            T.on(sp, "h_ready")
            sp.dma_start(X.xr[0:NS, :], I["x_sample"].rearrange("b t d -> (b t) d")).then_inc(s["xr_in"], 16)
            T.z_landed(sp, OZ)
            sp.dma_start(kc, I["cache_swa_k"][0].rearrange("b w h d -> w b (h d)")).then_inc(s["k_in"], 16)
            sp.dma_start(Cs, I["state_mlstm_C"][0].rearrange("b h v k -> v (b h) k")).then_inc(s["c_in"], 16)
            sp.dma_start(vc, I["cache_swa_v"][0].rearrange("b w h d -> w b (h d)")).then_inc(s["kv_in"], 16)
            sp.dma_start(nq, for_tokens(I["state_mlstm_n"][0].rearrange("b h k -> b (h k)"))).then_inc(s["small2_in"], 16)
            sp.dma_start(n8, I["state_mlstm_n"][0].rearrange("b h k -> b (h k)")).then_inc(s["small2_in"], 16)
            sp.dma_start(stc, I["state_conv"][0].rearrange("b w c -> (b w) c")).then_inc(s["small2_in"], 16)
            T.z_out(sp, GATES)
            T.z_out(sp, SVCB)
            for b in range(B):
                for new, rows in ((k_new, X.g5[b * TS:(b + 1) * TS, 264:392]), (v_new, X.g6[b * TS:(b + 1) * TS, 0:P])):
                    sp.dma_start(new[b, WIN - TS:WIN].rearrange("w h d -> w (h d)"), rows).then_inc(s["y_stored"], 16)
                    stored += 1
            T.on(sp, "u_ready")
            for j in range(CK - 1):
                sp.dma_start(O["conv_s"][0, :, j], X.u[TS - CK + 1 + j:NS:TS, :]).then_inc(s["y_stored"], 16)
                stored += 1
            sp.wait_ge(s["n_ready"], 1)
            sp.dma_start(O["n_s"][0].rearrange("b h k -> b (h k)"), n8).then_inc(s["y_stored"], 16)
            sp.dma_start(O["m_s"][0], w8[:, 4:8]).then_inc(s["y_stored"], 16)
            sp.wait_ge(s["cu_out"], 2 * MH)
            sp.dma_start(O["C_s"][0].rearrange("b h v k -> v (b h) k"), Cs).then_inc(s["y_stored"], 16)
            T.on(sp, "x1_ready")
            sp.dma_start(x1_dram[SEQ:SEQ + NS, :], X.xr[0:NS, :]).then_inc(s["y_stored"], 16)
            sp.wait_ge(s["y_stored"], 16 * (stored + 4))

        @block.gpsimd
        def _(pool):
            T.pool_gates(pool)

        @block.scalar
        def _(act):
            chain = Chain(act, s["act_step"])
            chain.n = 1
            a = nc.scalar.activation
            T.act_front(act, chain)
            for k, half in ((S_K0, 0), (S_K1, 4)):
                T.t_landed(act, k)
                a(kcT[:, half:half + 4, :], X.ps_t[:, :, :], ACT.Copy).then_inc(s["t_free"], 1)
            act.wait_ge(s["sw_full"], 1)
            for kv in range(KVH):
                a(sT[:, kv * 2 * NS:(kv + 1) * 2 * NS], X.ps_n[kv][:, 0:2 * NS], ACT.Copy)
                last = a(sN[:, kv * 2 * NS:(kv + 1) * 2 * NS], X.ps_n[kv][0:NS, P:P + 2 * NS], ACT.Copy)
            last.then_inc(s["st_ready"], 1)
            T.on(act, "sc_ready")
            a(sc, sc, ACT.Exp, bias=X.smx[:, 1:2], accum_out=X.ssum[:, 0:1])
            a(X.ses[:, 0:1], X.ses[:, 0:1], ACT.Exp).then_inc(s["swa_exp"], 1)
            for i in range(0, B, 2):
                act.wait_ge(s["ct_full"], i + 1)
                a(CTs[:, 4 * i:4 * i + 4, :], X.ps_s[:, 0, :], ACT.Copy).then_inc(s["ct_even_out"], 1)
            act.wait_ge(s["si_full"], 1)
            a(intT, X.ps_n[1][:, 0:P], ACT.Copy).then_inc(s["int_ready"], 1)
            T.act_norm(act, chain, X.ps_t[0:NS, :, :], lambda eng: T.t_landed(eng, S_I), "t_free")
            T.on(act, "pv_full")
            a(X.mixT[:, 4:6, 0:NS], X.ps_s[:, 0, 0:2 * NS].rearrange("p (a t) -> p a t", a=2), ACT.Copy)\
                .then_inc(s["oa_ready"], 1)

        @block.vector
        def _(dve):
            chain = Chain(dve, s["dve_step"])
            chain.n = 2
            v = nc.vector
            dve.wait_ge(s["small_in"], 16 * (2 + AH))
            T.dve_front(dve, chain, K)
            T.t_landed(dve, S_CONV)
            v.tensor_copy(full[:, :, :, CK - 1:], X.ps_t[:, 0:2, 0:NS].rearrange("p a (b t) -> p a b t", b=B))
            v.tensor_copy(cb, X.ps_t[:, 2:4, 0:NS]).then_inc(s["t_free"], 1)
            T.t_landed(dve, S_ST)
            v.tensor_copy(full[:, :, :, 0:CK - 1], X.ps_t[:, 0:2, 0:2 * B].rearrange("p a (b w) -> p a b w", b=B))\
                .then_inc(s["t_free"], 1)
            T.t_out(dve, S_ST)
            for a in range(2):
                last = v.tensor_scalar(y[:, a], full[:, a, :, 0:TS], X.cw[:, 0, a:a + 1], None, ALU.mult)
            chain(last)
            for j in range(1, CK):
                for a in range(2):
                    last = v.scalar_tensor_tensor(y[:, a], full[:, a, :, j:j + TS], X.cw[:, j, a:a + 1], y[:, a],
                                                  ALU.mult, ALU.add)
                chain(last)
            v.tensor_tensor(X.mixT[:, 6:8, 0:NS], y.rearrange("p a b t -> p a (b t)"), cb, ALU.mult)\
                .then_inc(s["yc_ready"], 1)
            T.t_landed(dve, S_SC)
            v.scalar_tensor_tensor(sc, X.ps_t[:, :, :].rearrange("p a b -> p (a b)")[:, 0:WIN + NS], AD ** -0.5,
                                   K["s_bias"][:, :], ALU.mult, ALU.add).then_inc(s["t_free"], 1)
            T.t_out(dve, S_SC)
            chain(v.tensor_reduce(X.smx[:, 0:1], sc, AX, ALU.max))
            chain(v.tensor_tensor(X.smx[:, 0:1], X.smx[:, 0:1], X.sink[:, 0:1], ALU.max))
            v.tensor_tensor(X.ses[:, 0:1], X.sink[:, 0:1], X.smx[:, 0:1], ALU.subtract)
            v.tensor_scalar(X.smx[:, 1:2], X.smx[:, 0:1], -1.0, None, ALU.mult).then_inc(s["sc_ready"], 1)
            T.on(dve, "swa_exp")
            chain(v.tensor_tensor(X.ssum[:, 0:1], X.ssum[:, 0:1], X.ses[:, 0:1], ALU.add))
            chain(v.reciprocal(X.ssum[:, 0:1], X.ssum[:, 0:1]))
            v.tensor_scalar(sc, sc, X.ssum[:, 0:1], None, ALU.mult).then_inc(s["pn_ready"], 1)
            for i in range(1, B, 2):
                dve.wait_ge(s["ct_full"], i + 1)
                v.tensor_copy(CTs[:, 4 * i:4 * i + 4, :], X.ps_s[:, 1, :].rearrange("p (a b) -> p a b", b=DH))\
                    .then_inc(s["ct_odd_out"], 1)
            T.t_landed(dve, S_P)
            v.tensor_copy(pTc, X.ps_t[:, 0, :])
            v.tensor_copy(pTn, X.ps_t[0:NS, 1, :]).then_inc(s["t_free"], 1)
            dve.wait_ge(s["small2_in"], 16 * 3)
            chain(v.tensor_tensor(nqz, X.qz[0:NS, :], nq, ALU.mult))
            chain(v.tensor_reduce(nden, nqz.rearrange("p (h k) -> p h k", h=MH), AX, ALU.add))
            T.dve_num(dve, chain, nden, lambda eng: T.t_out(eng, S_I))
            T.dve_last(dve, chain)
            same = K["same"][:, :]
            v.tensor_tensor(lw, repeat_mid(same, MH), repeat_last(X.lval[0:NS, 0:4], B), ALU.mult)
            v.tensor_tensor(wsel.rearrange("p (b h) -> p b h", b=B), repeat_last(last_of, MH),
                            repeat_mid(X.lval[0:NS, 4:8], B), ALU.mult)
            v.tensor_copy(lv8[:, 0:4], X.lval[0:NS, 4:8])
            v.tensor_copy(lv8[:, 4:8], X.mt[0:NS, :])
            for h in range(MH):
                last = v.tensor_tensor(Km[:, h], repeat_mid(X.kz[0:NS, h * DH:(h + 1) * DH], B), repeat_last(same, DH),
                                       ALU.mult)
            last.then_inc(s["km_ready"], 1)
            T.dve_norm(dve, chain)
            dve.wait_ge(s["w8_full"], 1)
            v.tensor_copy(w8, X.ps_m[0:B, 0:8])
            v.tensor_copy(wlib, X.ps_m[:, 32:32 + B * MH]).then_inc(s["w8_out"], 1)
            dve.wait_ge(s["w8_out"], 1)
            dve.wait_ge(s["nu_full"], 1)
            for h in range(MH):
                cols = slice(h * DH, (h + 1) * DH)
                last = v.scalar_tensor_tensor(n8[:, cols], n8[:, cols], w8[:, h:h + 1], X.ps_n[0][0:B, cols], ALU.mult, ALU.add)
            last.then_inc(s["n_ready"], 1)
            T.t_landed(dve, S_HM)
            v.tensor_copy(X.mixT[:, 0:4, 0:NS], X.ps_t[:, :, 0:NS]).then_inc(s["t_free"], 1)
            for i in range(2 * MH):
                h, half = i // 2, i % 2
                dve.wait_ge(s["cu_full"], i + 1)
                for j in range(B // 2):
                    m = (half * (B // 2) + j) * MH + h
                    last = v.scalar_tensor_tensor(Cs[:, m, :], Cs[:, m, :], wlib[:, m:m + 1],
                                                  X.ps_s[:, i % 2, j * DH:(j + 1) * DH], ALU.mult, ALU.add)
                last.then_inc(s["cu_out"], 1)
            T.dve_residual(dve, chain)

        @block.tensor
        def _(pe):
            e = K["ident"]
            T.transpose_rows(pe, K)
            T.project(pe, K)
            T.transpose_weights(pe, K)
            T.on(pe, "u_ready")
            T.batch(pe, S_CONV, [(X.u[0:NS, 0:P], NS, P), (X.u[0:NS, P:], NS, P),
                                 (X.g6[0:NS, 128:256], NS, P), (X.g6[0:NS, 256:384], NS, P)], e)
            pe.wait_ge(s["k_in"], 16)
            T.batch(pe, S_K0, [(kc[:, b, :], P, P) for b in range(4)], e)
            T.batch(pe, S_K1, [(kc[:, b, :], P, P) for b in range(4, 8)], e)
            T.t_out(pe, S_K1)
            for kv in range(KVH):
                rows = slice(kv * AD, (kv + 1) * AD)
                raw = X.ps_n[kv][:, 0:2 * NS].rearrange("p (g t) -> p g t", g=2)
                for b in range(B):
                    tokens = slice(b * TS, (b + 1) * TS)
                    nc.tensor.matmul(raw[:, :, tokens], kcT[rows, b, :], X.sqT[rows, :, tokens], start=True, stop=True)
                mm = nc.tensor.matmul(X.ps_n[kv][0:NS, P:P + 2 * NS].rearrange("p (g t) -> p g t", g=2),
                                      X.skT[rows, P:P + NS], X.sqT[rows, :, 0:NS], start=True, stop=True)
            mm.then_inc(s["sw_full"], 1)
            pe.wait_ge(s["small2_in"], 16 * 3)
            T.batch(pe, S_ST, [(stc[:, 0:P], 2 * B, P), (stc[:, P:], 2 * B, P)], e)
            pe.wait_ge(s["st_ready"], 1)
            T.batch(pe, S_SC, [(sT, P, P), (sN, NS, P)], e)
            pe.wait_ge(s["c_in"], 16)
            for i in range(B):
                out = ("ct_even_out", "ct_odd_out")[i % 2]
                if i >= 2:
                    pe.wait_ge(s[out], i // 2)
                for j in range(4):
                    last = nc.tensor.transpose(X.ps_s[:, i % 2, j * P:(j + 1) * P], Cs[:, 4 * i + j, :], e[:, :])
                last.then_inc(s["ct_full"], 1)
            pe.wait_ge(s["pn_ready"], 1)
            T.batch(pe, S_P, [(sc[:, 0:WIN], P, P), (sc[:, WIN:], P, NS)], e)
            T.t_out(pe, S_P)
            pe.wait_ge(s["ct_even_out"], B // 2)
            pe.wait_ge(s["ct_odd_out"], B // 2)
            for b in range(B):
                for h in range(MH):
                    mm = nc.tensor.matmul(X.ps_n[1][:, h * NS + b * TS:h * NS + (b + 1) * TS], CTs[:, b * MH + h, :],
                                          X.qT[:, h, b * TS:(b + 1) * TS], start=True, stop=True)
            mm.then_inc(s["si_full"], 1)
            pe.wait_ge(s["int_ready"], 1)
            T.batch(pe, S_I, [(intT[:, h * NS:(h + 1) * NS], P, NS) for h in range(MH)], e)
            T.intra(pe, K)
            pe.wait_ge(s["kv_in"], 16)
            for h in range(AH):
                kv = h // 2
                vals = slice(kv * AD, (kv + 1) * AD)
                out = X.ps_s[(h % 2) * AD:(h % 2 + 1) * AD, 0, (h // 2) * NS:(h // 2 + 1) * NS]
                nc.tensor.matmul(out, X.g6[0:NS, vals], pTn[:, h * NS:(h + 1) * NS], start=True, stop=False)
                for b in range(B):
                    mm = nc.tensor.matmul(out[:, b * TS:(b + 1) * TS], vc[:, b, vals],
                                          pTc[:, h * NS + b * TS:h * NS + (b + 1) * TS], start=False, stop=(b == B - 1))
            mm.then_inc(s["pv_full"], 1)
            T.on(pe, "numf_ready")
            T.on(pe, "vw_ready")
            pe.wait_ge(s["km_ready"], 1)
            nc.tensor.matmul(X.ps_m[0:B, 0:8], last_of, lv8, start=True, stop=True)
            nc.tensor.matmul(X.ps_m[:, 32:32 + B * MH], K["ones"][0:NS, :], wsel, start=True, stop=True)\
                .then_inc(s["w8_full"], 1)
            for h in range(MH):
                mm = nc.tensor.matmul(X.ps_n[0][0:B, h * DH:(h + 1) * DH], lw[:, h, :], X.kz[0:NS, h * DH:(h + 1) * DH],
                                      start=True, stop=True)
            mm.then_inc(s["nu_full"], 1)
            T.on(pe, "hm_ready")
            T.batch(pe, S_HM, [(X.h[0:NS, h * DH:(h + 1) * DH], NS, DH) for h in range(MH)], e)
            T.on(pe, "oa_ready")
            for i in range(2 * MH):
                h, half = i // 2, i % 2
                if i >= 2:
                    pe.wait_ge(s["cu_out"], i - 1)
                nc.tensor.matmul(X.ps_s[:, i % 2, :], X.diag[0:NS, h, :], Km[:, h, half * (B // 2):(half + 1) * (B // 2), :],
                                 start=True, stop=True).then_inc(s["cu_full"], 1)
            T.out_product(pe, lambda eng: T.on(eng, "oa_ready"), lambda eng: T.t_out(eng, S_HM))


NB = 8
GPT = PH * TOPK // NB
PPT = GPT // 2
NG = NT * GPT
QS = P // NS
SG = PH * TOPK // QS // NB


def experts(nc, I, O, mod, x1_dram, K):
    with ExitStack() as ctx:
        def sb(name, shape, dt=F32):
            return ctx.enter_context(nc.sbuf_tensor(name, shape, dt))

        def ps(name, shape):
            return ctx.enter_context(nc.psum_tensor(name, shape, F32))

        wq = sb("wq", [P, KC, PH * 2 * P])
        scale, shift, hstat = sb("norm2_scale", [P, D]), sb("norm2_shift", [P, D]), sb("norm2_stat", [P, 4])
        h_next, hT = sb("h_next", [P, D]), sb("hT_next", [P, KC, P])
        sub, subT = sb("subkeys", [PK, 2, P]), sb("subkeysT", [P, 2, PK])
        q, qT, sc, scw = sb("q", [P, 2, P]), sb("qT", [P, 2, P]), sb("key_scores", [P, 2, PK]), sb("key_scores_w", [P, 2, PK])
        top, topi, topf = sb("top", [P, 2, TOPK]), sb("top_i", [P, 2, TOPK], U32), sb("top_f", [P, 2, TOPK])
        cand, candw = sb("cand", [P, TOPK * TOPK]), sb("cand_w", [P, TOPK * TOPK])
        cs, ci = sb("cand_top", [P, TOPK]), sb("cand_i", [P, TOPK], U32)
        ab, abf = sb("sel_ab", [P, 2, TOPK], U32), sb("sel_abf", [P, 2, TOPK])
        hot, sel = sb("one_hot", [P, 2, TOPK, TOPK]), sb("selected", [P, 2, TOPK])
        iota = sb("iota_f", [P, TOPK])
        idx = sb("expert_idx", [P, (NT + 1) * PH * TOPK], U32)
        gate = sb("expert_gate", [P, (NT + 1) * PH * TOPK])
        gsum = sb("gate_sum", [P, 2])
        idx_s, gate_s = sb("sample_idx", [P, SG * NB], U32), sb("sample_gate", [P, SG * NB])
        h_cur = sb("h_cur", [P, D])
        u_rows, v_rows = sb("u_rows", [P, NB, D]), sb("v_rows", [P, NB, D])
        u_idx, v_idx = sb("u_idx", [P, 2, NB], U32), sb("v_idx", [P, 2, NB], U32)
        dots, act_val, wts = sb("dots", [P, 2, NB]), sb("act_val", [P, 2, NB]), sb("wts", [P, 2, NB])
        diag = sb("wt_diag", [P, 2, NB, P])
        x1, y, gate2, gate2_s, fin = sb("x1", [P, D]), sb("y", [P, D]), sb("gate2", [P, D]), sb("gate2_s", [NS, D]), sb("final_g", [P, D])
        gain_s = sb("gain_s", [NS, D])
        fs, eps = sb("final_stat", [P, 4]), sb("eps2", [P, 1])
        fold = sb("fold", [P, NS])
        ps_y, ps_h, ps_r = ps("ps_y", [P, D]), ps("ps_h", [P, KC, P]), ps("ps_r", [P, 3, 512])
        names = ("sub_in small_in rows2_in gain_in init h_sq h_sq_ready h_normed subT_full subT_out hn_in hT_full hT_out copied q_full q_out qt_full qt_out sc_full "
                 "sc_out sc_free routed gate_raw exp_ready normed hs_in u_staged v_staged u_used v_used "
                 "act_ready wts_ready diag_ready y_out x1_in ss_ready rt_ready done stored step "
                 "folded sub_step").split()
        wq_in = [ctx.enter_context(nc.semaphore(f"wq_in{i}")) for i in range(PH // 2)]
        spread_in = [ctx.enter_context(nc.semaphore(f"spread_in{g}")) for g in range(SG)]
        s = {n: ctx.enter_context(nc.semaphore("ex_" + n)) for n in names}
        u_in = [ctx.enter_context(nc.semaphore(f"u_in{j}")) for j in range(NB)]
        v_in = [ctx.enter_context(nc.semaphore(f"v_in{j}")) for j in range(NB)]

        with nc.Block() as block:
            @block.sync
            def _(sp):
                sp.dma_start(h_next[:, :], x1_dram[0:P, :]).then_inc(s["hn_in"], 16)
                sp.dma_start(scale[:, :], mod[0, 4 * D:5 * D].partition_broadcast(P)).then_inc(s["rows2_in"], 16)
                sp.dma_start(shift[:, :], mod[0, 3 * D:4 * D].partition_broadcast(P)).then_inc(s["rows2_in"], 16)
                sp.dma_start(y[:, :], I["norm_ffn_g"][0].partition_broadcast(P)).then_inc(s["gain_in"], 16)
                sp.dma_start(sub[:, :, :], I["peer_subkeys"][0].rearrange("a k d -> k a d")).then_inc(s["sub_in"], 16)
                wq_dram = I["peer_wq"][0].rearrange("(kc p) n -> p kc n", p=P)
                for i, landed in enumerate(wq_in):
                    cols = slice(i * 4 * P, (i + 1) * 4 * P)
                    sp.dma_start(wq[:, :, cols], wq_dram[:, :, cols]).then_inc(landed, 16)
                sp.dma_start(gate2[:, :], mod[0, 5 * D:6 * D].partition_broadcast(P)).then_inc(s["small_in"], 16)
                for b in range(B):
                    sp.dma_start(gate2_s[b * TS:(b + 1) * TS, :], mod[1 + b, 5 * D:6 * D].partition_broadcast(TS))\
                        .then_inc(s["small_in"], 16)
                sp.dma_start(fin[:, :], I["final_g"].partition_broadcast(P)).then_inc(s["small_in"], 16)
                sp.dma_start(x1[:, :], x1_dram[0:P, :]).then_inc(s["x1_in"], 16)

                def next_rows(t, rows=P):
                    hold(sp, s["copied"], t + 1)
                    hold(sp, s["hT_out"], t + 1)
                    sp.dma_start(h_next[0:rows, :], x1_dram[bass.ds(t * P + P, rows), :]).then_inc(s["hn_in"], 16)

                def finish(t, rows=P):
                    hold(sp, s["done"], t + 1)
                    sp.dma_start(O["y_p"][0, bass.ds(t * P, P), :], x1[:, :]).then_inc(s["stored"], 16)
                    hold(sp, s["stored"], t * 16 + 16)
                    sp.dma_start(x1[0:rows, :], x1_dram[bass.ds(t * P + P, rows), :]).then_inc(s["x1_in"], 16)

                next_rows(0)
                with sp.Fori(0, NT - 2) as t:
                    next_rows(t + 1)
                    finish(t)
                next_rows(NT - 1, NS)
                sp.wait_ge(s["h_normed"], NT)
                for b in range(B):
                    for dst, k in ((scale, 4), (shift, 3)):
                        sp.dma_start(dst[b * TS:(b + 1) * TS, :], mod[1 + b, k * D:(k + 1) * D].partition_broadcast(TS))\
                            .then_inc(s["rows2_in"], 16)
                sp.dma_start(gain_s[:, :], I["norm_ffn_g"][0].partition_broadcast(NS)).then_inc(s["gain_in"], 16)
                finish(NT - 2)
                for g in range(SG):
                    if g == SG - 1:
                        sp.wait_ge(s["u_used"], NG * NB)
                        for i in range(QS):
                            sp.dma_start(h_cur[i * NS:(i + 1) * NS, :], h_next[0:NS, :]).then_inc(s["hs_in"], 16)
                    sp.wait_ge(s["normed"], NT * PH + 2 * g + 2)
                    for i in range(QS):
                        rows, first = slice(i * NS, (i + 1) * NS), NT * P + (g * QS + i) * NB
                        for dst, src in ((idx_s, idx), (gate_s, gate)):
                            sp.dma_start(dst[rows, g * NB:(g + 1) * NB], src[0:NS, first:first + NB])\
                                .then_inc(spread_in[g], 16)
                finish(NT - 1, NS)
                sp.wait_ge(s["done"], NT + 1)
                sp.dma_start(O["y_s"].rearrange("b t d -> (b t) d"), x1[0:NS, :]).then_inc(s["stored"], 16)
                sp.wait_ge(s["stored"], 16 * (NT + 1))

            @block.gpsimd
            def _(pool):
                g = nc.gpsimd
                g.tensor_copy(iota[:, :], K["iota16"][:, :])
                g.memset(eps[:, :], EPS)
                g.memset(fold[:, :], 0.0).then_inc(s["init"], 1)
                pool.wait_ge(s["init"], 1)
                for i in range(QS):
                    g.affine_select(out=fold[:, :], in_=fold[:, :], compare_op=ALU.not_equal, fill=1.0, base=-i * NS,
                                    pattern=[[-1, NS]], channel_multiplier=1).then_inc(s["init"], 1)
                    pool.wait_ge(s["init"], 2 + i)

                def gather(rows, table, where, landed, used, i, j, first=False):
                    if not first:
                        hold(pool, used, i * NB + (j + 1 - NB))
                    g.indirect_dma_start(rows[:, j, :], None, table, bass.IndirectOffsetOnAxis(where[:, j:j + 1], 0))\
                        .then_inc(landed[j], 16)

                def stage(dst, src, signal, used, i, par, first=False):
                    if not first:
                        hold(pool, used, i * NB - NB)
                    g.tensor_copy(dst[:, par, :], src).then_inc(signal, 1)
                    hold(pool, signal, i + 1)

                U, V = I["peer_u"][0], I["peer_v"][0]

                def step(i, par, u_src, v_src, first=False):
                    stage(u_idx, u_src, s["u_staged"], s["u_used"], i, par, first)
                    stage(v_idx, v_src, s["v_staged"], s["v_used"], i - 1, 1 - par, first or (isinstance(i, int) and i == 2))
                    for j in range(NB):
                        gather(u_rows, U, u_idx[:, par], u_in, s["u_used"], i, j)
                        gather(v_rows, V, v_idx[:, 1 - par], v_in, s["v_used"], i - 1, j, first)

                def cols(i):
                    return idx[:, bass.ds(i * NB, NB)]

                pool.wait_ge(s["routed"], 1)
                stage(u_idx, cols(0), s["u_staged"], s["u_used"], 0, 0, True)
                for j in range(NB):
                    gather(u_rows, U, u_idx[:, 0], u_in, s["u_used"], 0, j, True)
                step(1, 1, cols(1), cols(0), True)
                pool.wait_ge(s["routed"], 2)
                step(2, 0, cols(2), cols(1))
                step(3, 1, cols(3), cols(2))
                with pool.Fori(2, NG // 2) as pair:
                    hold(pool, s["routed"], pair + 1)
                    first = pair * 2
                    for par in range(2):
                        step(first + par, par, idx[:, bass.ds(pair * (2 * NB) + par * NB, NB)],
                             idx[:, bass.ds(pair * (2 * NB) + (par - 1) * NB, NB)])
                for i in range(NG, NG + SG):
                    pool.wait_ge(spread_in[i - NG], 2 * 16 * QS)
                    step(i, i % 2, idx_s[:, (i - NG) * NB:(i - NG + 1) * NB],
                         cols(i - 1) if i == NG else idx_s[:, (i - 1 - NG) * NB:(i - NG) * NB])
                i = NG + SG
                stage(v_idx, idx_s[:, (SG - 1) * NB:], s["v_staged"], s["v_used"], i - 1, (i - 1) % 2)
                for j in range(NB):
                    gather(v_rows, V, v_idx[:, (i - 1) % 2], v_in, s["v_used"], i - 1, j)

            @block.scalar
            def _(act):
                a = nc.scalar.activation

                def hT_copy(t, n=P):
                    hold(act, s["hn_in"], t * 16 + 16)
                    a(hT[0:n, :, :], h_next[0:n, :].rearrange("p (a b) -> p a b", b=P), ACT.Square,
                      accum_out=hstat[0:n, 0:1]).then_inc(s["h_sq"], 1)
                    hold(act, s["h_sq"], t + 1)
                    a(hstat[0:n, 1:2], hstat[0:n, 0:1], ACT.Sqrt, scale=1.0 / D, bias=eps[0:n, :]).then_inc(s["h_sq_ready"], 1)
                    hold(act, s["hT_full"], t + 1)
                    a(hT[:, 0:4, :], ps_h[:, 0:4, :], ACT.Copy)
                    a(hT[:, 4:8, :], ps_h[:, 4:8, :], ACT.Copy).then_inc(s["hT_out"], 1)

                def head(H):
                    hold(act, s["q_full"], H + 1)
                    a(q[:, :, :], ps_r[:, 0, 0:256], ACT.Copy).then_inc(s["q_out"], 1)
                    hold(act, s["qt_full"], H + 1)
                    a(qT[:, :, :], ps_r[:, 1, 0:256], ACT.Copy).then_inc(s["qt_out"], 1)
                    hold(act, s["sc_full"], H + 1)
                    hold(act, s["sc_free"], H + 1)
                    a(sc[:, :, :], ps_r[:, 2, 0:256], ACT.Copy).then_inc(s["sc_out"], 1)

                def group(i, par, first=False):
                    hold(act, s["u_used"], i * NB + NB)
                    a(act_val[:, par, :], dots[:, par, :], ACT.Gelu_apprx_tanh).then_inc(s["act_ready"], 1)
                    if not first:
                        hold(act, s["v_used"], i * NB - NB)
                    hold(act, s["wts_ready"], i + 1)
                    for j in range(NB):
                        a(diag[:, par, j, :], K["ident"][:, :], ACT.Copy, scale=wts[:, par, j:j + 1])\
                            .then_inc(s["diag_ready"], 1)

                def gate_exp(H):
                    hold(act, s["gate_raw"], H + 1)
                    cols = bass.ds(H * TOPK, TOPK)
                    a(gate[:, cols], gate[:, cols], ACT.Exp, accum_out=gsum[:, 0:1]).then_inc(s["exp_ready"], 1)

                def pair(i, H, two=False, first=False, between=None):
                    head(H)
                    group(i, 0, first)
                    if between:
                        between()
                    if two:
                        gate_exp(H)
                        head(H + 1)
                    group(i + 1, 1, first)
                    gate_exp(H + 1 if two else H)

                def y_copy(last_group):
                    hold(act, s["v_used"], last_group * NB + NB)
                    a(y[:, 0:512], ps_y[:, 0:512], ACT.Copy)
                    a(y[:, 512:D], ps_y[:, 512:D], ACT.Copy).then_inc(s["y_out"], 1)

                def root(t, n=P):
                    hold(act, s["ss_ready"], t + 1)
                    a(fs[0:n, 1:2], fs[0:n, 0:1], ACT.Sqrt, scale=1.0 / D, bias=eps[0:n, :]).then_inc(s["rt_ready"], 1)

                act.wait_ge(s["init"], 1 + QS)
                act.wait_ge(s["subT_full"], 1)
                a(subT[:, :, :], ps_r[:, 1, 0:256], ACT.Copy).then_inc(s["subT_out"], 1)
                hT_copy(0)
                for H in range(2):
                    head(H)
                    gate_exp(H)
                pair(0, 2, first=True)
                with act.Fori(0, NT - 1) as t:
                    with act.Fori(1, PPT - 2) as p:
                        pair(t * GPT + p * 2, t * PH + p + 2)
                    hT_copy(t + 1)
                    with act.Fori(PPT - 2, PPT) as p:
                        pair(t * GPT + p * 2, t * PH + p + 2)
                    pair(t * GPT + GPT, t * PH + (PH + 2), between=lambda: y_copy(t * GPT + (GPT - 1)))
                    root(t)
                with act.Fori(1, 3) as p:
                    pair(p * 2 + (NT - 1) * GPT, p * 2 + ((NT - 1) * PH + 1), two=True)
                pair((NT - 1) * GPT + 6, NT * PH - 1)
                hT_copy(NT, NS)
                with act.Fori(4, PPT) as p:
                    pair(p * 2 + (NT - 1) * GPT, p * 2 + (NT * PH - 8), two=True)
                group(NG, 0)
                y_copy(NG - 1)
                group(NG + 1, 1)
                root(NT - 1)
                group(NG + 2, 0)
                group(NG + 3, 1)
                y_copy(NG + SG - 1)
                root(NT, NS)

            @block.vector
            def _(dve):
                chain = Chain(dve, s["step"])
                v = nc.vector

                def group(i, par, gates):
                    for j in range(NB):
                        hold(dve, u_in[j], i * 16 + 16)
                        v.tensor_tensor_reduce(u_rows[:, j, :], u_rows[:, j, :], h_cur[:, :], 1.0, 0.0, ALU.mult, ALU.add,
                                               dots[:, par, j:j + 1]).then_inc(s["u_used"], 1)
                    hold(dve, s["act_ready"], i + 1)
                    v.tensor_tensor(wts[:, par, :], act_val[:, par, :], gates, ALU.mult).then_inc(s["wts_ready"], 1)

                def top16(vals, where, scores, work):
                    chain(v.max(vals[:, 0:8], scores))
                    chain(v.match_replace(work, vals[:, 0:8], scores, NEG))
                    chain(v.max(vals[:, 8:16], work))
                    v.max_index(where[:, 0:8], vals[:, 0:8], scores)
                    return v.max_index(where[:, 8:16], vals[:, 8:16], work)

                def route(H):
                    hold(dve, s["sc_out"], H + 1)
                    top16(top[:, 0], topi[:, 0], sc[:, 0, :], scw[:, 0, :])
                    top16(top[:, 1], topi[:, 1], sc[:, 1, :], scw[:, 1, :]).then_inc(s["sc_free"], 1)
                    v.tensor_tensor(cand[:, :].rearrange("p (a b) -> p a b", a=TOPK), repeat_last(top[:, 0, :], TOPK),
                                    repeat_mid(top[:, 1, :], TOPK), ALU.add).then_inc(s["sub_step"], 1)
                    hold(dve, s["sub_step"], H + 1)
                    v.tensor_copy(topf[:, :, :], topi[:, :, :])
                    chain(top16(cs, ci, cand[:, :], candw[:, :]))
                    cols = bass.ds(H * TOPK, TOPK)
                    v.tensor_scalar(gate[:, cols], cs[:, :], cs[:, 0:1], None, ALU.subtract).then_inc(s["gate_raw"], 1)
                    v.tensor_scalar(ab[:, 0, :], ci[:, :], 4, None, ALU.logical_shift_right)
                    chain(v.tensor_scalar(ab[:, 1, :], ci[:, :], 15, None, ALU.bitwise_and))
                    chain(v.tensor_copy(abf[:, :, :], ab[:, :, :]))
                    for k in range(2):
                        last = v.tensor_tensor(hot[:, k], repeat_last(abf[:, k, :], TOPK), repeat_mid(iota[:, :], TOPK),
                                               ALU.is_equal)
                    chain(last)
                    for k in range(2):
                        last = v.tensor_tensor(hot[:, k], hot[:, k], repeat_mid(topf[:, k, :], TOPK), ALU.mult)
                    chain(last)
                    chain(v.tensor_reduce(sel[:, :, :], hot[:, :, :, :], AX, ALU.add))
                    v.scalar_tensor_tensor(idx[:, cols], sel[:, 0, :], float(PK), sel[:, 1, :], ALU.mult, ALU.add)\
                        .then_inc(s["routed"], 1)
                    hold(dve, s["exp_ready"], H + 1)
                    chain(v.reciprocal(gsum[:, 1:2], gsum[:, 0:1]))
                    v.tensor_scalar(gate[:, cols], gate[:, cols], gsum[:, 1:2], None, ALU.mult).then_inc(s["normed"], 1)
                    hold(dve, s["normed"], H + 1)

                ROUTE = 16

                def norm(t, n=P):
                    hold(dve, s["h_sq_ready"], t + 1)
                    chain(v.reciprocal(hstat[0:n, 2:3], hstat[0:n, 1:2]))
                    chain(v.scalar_tensor_tensor(h_next[0:n, :], h_next[0:n, :], hstat[0:n, 2:3], scale[0:n, :],
                                                 ALU.mult, ALU.mult))
                    v.tensor_tensor(h_next[0:n, :], h_next[0:n, :], shift[0:n, :], ALU.add).then_inc(s["h_normed"], 1)

                def gained(rows, gain, loads, turn):
                    n = rows
                    dve.wait_ge(s["rows2_in"], 16 * loads)
                    dve.wait_ge(s["gain_in"], 16 * turn)
                    chain(v.scalar_tensor_tensor(scale[0:n, :], scale[0:n, :], 1.0, gain[0:n, :], ALU.add, ALU.mult))

                def begin(t):
                    hold(dve, s["h_normed"], t + 1)
                    v.tensor_copy(h_cur[:, :], h_next[:, :]).then_inc(s["copied"], 1)
                    hold(dve, s["copied"], t + 1)

                def pair(i, first, H, two=False):
                    group(i, 0, gate[:, bass.ds(first, NB)])
                    if two:
                        route(H)
                    group(i + 1, 1, gate[:, bass.ds(first + NB, NB)])
                    route(H + 1 if two else H)

                def finish(t, n, src, row):
                    hold(dve, s["x1_in"], t * 16 + 16)
                    chain(v.tensor_tensor(y[0:n, :], src, row, ALU.mult))
                    chain(v.tensor_tensor(x1[0:n, :], x1[0:n, :], y[0:n, :], ALU.add))
                    v.tensor_tensor_reduce(y[0:n, :], x1[0:n, :], x1[0:n, :], 1.0, 0.0, ALU.mult, ALU.add, fs[0:n, 0:1])\
                        .then_inc(s["ss_ready"], 1)
                    hold(dve, s["rt_ready"], t + 1)
                    chain(v.reciprocal(fs[0:n, 2:3], fs[0:n, 1:2]))
                    v.scalar_tensor_tensor(x1[0:n, :], x1[0:n, :], fs[0:n, 2:3], fin[0:n, :], ALU.mult, ALU.mult)\
                        .then_inc(s["done"], 1)

                dve.wait_ge(s["init"], 1 + QS)
                v.memset(fs[:, :], 0.0).then_inc(s["sc_free"], 1)
                gained(P, y, 2, 1)
                norm(0)
                route(0)
                route(1)
                begin(0)
                pair(0, 0, 2)
                NORM = 2
                TILE = PPT * ROUTE + 3 + NORM
                outer = chain.n
                with dve.Fori(0, NT - 1) as t:
                    with dve.Fori(1, PPT - 2) as p:
                        chain.base, chain.n = t * TILE + p * ROUTE + (outer - ROUTE), 0
                        pair(t * GPT + p * 2, t * P + p * TOPK, t * PH + p + 2)
                        assert chain.n == ROUTE
                    chain.base, chain.n = t * TILE + outer + (PPT - 3) * ROUTE, 0
                    norm(t + 1)
                    with dve.Fori(PPT - 2, PPT) as p:
                        chain.base, chain.n = t * TILE + p * ROUTE + (outer - ROUTE + NORM), 0
                        pair(t * GPT + p * 2, t * P + p * TOPK, t * PH + p + 2)
                    chain.base, chain.n = t * TILE + outer + ((PPT - 1) * ROUTE + NORM), 0
                    begin(t + 1)
                    pair(t * GPT + GPT, t * P + P, t * PH + (PH + 2))
                    hold(dve, s["small_in"], 16 * (B + 2))
                    hold(dve, s["y_out"], t + 1)
                    finish(t, P, y[:, :], gate2[:, :])
                    assert chain.n == ROUTE + 3, chain.n
                base = outer + (NT - 1) * TILE
                last_tile = (NT - 1) * P
                with dve.Fori(1, 3) as p:
                    chain.base, chain.n = p * (2 * ROUTE) + (base - 2 * ROUTE), 0
                    pair(p * 2 + (NT - 1) * GPT, p * TOPK + last_tile, p * 2 + ((NT - 1) * PH + 1), two=True)
                base += 4 * ROUTE
                chain.base, chain.n = base, 0
                pair((NT - 1) * GPT + 6, last_tile + 3 * TOPK, NT * PH - 1)
                gained(NS, gain_s, 2 + 2 * B, 2)
                norm(NT, NS)
                base += chain.n
                with dve.Fori(4, PPT) as p:
                    chain.base, chain.n = p * (2 * ROUTE) + (base - 8 * ROUTE), 0
                    pair(p * 2 + (NT - 1) * GPT, p * TOPK + last_tile, p * 2 + (NT * PH - 8), two=True)
                chain.base, chain.n = base + 8 * ROUTE, 0
                dve.wait_ge(s["hs_in"], 16 * QS)
                for i in range(SG):
                    dve.wait_ge(spread_in[i], 2 * 16 * QS)
                    group(NG + i, i % 2, gate_s[:, i * NB:(i + 1) * NB])
                    if i == 1:
                        dve.wait_ge(s["y_out"], NT)
                        finish(NT - 1, P, y[:, :], gate2[:, :])
                dve.wait_ge(s["folded"], 2)
                finish(NT, NS, ps_h[0:NS, :, :].rearrange("p a b -> p (a b)"), gate2_s[:, :])

            @block.tensor
            def _(pe):
                e = K["ident"]

                def rows_t(t):
                    hold(pe, s["h_normed"], t + 1)
                    for kc in range(KC):
                        last = nc.tensor.transpose(ps_h[:, kc, :], h_next[:, kc * P:(kc + 1) * P], e[:, :])
                    last.then_inc(s["hT_full"], 1)
                    hold(pe, s["hT_out"], t + 1)

                def head(H, h, first=False):
                    for kc in range(KC):
                        mm = nc.tensor.matmul(ps_r[:, 0, 0:256], hT[:, kc, :], wq[:, kc, bass.ds(h * 256, 256)],
                                              start=(kc == 0), stop=(kc == KC - 1))
                    mm.then_inc(s["q_full"], 1)
                    hold(pe, s["q_out"], H + 1)
                    for k in range(2):
                        last = nc.tensor.transpose(ps_r[:, 1, k * P:(k + 1) * P], q[:, k, :], e[:, :])
                    last.then_inc(s["qt_full"], 1)
                    hold(pe, s["qt_out"], H + 1)
                    if not first:
                        hold(pe, s["sc_out"], H)
                    for k in range(2):
                        mm = nc.tensor.matmul(ps_r[:, 2, k * PK:(k + 1) * PK], qT[:, k, :], subT[:, k, :], start=True, stop=True)
                    mm.then_inc(s["sc_full"], 1)

                def group(i, par, first=False):
                    for j in range(NB):
                        hold(pe, s["diag_ready"], i * NB + (j + 1))
                        hold(pe, v_in[j], i * 16 + 16)
                        for c in range(2):
                            mm = nc.tensor.matmul(ps_y[:, c * 512:(c + 1) * 512], diag[:, par, j, :],
                                                  v_rows[:, j, c * 512:(c + 1) * 512], start=(first and j == 0), stop=False,
                                                  skip_group_check=True)
                        mm.then_inc(s["v_used"], 1)

                def pair(i, H, h, two=False, first=False, new_tile=None):
                    head(H, h)
                    if new_tile is not None:
                        hold(pe, s["y_out"], new_tile)
                    group(i, 0, first)
                    if two:
                        head(H + 1, h + 1)
                    group(i + 1, 1)

                pe.wait_ge(s["sub_in"], 16)
                for k in range(2):
                    last = nc.tensor.transpose(ps_r[:, 1, k * PK:(k + 1) * PK], sub[:, k, :], e[:, :])
                last.then_inc(s["subT_full"], 1)
                pe.wait_ge(s["subT_out"], 1)
                rows_t(0)
                pe.wait_ge(wq_in[0], 16)
                head(0, 0, True)
                head(1, 1)
                for landed in wq_in[1:]:
                    pe.wait_ge(landed, 16)
                pair(0, 2, 2, first=True)
                with pe.Fori(0, NT - 1) as t:
                    with pe.Fori(1, PPT - 2) as p:
                        pair(t * GPT + p * 2, t * PH + p + 2, p + 2)
                    rows_t(t + 1)
                    with pe.Fori(PPT - 2, PPT) as p:
                        pair(t * GPT + p * 2, t * PH + p + 2, p + (2 - PPT))
                    pair(t * GPT + GPT, t * PH + (PH + 2), 2, first=True, new_tile=t + 1)
                with pe.Fori(1, 3) as p:
                    pair(p * 2 + (NT - 1) * GPT, p * 2 + ((NT - 1) * PH + 1), p * 2 + 1, two=True)
                pair((NT - 1) * GPT + 6, NT * PH - 1, PH - 1)
                rows_t(NT)
                with pe.Fori(4, PPT) as p:
                    pair(p * 2 + (NT - 1) * GPT, p * 2 + (NT * PH - 8), p * 2 - 8, two=True)
                pe.wait_ge(s["y_out"], NT)
                for i in range(SG):
                    group(NG + i, i % 2, i == 0)
                pe.wait_ge(s["y_out"], NT + 1)
                for c in range(2):
                    nc.tensor.matmul(ps_h[0:NS, 4 * c:4 * c + 4, :], fold[:, :], y[:, c * 512:(c + 1) * 512],
                                     start=True, stop=True).then_inc(s["folded"], 1)


def trunk_step(nc, I, O):
    mod = nc.dram_tensor("mod_rows", (NC, 6 * D), F32, kind="Internal").ap()
    x1_dram = nc.dram_tensor("x1_rows", (SEQ + P, D), F32, kind="Internal").ap()
    with ExitStack() as ctx:
        def const(name, shape, dt=F32):
            return ctx.enter_context(nc.sbuf_tensor(name, shape, dt))

        K = {"ident": const("ident", [P, P]), "ones": const("ones", [P, P]), "iota16": const("iota16", [P, TOPK], I32)}
        with ExitStack() as mix:
            def mconst(name, shape):
                return mix.enter_context(nc.sbuf_tensor(name, shape, F32))

            K.update(tri=mconst("tri", [P, P]), mask=mconst("mask", [P, P]), last=mconst("last", [P, P]),
                     tri_s=mconst("tri_s", [NS, NS]), mask_s=mconst("mask_s", [NS, NS]), last_s=mconst("last_s", [NS, NS]),
                     same=mconst("same", [NS, B]), s_bias=mconst("s_bias", [P, WIN + NS]), bias=mconst("swa_bias", [P, AH, 2 * P]),
                     live_bias=mconst("swa_live_bias", [P, AH, 2 * P]))
            w_in = mix.enter_context(nc.sbuf_tensor("w_in", [P, KC, INW], F32))
            s = {n: nc.alloc_semaphore("mix_" + n) for n in SIGNALS}
            s["w_in_in"] = nc.alloc_semaphore("mix_w_in_in")
            modulation_rows(nc, I, mod, w_in, s["w_in_in"], K)
            X = Mixer(nc, mix, w_in)
            s2 = {n: nc.alloc_semaphore("smp_" + n) for n in SIGNALS + EXTRA if n != "w_out_in"}
            s2["w_out_in"] = s["w_out_in"]
            S = sample_tile(nc, X, K, s2)
            mix_prompt(nc, I, O, mod, x1_dram, X, K, s, S)
            mix_sample(nc, I, O, mod, x1_dram, X, K, s2, S)
        del s2["w_out_in"]
        nc.clear_and_free_semaphores([*s.values(), *s2.values()])
        nc.all_engine_barrier()
        experts(nc, I, O, mod, x1_dram, K)


_OUTS = [("y_p", (1, SEQ, D)), ("y_s", (B, TS, D)),
         ("swa_k_p", (1, 1, WIN, KVH, AD)), ("swa_v_p", (1, 1, WIN, KVH, AD)), ("conv_p", (1, 1, CK - 1, CW)),
         ("C_p", (1, 1, MH, DH, DH)), ("n_p", (1, 1, MH, DH)), ("m_p", (1, 1, MH)),
         ("swa_k_s", (1, B, WIN, KVH, AD)), ("swa_v_s", (1, B, WIN, KVH, AD)), ("conv_s", (1, B, CK - 1, CW)),
         ("C_s", (1, B, MH, DH, DH)), ("n_s", (1, B, MH, DH)), ("m_s", (1, B, MH))]


def kernel(**inputs):
    import numpy as _np
    import concourse.bacc as _bacc
    from concourse import mybir as _mybir
    from concourse.bass_utils import run_bass_kernel_spmd as _run

    nc = _bacc.Bacc("TRN2", target_bir_lowering=False, num_devices=1)
    arrays, ins, outs = {}, {}, {}
    for name, a in inputs.items():
        a = _np.ascontiguousarray(a)
        arrays[f"in_{name}_dram"] = a
        ins[name] = nc.dram_tensor(f"in_{name}_dram", a.shape, _mybir.dt.from_np(a.dtype), kind="ExternalInput").ap()
    for name, shape in _OUTS:
        outs[name] = nc.dram_tensor(f"out_{name}_dram", shape, F32, kind="ExternalOutput").ap()
    trunk_step(nc, ins, outs)
    r = _run(nc, [arrays], core_ids=[0])
    return tuple(r.results[0][f"out_{name}_dram"] for name, _ in _OUTS)
```
